# Optimizing a Trainium2 kernel written in Bass

```python
import math
import jax, jax.numpy as jnp
from jax import lax
import numpy as np

D_MODEL = 1024
BATCH = 1
SEQ = 256
DEPTH = 2

CHUNK = 64
QBLK = 128
A_HEADS = 4
A_DQK = 64
A_DV = 2 * A_DQK
B_HEADS = 4
B_DH = 128
C_HEADS = 4
C_DK = 128
C_DV = 256
ROPE_BASE = 10000.0
N_BRANCH = 3
D_FF = 2816
CONV_W = 3
LN_EPS = 1e-5
ALPHA = (2 * DEPTH) ** 0.25
BETA = (8 * DEPTH) ** -0.25

SPLITS = (A_HEADS * 2 * A_DQK, A_HEADS * 2 * A_DQK, A_HEADS * A_DV,
          B_HEADS * B_DH, B_HEADS * B_DH, B_HEADS * B_DH, B_HEADS,
          C_HEADS * C_DK, C_HEADS * C_DK, C_HEADS * C_DV, C_HEADS * C_DV,
          N_BRANCH * D_MODEL)
D_IN = int(sum(SPLITS))
SPLIT_IDX = tuple(int(v) for v in np.cumsum(SPLITS)[:-1])


def _layernorm(x, g, b):
    xf = x.astype(jnp.float32)
    mu = jnp.mean(xf, -1, keepdims=True)
    var = jnp.mean(jnp.square(xf - mu), -1, keepdims=True)
    return ((xf - mu) * lax.rsqrt(var + LN_EPS) * g + b).astype(x.dtype)

def _head_rmsnorm(o, g):
    of = o.astype(jnp.float32)
    of = of * lax.rsqrt(jnp.mean(jnp.square(of), -1, keepdims=True) + LN_EPS)
    return of * g.reshape(o.shape[2], o.shape[3])

def _head_groupnorm(o, g):
    of = o.astype(jnp.float32)
    mu = jnp.mean(of, -1, keepdims=True)
    var = jnp.mean(jnp.square(of - mu), -1, keepdims=True)
    return (of - mu) * lax.rsqrt(var + LN_EPS) * g.reshape(o.shape[2], o.shape[3])

def _query_blocks(t):
    t = t.reshape((t.shape[0], t.shape[1] // QBLK, QBLK) + t.shape[2:])
    return jnp.moveaxis(t, 1, 0)

def _merge_blocks(o):
    o = jnp.moveaxis(o, 0, 1)
    return o.reshape((o.shape[0], o.shape[1] * o.shape[2]) + o.shape[3:])

def _diff_attention(q, k, v, lam):
    S_ = q.shape[1]
    scale = A_DQK ** -0.5
    k_chunk = jnp.arange(S_) // CHUNK

    def block(args):
        qb, i = args
        s = jnp.einsum('bqhmd,bkhmd->bhmqk', qb, k).astype(jnp.float32) * scale
        q_chunk = (i * QBLK + jnp.arange(QBLK)) // CHUNK
        mask = k_chunk[None, :] <= q_chunk[:, None]
        p = jax.nn.softmax(jnp.where(mask, s, -jnp.inf), axis=-1)
        a = p[:, :, 0] - lam * p[:, :, 1]
        return jnp.einsum('bhqk,bkhe->bqhe', a.astype(v.dtype), v)

    o = lax.map(block, (_query_blocks(q), jnp.arange(S_ // QBLK)))
    return _merge_blocks(o)

def _forgetting_attention(q, k, v, log_f):
    S_ = q.shape[1]
    scale = B_DH ** -0.5
    F = jnp.cumsum(log_f, axis=1)
    Fk = jnp.transpose(F, (0, 2, 1))[:, :, None, :]
    pos = jnp.arange(S_)

    def block(args):
        qb, Fq, i = args
        s = jnp.einsum('bqhd,bkhd->bhqk', qb, k).astype(jnp.float32) * scale
        s = s + jnp.transpose(Fq, (0, 2, 1))[..., None] - Fk
        q_pos = i * QBLK + jnp.arange(QBLK)
        mask = pos[None, :] <= q_pos[:, None]
        p = jax.nn.softmax(jnp.where(mask, s, -jnp.inf), axis=-1)
        return jnp.einsum('bhqk,bkhd->bqhd', p.astype(v.dtype), v)

    o = lax.map(block, (_query_blocks(q), _query_blocks(F), jnp.arange(S_ // QBLK)))
    return _merge_blocks(o)

def _rotary(t, pos):
    half = t.shape[-1] // 2
    inv = 1.0 / (ROPE_BASE ** jnp.linspace(0.0, 1.0, half, dtype=jnp.float32))
    ang = pos.astype(jnp.float32)[:, None] * inv[None, :]
    cos, sin = jnp.cos(ang)[None, :, None, :], jnp.sin(ang)[None, :, None, :]
    tf = t.astype(jnp.float32)
    t1, t2 = tf[..., :half], tf[..., half:]
    return jnp.concatenate([t1 * cos - t2 * sin, t1 * sin + t2 * cos], axis=-1)

def _retention(q, k, v):
    B_, S_ = q.shape[0], q.shape[1]
    nc = S_ // CHUNK
    log_gamma = jnp.log(1.0 - 2.0 ** (-5.0 - jnp.arange(C_HEADS, dtype=jnp.float32)))
    pos = jnp.arange(S_)
    qc = _rotary(q, pos).reshape(B_, nc, CHUNK, C_HEADS, C_DK)
    kc = (_rotary(k, pos) * C_DK ** -0.5).reshape(B_, nc, CHUNK, C_HEADS, C_DK)
    vc = v.astype(jnp.float32).reshape(B_, nc, CHUNK, C_HEADS, C_DV)
    i = jnp.arange(CHUNK, dtype=jnp.float32)
    diff = i[:, None] - i[None, :]
    dmask = jnp.where(diff >= 0, jnp.exp(log_gamma[:, None, None] * jnp.maximum(diff, 0.0)), 0.0)
    s = jnp.einsum('bnihd,bnjhd->bnhij', qc, kc) * dmask
    inner = jnp.einsum('bnhij,bnjhe->bnihe', s, vc)
    q_dec = qc * jnp.exp(log_gamma[None, :] * (i[:, None] + 1.0))[:, :, None]
    k_dec = kc * jnp.exp(log_gamma[None, :] * (CHUNK - 1.0 - i[:, None]))[:, :, None]
    chunk_decay = jnp.exp(log_gamma * CHUNK)[None, :, None, None]

    def step(R, xs):
        qd, kd, vv = xs
        cross = jnp.einsum('bihd,bhde->bihe', qd, R)
        R = chunk_decay * R + jnp.einsum('bjhd,bjhe->bhde', kd, vv)
        return R, cross

    R0 = jnp.zeros((B_, C_HEADS, C_DK, C_DV), jnp.float32)
    _, cross = lax.scan(step, R0, (jnp.moveaxis(q_dec, 1, 0), jnp.moveaxis(k_dec, 1, 0),
                                   jnp.moveaxis(vc, 1, 0)))
    o = inner + jnp.moveaxis(cross, 0, 1)
    return o.reshape(B_, S_, C_HEADS, C_DV)

def _token_mixer(h, w_in, b_in, lam, lam_init, g_diff, g_ret, w_pa, w_pb, w_pc, w_out):
    B_, S_, _ = h.shape
    z = h @ w_in + b_in
    aq, ak, av, bq, bk, bv, bf, cq, ck, cv, cg, gates = jnp.split(z, SPLIT_IDX, axis=-1)
    ya = _diff_attention(aq.reshape(B_, S_, A_HEADS, 2, A_DQK), ak.reshape(B_, S_, A_HEADS, 2, A_DQK),
                         av.reshape(B_, S_, A_HEADS, A_DV), lam)
    ya = (_head_rmsnorm(ya, g_diff) * (1.0 - lam_init)).astype(h.dtype).reshape(B_, S_, -1)
    yb = _forgetting_attention(bq.reshape(B_, S_, B_HEADS, B_DH), bk.reshape(B_, S_, B_HEADS, B_DH),
                               bv.reshape(B_, S_, B_HEADS, B_DH),
                               jax.nn.log_sigmoid(bf.astype(jnp.float32)))
    yb = yb.reshape(B_, S_, -1)
    yc = _retention(cq.reshape(B_, S_, C_HEADS, C_DK), ck.reshape(B_, S_, C_HEADS, C_DK),
                    cv.reshape(B_, S_, C_HEADS, C_DV))
    yc = _head_groupnorm(yc, g_ret).astype(h.dtype).reshape(B_, S_, -1) * jax.nn.silu(cg)
    ga, gb, gc = jnp.split(jax.nn.sigmoid(gates), N_BRANCH, axis=-1)
    m = ga * (ya @ w_pa) + gb * (yb @ w_pb) + gc * (yc @ w_pc)
    return m @ w_out

def _conv_ffn(h, w_up, w_conv, b_conv, w_down):
    S_ = h.shape[1]
    u, g = jnp.split(h @ w_up, 2, axis=-1)
    up = jnp.pad(u, ((0, 0), (CONV_W - 1, 0), (0, 0)))
    conv = b_conv + up[:, 0:S_] * w_conv[0]
    for j in range(1, CONV_W):
        conv = conv + up[:, j:j + S_] * w_conv[j]
    return (jax.nn.gelu(conv, approximate=False) * g) @ w_down

def first_inputs(seed: int = 0) -> dict:
    key = jax.random.key(seed)
    ks = jax.random.split(key, 24)
    nrm = lambda k, shape, s: jax.random.normal(k, shape, jnp.float32) * s
    D = D_MODEL
    return {
        "x": nrm(ks[0], (BATCH, SEQ, D), 1.0),
        "c": nrm(ks[1], (BATCH, D), 1.0),
        "w_ada": nrm(ks[2], (DEPTH, D, 6 * D), D ** -0.5),
        "b_ada": nrm(ks[3], (DEPTH, 6 * D), 0.02),
        "w_in": nrm(ks[4], (DEPTH, D, D_IN), D ** -0.5),
        "b_in": nrm(ks[5], (DEPTH, D_IN), 0.02),
        "lam_q1": nrm(ks[6], (DEPTH, A_DQK), 0.1),
        "lam_k1": nrm(ks[7], (DEPTH, A_DQK), 0.1),
        "lam_q2": nrm(ks[8], (DEPTH, A_DQK), 0.1),
        "lam_k2": nrm(ks[9], (DEPTH, A_DQK), 0.1),
        "g_diff": 1.0 + nrm(ks[10], (DEPTH, A_HEADS * A_DV), 0.02),
        "g_ret": 1.0 + nrm(ks[11], (DEPTH, C_HEADS * C_DV), 0.02),
        "w_pa": nrm(ks[12], (DEPTH, A_HEADS * A_DV, D), (A_HEADS * A_DV) ** -0.5),
        "w_pb": nrm(ks[13], (DEPTH, B_HEADS * B_DH, D), (B_HEADS * B_DH) ** -0.5),
        "w_pc": nrm(ks[14], (DEPTH, C_HEADS * C_DV, D), (C_HEADS * C_DV) ** -0.5),
        "w_out": nrm(ks[15], (DEPTH, D, D), BETA * D ** -0.5),
        "ln_g": 1.0 + nrm(ks[16], (DEPTH, 2, D), 0.02),
        "ln_b": nrm(ks[17], (DEPTH, 2, D), 0.02),
        "w_up": nrm(ks[18], (DEPTH, D, 2 * D_FF), D ** -0.5),
        "w_conv": nrm(ks[19], (DEPTH, CONV_W, D_FF), CONV_W ** -0.5),
        "b_conv": nrm(ks[20], (DEPTH, D_FF), 0.02),
        "w_down": nrm(ks[21], (DEPTH, D_FF, D), BETA * D_FF ** -0.5),
    }

def first_block(x, c, w_ada, b_ada, w_in, b_in, lam_q1, lam_k1, lam_q2, lam_k2, g_diff, g_ret,
              w_pa, w_pb, w_pc, w_out, ln_g, ln_b, w_up, w_conv, b_conv, w_down):
    c_act = jax.nn.silu(c)
    for l in range(DEPTH):
        mod = c_act @ w_ada[l] + b_ada[l]
        sh1, sc1, gt1, sh2, sc2, gt2 = [m[:, None, :] for m in jnp.split(mod, 6, axis=-1)]
        lam_init = 0.8 - 0.6 * math.exp(-0.3 * l)
        lam = (jnp.exp(jnp.sum(lam_q1[l].astype(jnp.float32) * lam_k1[l].astype(jnp.float32)))
               - jnp.exp(jnp.sum(lam_q2[l].astype(jnp.float32) * lam_k2[l].astype(jnp.float32)))
               + lam_init)
        h = x * (1.0 + sc1) + sh1
        y = _token_mixer(h, w_in[l], b_in[l], lam, lam_init, g_diff[l], g_ret[l],
                         w_pa[l], w_pb[l], w_pc[l], w_out[l])
        x = _layernorm(ALPHA * x + gt1 * y, ln_g[l, 0], ln_b[l, 0])
        h = x * (1.0 + sc2) + sh2
        y = _conv_ffn(h, w_up[l], w_conv[l], b_conv[l], w_down[l])
        x = _layernorm(ALPHA * x + gt2 * y, ln_g[l, 1], ln_b[l, 1])
    return x


N_MIXERS = 2
N_EVEN = (DEPTH + 1) // 2
N_ODD = DEPTH // 2
ALPHA_2 = (2.0 * DEPTH) ** 0.25
BETA_INIT = (8.0 * DEPTH) ** -0.25

GDN_K_HEADS = 4
GDN_V_HEADS = 8
GDN_HEAD_K = 128
GDN_HEAD_V = 128
GDN_KDIM = GDN_K_HEADS * GDN_HEAD_K
GDN_VDIM = GDN_V_HEADS * GDN_HEAD_V
GDN_CONV = 4
GDN_CHUNK = 64
GDN_QKV = 2 * GDN_KDIM + GDN_VDIM
GDN_IN = GDN_QKV + GDN_VDIM + 2 * GDN_V_HEADS
GDN_EPS = 1e-6

SWA_Q_HEADS = 16
SWA_KV_HEADS = 2
SWA_GROUP = SWA_Q_HEADS // SWA_KV_HEADS
SWA_HEAD_DIM = 64
SWA_WINDOW = 128
SWA_BLOCK = 128
SWA_QDIM = SWA_Q_HEADS * SWA_HEAD_DIM
SWA_KVDIM = SWA_KV_HEADS * SWA_HEAD_DIM
SWA_IN = SWA_QDIM + 2 * SWA_KVDIM

REL_BUCKETS = 32
REL_MAX_DIST = 128

FFN_DIM = 2816
N_EXPERTS = 8
TOP_K = 2
EXPERT_DIM = 3584


def layer_norm(x, g, b):
    xf = x.astype(jnp.float32)
    mu = jnp.mean(xf, axis=-1, keepdims=True)
    var = jnp.mean(jnp.square(xf - mu), axis=-1, keepdims=True)
    return ((xf - mu) * lax.rsqrt(var + LN_EPS) * g.astype(jnp.float32) + b.astype(jnp.float32)).astype(x.dtype)

def l2_normalize(x):
    xf = x.astype(jnp.float32)
    return xf * lax.rsqrt(jnp.sum(xf * xf, axis=-1, keepdims=True) + GDN_EPS)

def causal_depthwise_conv(x, w):
    width = w.shape[0]
    return lax.conv_general_dilated(
        x, w[:, None, :].astype(x.dtype), window_strides=(1,), padding=[(width - 1, 0)],
        dimension_numbers=('NWC', 'WIO', 'NWC'), feature_group_count=x.shape[-1])

def gated_delta_rule_chunked(q, k, v, g, beta):
    bsz, t, h, dk = q.shape
    dv = v.shape[-1]
    c = GDN_CHUNK
    n = t // c
    f32 = jnp.float32

    def blocks(a):
        a = a.astype(f32).reshape((bsz, n, c, h) + a.shape[3:])
        return jnp.moveaxis(a, 2, 3)

    q, k, v, g, beta = blocks(q), blocks(k), blocks(v), blocks(g), blocks(beta)
    g_cum = jnp.cumsum(g, axis=-1)
    causal = jnp.tril(jnp.ones((c, c), dtype=bool))
    strict = jnp.tril(jnp.ones((c, c), dtype=bool), -1)
    diff = g_cum[..., :, None] - g_cum[..., None, :]
    decay = jnp.exp(jnp.where(causal, diff, -jnp.inf))
    k_beta = k * beta[..., None]
    v_beta = v * beta[..., None]
    a_kk = jnp.where(strict, jnp.einsum('bnhid,bnhjd->bnhij', k_beta, k) * decay, 0.0)
    eye = jnp.eye(c, dtype=f32)
    t_inv = lax.linalg.triangular_solve(eye + a_kk, jnp.broadcast_to(eye, a_kk.shape),
                                        left_side=True, lower=True, unit_diagonal=True)
    u = jnp.einsum('bnhij,bnhje->bnhie', t_inv, v_beta)
    w = jnp.einsum('bnhij,bnhjd->bnhid', t_inv, k_beta * jnp.exp(g_cum)[..., None])
    a_qk = jnp.einsum('bnhid,bnhjd->bnhij', q, k) * decay
    g_last = g_cum[..., -1]
    q_dec = q * jnp.exp(g_cum)[..., None]
    k_dec = k * jnp.exp(g_last[..., None] - g_cum)[..., None]
    xs = (jnp.moveaxis(q_dec, 1, 0), jnp.moveaxis(k_dec, 1, 0), jnp.moveaxis(u, 1, 0),
          jnp.moveaxis(w, 1, 0), jnp.moveaxis(a_qk, 1, 0), jnp.moveaxis(jnp.exp(g_last), 1, 0))

    def step(s, inp):
        qd, kd, uc, wc, aqk, dl = inp
        v_new = uc - jnp.einsum('bhcd,bhde->bhce', wc, s)
        o = jnp.einsum('bhcd,bhde->bhce', qd, s) + jnp.einsum('bhcs,bhse->bhce', aqk, v_new)
        s = s * dl[..., None, None] + jnp.einsum('bhcd,bhce->bhde', kd, v_new)
        return s, o

    s0 = jnp.zeros((bsz, h, dk, dv), f32)
    _, o = lax.scan(step, s0, xs)
    o = jnp.moveaxis(o, 0, 1)
    return jnp.moveaxis(o, 2, 3).reshape(bsz, t, h, dv)

def gated_deltanet(x, w_in, conv_w, a_log, dt_bias, norm_w, w_out):
    bsz, t, _ = x.shape
    proj = x @ w_in
    o1 = GDN_QKV
    o2 = o1 + GDN_VDIM
    o3 = o2 + GDN_V_HEADS
    qkv = jax.nn.silu(causal_depthwise_conv(proj[..., :o1], conv_w))
    z = proj[..., o1:o2].reshape(bsz, t, GDN_V_HEADS, GDN_HEAD_V)
    b_logit = proj[..., o2:o3]
    a_logit = proj[..., o3:]
    q = qkv[..., :GDN_KDIM].reshape(bsz, t, GDN_K_HEADS, GDN_HEAD_K)
    k = qkv[..., GDN_KDIM:2 * GDN_KDIM].reshape(bsz, t, GDN_K_HEADS, GDN_HEAD_K)
    v = qkv[..., 2 * GDN_KDIM:].reshape(bsz, t, GDN_V_HEADS, GDN_HEAD_V)
    rep = GDN_V_HEADS // GDN_K_HEADS
    q = jnp.repeat(l2_normalize(q) * (GDN_HEAD_K ** -0.5), rep, axis=2)
    k = jnp.repeat(l2_normalize(k), rep, axis=2)
    beta = jax.nn.sigmoid(b_logit.astype(jnp.float32))
    g = -jnp.exp(a_log.astype(jnp.float32)) * jax.nn.softplus(
        a_logit.astype(jnp.float32) + dt_bias.astype(jnp.float32))
    o = gated_delta_rule_chunked(q, k, v, g, beta)
    o = o * lax.rsqrt(jnp.mean(o * o, axis=-1, keepdims=True) + GDN_EPS) * norm_w.astype(jnp.float32)
    o = o * jax.nn.silu(z.astype(jnp.float32))
    return o.reshape(bsz, t, GDN_VDIM).astype(x.dtype) @ w_out

def t5_bucket(dist):
    max_exact = REL_BUCKETS // 2
    df = jnp.maximum(dist, 1).astype(jnp.float32)
    large = max_exact + (jnp.log(df / max_exact) / math.log(REL_MAX_DIST / max_exact)
                         * (REL_BUCKETS - max_exact)).astype(jnp.int32)
    large = jnp.minimum(large, REL_BUCKETS - 1)
    return jnp.where(dist < max_exact, dist, large)

def swa_sink_attention(x, w_in, b_in, sinks, rel_bias, w_out):
    bsz, t, _ = x.shape
    nb = t // SWA_BLOCK
    proj = x @ w_in + b_in
    q = proj[..., :SWA_QDIM].reshape(bsz, nb, SWA_BLOCK, SWA_KV_HEADS, SWA_GROUP, SWA_HEAD_DIM)
    k = proj[..., SWA_QDIM:SWA_QDIM + SWA_KVDIM]
    v = proj[..., SWA_QDIM + SWA_KVDIM:]

    def band(a):
        ab = a.reshape(bsz, nb, SWA_BLOCK, SWA_KV_HEADS, SWA_HEAD_DIM)
        prev = jnp.pad(ab, ((0, 0), (1, 0), (0, 0), (0, 0), (0, 0)))[:, :-1]
        return jnp.concatenate([prev, ab], axis=2)

    kb, vb = band(k), band(v)
    s = jnp.einsum('bnqkgd,bnskd->bnkgqs', q, kb).astype(jnp.float32) * (SWA_HEAD_DIM ** -0.5)
    qi = jnp.arange(SWA_BLOCK)[:, None]
    kj = jnp.arange(2 * SWA_BLOCK)[None, :]
    dist = qi + SWA_BLOCK - kj
    bias = rel_bias.astype(jnp.float32)[t5_bucket(jnp.maximum(dist, 0))]
    bias = jnp.transpose(bias, (2, 0, 1)).reshape(SWA_KV_HEADS, SWA_GROUP, SWA_BLOCK, 2 * SWA_BLOCK)
    band_ok = (dist >= 0) & (dist < SWA_WINDOW)
    blk = jnp.arange(nb)[:, None, None]
    mask = band_ok[None] & ((blk > 0) | (kj >= SWA_BLOCK)[None])
    s = jnp.where(mask[None, :, None, None], s + bias, -jnp.inf)
    sink = jnp.broadcast_to(sinks.astype(jnp.float32).reshape(SWA_KV_HEADS, SWA_GROUP, 1, 1),
                            s.shape[:-1] + (1,))
    p = jax.nn.softmax(jnp.concatenate([s, sink], axis=-1), axis=-1)[..., :-1]
    o = jnp.einsum('bnkgqs,bnskd->bnqkgd', p.astype(vb.dtype), vb).reshape(bsz, t, SWA_QDIM)
    return o @ w_out

def swiglu(x, w_gate, w_up, w_down):
    return (jax.nn.silu(x @ w_gate) * (x @ w_up)) @ w_down

def moe_swiglu(x, w_router, w_gate, w_up, w_down):
    bsz, t, d = x.shape
    xf = x.reshape(bsz * t, d)
    logits = (xf @ w_router).astype(jnp.float32)
    top_val, top_idx = lax.top_k(logits, TOP_K)
    top_w = jax.nn.softmax(top_val, axis=-1)
    gates = jnp.einsum('nk,nke->ne', top_w, jax.nn.one_hot(top_idx, N_EXPERTS, dtype=jnp.float32))
    out = jnp.zeros_like(xf)
    for e in range(N_EXPERTS):
        h = jax.nn.silu(xf @ w_gate[e]) * (xf @ w_up[e])
        out = out + gates[:, e:e + 1].astype(xf.dtype) * (h @ w_down[e])
    return out.reshape(bsz, t, d)

def second_inputs(seed: int = 0) -> dict:
    key = jax.random.key(seed)
    ks = jax.random.split(key, 24)

    def nrm(k, shape, scale):
        return jax.random.normal(k, shape, jnp.float32) * scale

    x = nrm(ks[0], (BATCH, SEQ, D_MODEL), 1.0)
    a_w_in = nrm(ks[1], (N_EVEN, D_MODEL, GDN_IN), D_MODEL ** -0.5)
    a_conv_w = nrm(ks[2], (N_EVEN, GDN_CONV, GDN_QKV), GDN_CONV ** -0.5)
    a_a_log = jnp.log(jax.random.uniform(ks[3], (N_EVEN, GDN_V_HEADS), jnp.float32, 1.0, 16.0))
    dt = jnp.exp(jax.random.uniform(ks[4], (N_EVEN, GDN_V_HEADS), jnp.float32,
                                    math.log(1e-3), math.log(1e-1)))
    a_dt_bias = dt + jnp.log(-jnp.expm1(-dt))
    a_norm_w = 1.0 + nrm(ks[5], (N_EVEN, GDN_HEAD_V), 0.02)
    a_w_out = nrm(ks[6], (N_EVEN, GDN_VDIM, D_MODEL), GDN_VDIM ** -0.5 * BETA_INIT)
    b_w_in = nrm(ks[7], (N_ODD, D_MODEL, SWA_IN), D_MODEL ** -0.5)
    b_b_in = nrm(ks[8], (N_ODD, SWA_IN), 0.02)
    b_sinks = nrm(ks[9], (N_ODD, SWA_Q_HEADS), 1.0)
    b_w_out = nrm(ks[10], (N_ODD, SWA_QDIM, D_MODEL), SWA_QDIM ** -0.5 * BETA_INIT)
    rel_bias = nrm(ks[11], (REL_BUCKETS, SWA_Q_HEADS), 0.3)
    ffn_w_gate = nrm(ks[12], (N_EVEN, D_MODEL, FFN_DIM), D_MODEL ** -0.5)
    ffn_w_up = nrm(ks[13], (N_EVEN, D_MODEL, FFN_DIM), D_MODEL ** -0.5)
    ffn_w_down = nrm(ks[14], (N_EVEN, FFN_DIM, D_MODEL), FFN_DIM ** -0.5 * BETA_INIT)
    moe_router = nrm(ks[15], (N_ODD, D_MODEL, N_EXPERTS), D_MODEL ** -0.5)
    moe_w_gate = nrm(ks[16], (N_ODD, N_EXPERTS, D_MODEL, EXPERT_DIM), D_MODEL ** -0.5)
    moe_w_up = nrm(ks[17], (N_ODD, N_EXPERTS, D_MODEL, EXPERT_DIM), D_MODEL ** -0.5)
    moe_w_down = nrm(ks[18], (N_ODD, N_EXPERTS, EXPERT_DIM, D_MODEL), EXPERT_DIM ** -0.5 * BETA_INIT)
    ln_g = 1.0 + nrm(ks[19], (DEPTH, 2, D_MODEL), 0.02)
    ln_b = nrm(ks[20], (DEPTH, 2, D_MODEL), 0.02)
    return {'x': x, 'a_w_in': a_w_in, 'a_conv_w': a_conv_w, 'a_a_log': a_a_log, 'a_dt_bias': a_dt_bias,
            'a_norm_w': a_norm_w, 'a_w_out': a_w_out, 'b_w_in': b_w_in, 'b_b_in': b_b_in,
            'b_sinks': b_sinks, 'b_w_out': b_w_out, 'rel_bias': rel_bias, 'ffn_w_gate': ffn_w_gate,
            'ffn_w_up': ffn_w_up, 'ffn_w_down': ffn_w_down, 'moe_router': moe_router,
            'moe_w_gate': moe_w_gate, 'moe_w_up': moe_w_up, 'moe_w_down': moe_w_down,
            'ln_g': ln_g, 'ln_b': ln_b}

def second_block(x, a_w_in, a_conv_w, a_a_log, a_dt_bias, a_norm_w, a_w_out, b_w_in, b_b_in, b_sinks,
              b_w_out, rel_bias, ffn_w_gate, ffn_w_up, ffn_w_down, moe_router, moe_w_gate, moe_w_up,
              moe_w_down, ln_g, ln_b):
    for i in range(DEPTH):
        j = i // N_MIXERS
        if i % N_MIXERS == 0:
            h = gated_deltanet(x, a_w_in[j], a_conv_w[j], a_a_log[j], a_dt_bias[j], a_norm_w[j], a_w_out[j])
        else:
            h = swa_sink_attention(x, b_w_in[j], b_b_in[j], b_sinks[j], rel_bias, b_w_out[j])
        x = layer_norm(ALPHA_2 * x + h, ln_g[i, 0], ln_b[i, 0])
        if i % 2 == 0:
            f = swiglu(x, ffn_w_gate[j], ffn_w_up[j], ffn_w_down[j])
        else:
            f = moe_swiglu(x, moe_router[j], moe_w_gate[j], moe_w_up[j], moe_w_down[j])
        x = layer_norm(ALPHA_2 * x + f, ln_g[i, 1], ln_b[i, 1])
    return x


def setup_inputs(seed=0):
    out = dict(first_inputs(seed))
    for name, value in second_inputs(seed + 1).items():
        if name != "x":
            out[name + "_2"] = value
    return out


def reference(
    x, c, w_ada, b_ada, w_in, b_in, lam_q1, lam_k1, lam_q2, lam_k2, g_diff, g_ret, w_pa, w_pb,
    w_pc, w_out, ln_g, ln_b, w_up, w_conv, b_conv, w_down, a_w_in_2, a_conv_w_2, a_a_log_2,
    a_dt_bias_2, a_norm_w_2, a_w_out_2, b_w_in_2, b_b_in_2, b_sinks_2, b_w_out_2, rel_bias_2,
    ffn_w_gate_2, ffn_w_up_2, ffn_w_down_2, moe_router_2, moe_w_gate_2, moe_w_up_2,
    moe_w_down_2, ln_g_2, ln_b_2,
):
    x = first_block(
        x, c, w_ada, b_ada, w_in, b_in, lam_q1, lam_k1, lam_q2, lam_k2, g_diff, g_ret, w_pa,
        w_pb, w_pc, w_out, ln_g, ln_b, w_up, w_conv, b_conv, w_down,
    )
    return second_block(
        x, a_w_in_2, a_conv_w_2, a_a_log_2, a_dt_bias_2, a_norm_w_2, a_w_out_2, b_w_in_2,
        b_b_in_2, b_sinks_2, b_w_out_2, rel_bias_2, ffn_w_gate_2, ffn_w_up_2, ffn_w_down_2,
        moe_router_2, moe_w_gate_2, moe_w_up_2, moe_w_down_2, ln_g_2, ln_b_2,
    )


_drawn_inputs = setup_inputs


def setup_inputs(seed=0):
    import zlib

    import numpy as np

    out = dict(_drawn_inputs(seed))
    spreads = {}
    factors = {'b_in': 4.112,
     'lam_q1': 43.81,
     'lam_k1': 5.207,
     'lam_q2': 8.0,
     'lam_k2': 5.32,
     'g_diff': 8.0,
     'g_ret': 8.0,
     'b_conv': 8.0,
     'a_norm_w_2': 18.332,
     'b_b_in_2': 5.057,
     'b_sinks_2': 8.0,
     'rel_bias_2': 3.052}
    for name, (base, spread) in spreads.items():
        noise = np.random.default_rng([zlib.crc32(name.encode()), seed]).standard_normal(out[name].shape)
        drawn = base * np.exp(spread * noise) if base else spread * noise
        out[name] = __import__('jax').numpy.asarray(drawn.astype(out[name].dtype))
    for name, factor in factors.items():
        out[name] = (out[name] * factor).astype(out[name].dtype)
    return out
```

```python
from contextlib import ExitStack
import math

import numpy as np
import concourse.bass as bass
from concourse import mybir

ALU = mybir.AluOpType
ACT = mybir.ActivationFunctionType
F32 = mybir.dt.float32
AX = mybir.AxisListType.X

P = 128
S = 256
NT = S // P
D = 1024
KD = D // P
DEPTH = 2
ALPHA = (2 * DEPTH) ** 0.25
EPS = 1e-5
CHUNK = 64
A_HEADS, A_DQK = 4, 64
B_HEADS, B_DH = 4, 128
C_HEADS, C_DK, C_DV = 4, 128, 256
FF1 = 2816
GK, GV, GD = 4, 8, 128
GDN_EPS = 1e-6
GDN_TAPS = 4
LEVELS = 7
WQ_HEADS, WKV_HEADS, WD = 16, 2, 64
WINDOW = 128
BUCKETS, MAX_DIST = 32, 128
FF2 = 2816
NE = 8
FFE = 3584
NEG = -1.0e30

PASSES = (("start", 1), ("layer", DEPTH), ("middle", 1), ("expert", NE), ("over", None), ("end", 1))
OVER = 2 * S // (P + 1)

W_LOADS = {
    "start": [],
    "layer": [("ada", c) for c in range(12)] + [("A", c) for c in range(3)]
    + [("B", c) for c in range(3)] + [("bf", 0)] + [("C", c) for c in range(6)]
    + [("gate", c) for c in range(6)] + [("pa", n) for n in range(2)]
    + [("pb", n) for n in range(2)] + [("pc", n) for n in range(2)]
    + [("out", n) for n in range(2)]
    + [("up", c) for c in range(FF1 // 256)] + [("down", c) for c in range((FF1 // P + 3) // 4)],
    "middle": [("qkv", c) for c in range(4)] + [("z", c) for c in range(2)] + [("ba", 0)]
    + [("gout", n) for n in range(2)]
    + [("up", c) for c in range(FF2 // 256)] + [("down", c) for c in range((FF2 // P + 3) // 4)]
    + [("wq", c) for c in range(2)] + [("wkv", 0)] + [("wout", n) for n in range(2)]
    + [("router", 0)],
    "expert": [("up", c) for c in range(FFE // 256)] + [("down", c) for c in range(FFE // P // 4)],
    "end": [],
}
W_LOADS["over"] = W_LOADS["expert"]
LN_ROWS = ["g0", "b0", "g1", "b1"]
R_LOADS = {
    "start": [],
    "layer": [("ada", c) for c in range(12)] + [("lam", 0)] + [("A", c) for c in range(3)]
    + [("B", c) for c in range(3)] + [("bf", 0)] + [("C", c) for c in range(6)]
    + [("gate", c) for c in range(6)] + [("gdiff", 0), ("gret", 0), ("gret", 1)]
    + [("ln1", r) for r in LN_ROWS] + [("conv", 0)] + [("ln2", r) for r in LN_ROWS],
    "middle": [("gconv", 0), ("gpar", 0)] + [("ln1", r) for r in LN_ROWS]
    + [("relb", 0), ("hot", 0), ("tmask", 0)] + [("ln2", r) for r in LN_ROWS]
    + [("wq", c) for c in range(2)] + [("wkv", 0), ("sink", 0)] + [("ln3", r) for r in LN_ROWS],
    "expert": [], "over": [],
    "end": [("ln4", r) for r in LN_ROWS],
}
PER_PARTITION = {"conv", "gconv", "relb", "hot"}
W_WIDTH = {"ada": 4096, "A": 4096, "B": 4096, "bf": 32, "C": 4096, "gate": 4096, "pa": 2048,
           "pb": 2048, "pc": 4096, "out": 4096, "up": 4096, "down": 4096, "qkv": 4096, "z": 4096,
           "ba": 128, "gout": 4096, "wq": 4096, "wkv": 2048, "wout": 4096, "router": 64}
W_SLOTS, R_SLOTS, BANKS = 3, 4, 8
JOBS = {'start': 0, 'layer': 196, 'middle': 288, 'expert': 37, 'over': 37, 'end': 0}
GIVEN = {
    'c_ready': {'layer': 1},
    'c_silu': {'start': 1},
    'h_ready': {'layer': 6, 'middle': 4, 'end': 1},
    'hT_ready': {'layer': 12, 'middle': 16},
    'zA_ready': {'layer': 6},
    'zB_ready': {'layer': 6, 'middle': 1},
    'zC_ready': {'layer': 2},
    'qkT_ready': {'layer': 12, 'middle': 6},
    'lam_dots': {'layer': 1},
    'lam_exps': {'layer': 1},
    'forget_pre': {'layer': 2},
    'forget_exp': {'layer': 1},
    'forget_ln': {'layer': 1},
    'forget_ready': {'layer': 1},
    'masked': {'layer': 16, 'middle': 16},
    'exped': {'layer': 16, 'middle': 16},
    'probs': {'layer': 16, 'middle': 16},
    'probsT_ready': {'layer': 16, 'middle': 16},
    'retained': {'layer': 8},
    'gate_pre': {'layer': 4, 'middle': 1},
    'gate_done': {'layer': 4, 'middle': 1},
    'var_ready': {'layer': 4, 'middle': 4, 'end': 1},
    'std_ready': {'layer': 4, 'middle': 4, 'end': 1},
    'y_ready': {'layer': 6, 'middle': 4},
    'yT_ready': {'layer': 8, 'middle': 8},
    'hid_pre': {'layer': 22},
    'hid_act': {'layer': 22, 'middle': 22, 'expert': 14, 'over': 14},
    'hid_ready': {'layer': 22, 'middle': 22, 'expert': 14, 'over': 14},
    'g_pre': {'middle': 15},
    'g_act': {'middle': 23},
    'g_in': {'middle': 25},
    'g_out': {'middle': 36},
    'bias_made': {'middle': 1},
    'route_in': {'middle': 1},
    'plan_ready': {'middle': 1},
    'select_ready': {'expert': 2, 'over': 2},
    'chosen_ready': {'expert': 5, 'over': 5},
    'down_ready': {'expert': 14, 'over': 14},
}

CONST = {}
for _name, _width in (("ident", P), ("ones", P), ("steps", 3 * P), ("causal", 2 * P),
                      ("blocks", 2 * P), ("strict", P), ("levels", LEVELS * P),
                      ("decay", C_HEADS * S), ("cos", NT * 64), ("sin", NT * 64), ("below", NE * NE),
                      ("slots", 2 * P)):
    CONST[_name] = (sum(w for _, w in CONST.values()), _width)
N_CONST = sum(w for _, w in CONST.values())


def constants():
    j = np.arange(P)[:, None]
    i = np.arange(P)[None, :]
    t = {}
    t["ident"] = np.eye(P)
    t["ones"] = np.ones((P, P))
    upto = (j <= i).astype(np.float64)
    t["steps"] = np.concatenate([np.zeros((P, P)), upto, np.ones((P, P))], 1)
    t["causal"] = np.concatenate([np.zeros((P, P)), np.where(i <= j, 0.0, NEG)], 1)
    t["blocks"] = np.concatenate([np.zeros((P, P)), np.where(i // CHUNK <= j // CHUNK, 0.0, NEG)], 1)
    t["strict"] = (i < j).astype(np.float64)
    t["levels"] = np.concatenate(
        [((i >> n) % 2 == 1) & ((i >> n) - 1 == (j >> n)) for n in range(LEVELS)], 1)
    gamma = 1.0 - 2.0 ** (-5.0 - np.arange(C_HEADS))
    far = np.arange(S)[None, :] - j
    t["decay"] = np.concatenate(
        [np.where(far >= 0, g ** np.maximum(far, 0), 0.0) * C_DK ** -0.5 for g in gamma], 1)
    half = C_DK // 2
    inv = (1.0 / (10000.0 ** np.linspace(0.0, 1.0, half, dtype=np.float32))).astype(np.float32)
    ang = (np.arange(S, dtype=np.float32)[:, None] * inv[None, :]).astype(np.float32).astype(np.float64)
    for name, f in (("cos", np.cos), ("sin", np.sin)):
        t[name] = f(ang).reshape(NT, P, half).transpose(1, 0, 2).reshape(P, NT * half)
    e = np.arange(NE)
    t["below"] = np.broadcast_to((e[None, :] < e[:, None]).reshape(1, NE * NE), (P, NE * NE))
    t["slots"] = np.broadcast_to(np.arange(2 * P)[None, :], (P, 2 * P))
    return np.ascontiguousarray(np.concatenate([t[n] for n in CONST], 1).astype(np.float32))


def bias_tables():
    dist = 255 - np.arange(384)
    d = np.clip(dist, 0, None)
    exact = BUCKETS // 2
    df = np.maximum(d, 1).astype(np.float32)
    large = exact + (np.log(df / np.float32(exact)) / np.float32(math.log(MAX_DIST / exact))
                     * np.float32(BUCKETS - exact)).astype(np.int32)
    bucket = np.where(d < exact, d, np.minimum(large, BUCKETS - 1))
    ok = (dist >= 0) & (dist < WINDOW)
    hot = np.zeros((P, 512), np.float32)
    hot[:BUCKETS, :384] = (np.arange(BUCKETS)[:, None] == bucket[None, :]) & ok[None, :]
    mask = np.zeros(512, np.float32)
    mask[:384] = np.where(ok, 0.0, NEG)
    return hot, mask


class Pass:

    def __init__(self, part, turn=None):
        self.part, self.turn = part, turn

    def value(self, per, k):
        for part, times in PASSES:
            if part == self.part:
                break
            assert times is not None or not per.get(part, 0)
            k += (times or 0) * per.get(part, 0)
        step = per.get(self.part, 0)
        return k if self.turn is None or step == 0 else self.turn * step + k


class Signal:

    def __init__(self, sem, name):
        self.sem, self.name, self.per, self.seen = sem, name, GIVEN.get(name, {}), {}

    def event(self, at):
        self.seen[at.part] = self.seen.get(at.part, 0) + 1
        return self.sem, 1

    def nth(self, at, k):
        return self.sem, at.value(self.per, k)

    def last(self, at):
        return self.nth(at, self.seen[at.part])


class Ring:

    def __init__(self, n, filled, freed, unit, order, count):
        self.n, self.filled, self.freed, self.unit = n, filled, freed, unit
        self.order, self.count = order, count

    def place(self, at, name):
        i = self.order[at.part].index(name)
        slot = i % self.n
        per = {p: (c + self.n - 1 - slot) // self.n for p, c in self.count.items()}
        return slot, i // self.n, per

    def slot(self, at, name):
        return self.place(at, name)[0]

    def vacant(self, at, name):
        slot, before, per = self.place(at, name)
        return self.freed[slot], at.value(per, before + 1)

    def fills(self, at, name):
        return self.filled[self.slot(at, name)], self.unit

    def full(self, at, name):
        slot, before, per = self.place(at, name)
        v = at.value(per, before + 1)
        return self.filled[slot], v * self.unit

    def frees(self, at, name):
        return self.freed[self.slot(at, name)], 1

    def vacated(self, at, name):
        slot, before, per = self.place(at, name)
        return self.freed[slot], at.value(per, before + 2)


class Banks(Ring):

    def vacant(self, at, name):
        self.order[at.part].append(name)
        return super().vacant(at, name)


class Steps:

    def __init__(self):
        self.n, self.at = 0, None

    def count(self):
        self.n += 1
        return self.n

    def enter(self, part, turn=None):
        self.at, self.n = Pass(part, turn), 0


def program(nc, ins, out):
    ctx = ExitStack()
    with ctx:
        def sb(name, shape):
            return ctx.enter_context(nc.sbuf_tensor(name, shape, F32))

        def sem(name):
            return ctx.enter_context(nc.semaphore(name))

        def sig(name):
            s = Signal(sem(name), name)
            signals.append(s)
            return s

        signals = []
        W = sb("W", [P, W_SLOTS, 4096])
        R = sb("R", [P, R_SLOTS, 512])
        x = sb("x", [P, NT, D])
        h = sb("h", [P, NT, D])
        hT = sb("hT", [P, KD, S])
        consts = sb("consts", [P, N_CONST])
        arena = sb("arena", [P, 24592])
        scores = sb("scores", [P, 2, 2, S])
        probsT = sb("probsT", [P, 2, 4, P])
        work = sb("work", [P, 1024])
        acted = sb("acted", [P, 2, S])
        small = sb("small", [P, 256])
        banks = [ctx.enter_context(nc.psum_tensor(f"bank{i}", [P, 512], F32)) for i in range(BANKS)]
        spread = nc.dram_tensor("spread", (WQ_HEADS, P, 384), F32, kind="Internal").ap()

        def const(name):
            a, w = CONST[name]
            return consts[:, a:a + w]

        def view(at, *dims):
            n = int(np.prod(dims))
            v = arena[:, at:at + n]
            if len(dims) == 1:
                return v
            names = "abc"[:len(dims)]
            return v.rearrange("p (" + " ".join(names) + ") -> p " + " ".join(names),
                               **dict(zip(names, dims)))

        ident, ones = const("ident"), const("ones")
        steps, causal, blocks = const("steps"), const("causal"), const("blocks")
        upto = steps[:, P:2 * P]
        levels = const("levels").rearrange("p (n i) -> p n i", n=LEVELS)
        decay = const("decay").rearrange("p (h i) -> p h i", h=C_HEADS)
        cos = const("cos").rearrange("p (t f) -> p t f", t=NT)
        sin = const("sin").rearrange("p (t f) -> p t f", t=NT)
        below = const("below").rearrange("p (a b) -> p a b", a=NE)

        mod = view(0, 12, 512)
        forget = view(0, NT, B_HEADS, S)
        zA = view(6144, NT, 1536)
        zB = view(9216, NT, 1544)
        zCqk = view(12304, NT, 1024)
        zCv = view(14352, NT, 1024)
        zCg = view(16400, NT, 1024)
        aT = view(18448, 8, S)
        bT = view(20496, 8, S)
        cT = view(22544, 8, S)
        forget_neg = view(22544, NT, B_HEADS, P)
        gA, gB, gC = h, view(18448, NT, 1024), zA[:, :, 512:1536]
        yA, yB, yC = zA[:, :, 0:512], zB[:, :, 0:512], zCqk
        yAT, yBT, yCT = view(20496, 4, S), view(21520, 4, S), view(22544, 8, S)
        mix, mixT = zCv, view(16400, KD, S)
        hid1 = view(6144, FF1 // P, S)
        gT = view(0, 16, S)
        gq, gk = gT[:, 0:4, :], gT[:, 4:8, :]
        gz = view(4096, NT, 1024)
        gvb = view(6144, NT, GV, P)
        gkn = view(8192, NT, GK, P)
        go = view(9216, NT, 1024)
        gsq = view(11264, 8, S)
        g9 = [view(11264 + 1024 * n, GV, P) for n in range(9)]
        gdec, gaT, gbT, gt, gtT, gu, gaq, gvn, gst = g9
        gplus, gminus, gpair = gbT, gu, gt
        goT = view(0, KD, S)
        hid2 = view(0, FF2 // P, S)
        relw = view(5632, WQ_HEADS, 384)
        wbias = view(11776, WQ_HEADS, S)
        relspread = view(15872, WQ_HEADS, P)
        wq = view(0, NT, 1024)
        wkv = view(2048, NT, 256)
        wkd = view(2560, NT, 256)
        wqT = view(3072, 8, S)
        wkT = view(5120, 2, S)
        wo = view(15872, NT, 1024)
        woT = view(0, KD, S)
        hidT = view(0, FFE // P, P)
        chosenT = view(3584, KD, P)
        chosen_out = view(4608, NT, 512)
        select = view(5632, NT, P)
        weigh = view(5888, NT, P)
        weighT = view(6144, NT, P)
        hid_tok = view(6400, 2, S)
        xin = h

        nmax = small[:, 0:4].rearrange("p (b m) -> p b m", b=2)
        rsum = small[:, 4:8].rearrange("p (b m) -> p b m", b=2)
        lam = small[:, 8:12]
        stats = small[:, 12:36].rearrange("p (a s) -> p a s", a=4)
        meanvar = small[:, 36:52].rearrange("p (a s) -> p a s", a=8)
        inv = small[:, 52:60]
        logf = small[:, 60:76]
        beta = small[:, 76:92]
        decays = small[:, 92:108]
        cums = small[:, 108:140]
        egc = small[:, 140:156]
        egl = small[:, 156:172]
        tmp = small[:, 172:204]
        esink = small[:, 204:208].rearrange("p (b m) -> p b m", b=2)
        route = sb("route", [P, 2, NT, NE])
        gates, places = route[:, 0, :, :], route[:, 1, :, :]
        now = small[:, 208:212].rearrange("p (a t) -> p a t", a=2)
        plan = ctx.enter_context(nc.sbuf_tensor("plan", [P, 1 + OVER], mybir.dt.int32))
        csil = small[:, 226:234]
        rinv = small[:, 234:240].rearrange("p (b m) -> p b m", b=3)
        cspread = hT[:, :, 0:P]
        nw = acted[:, 0, 0:P]

        weights = Ring(W_SLOTS, [sem(f"weights_in{i}") for i in range(W_SLOTS)],
                       [sem(f"weights_freed{i}") for i in range(W_SLOTS)], 16, W_LOADS,
                       {p: len(n) for p, n in W_LOADS.items()})
        rows = Ring(R_SLOTS, [sem(f"rows_in{i}") for i in range(R_SLOTS)],
                    [sem(f"rows_freed{i}") for i in range(R_SLOTS)], 16, R_LOADS,
                    {p: len(n) for p, n in R_LOADS.items()})
        psum = Banks(BANKS, [sem(f"product_done{i}") for i in range(BANKS)],
                    [sem(f"bank_freed{i}") for i in range(BANKS)], 1, {p: [] for p, _ in PASSES}, JOBS)
        consts_in, x_in, c_in = sem("consts_in"), sem("x_in"), sem("c_in")
        out_written, bias_out, bias_in = sem("out_written"), sem("bias_out"), sem("bias_in")
        pe_step, act_done, dve_done = sem("pe_step"), sem("act_done"), sem("dve_done")

        c_ready = sig("c_ready")
        c_silu = sig("c_silu")
        h_ready = sig("h_ready")
        hT_ready = sig("hT_ready")
        zA_ready, zB_ready, zC_ready = sig("zA_ready"), sig("zB_ready"), sig("zC_ready")
        qkT_ready = sig("qkT_ready")
        lam_dots, lam_exps = sig("lam_dots"), sig("lam_exps")
        forget_pre, forget_exp, forget_ln = sig("forget_pre"), sig("forget_exp"), sig("forget_ln")
        forget_ready = sig("forget_ready")
        masked = sig("masked")
        exped = sig("exped")
        probs = sig("probs")
        probsT_ready = sig("probsT_ready")
        retained = sig("retained")
        y_done = sig("y_done")
        gate_pre, gate_done = sig("gate_pre"), sig("gate_done")
        var_ready, std_ready = sig("var_ready"), sig("std_ready")
        y_ready = sig("y_ready")
        yT_ready = sig("yT_ready")
        hid_pre, hid_act, hid_ready = sig("hid_pre"), sig("hid_act"), sig("hid_ready")
        g_pre, g_act = sig("g_pre"), sig("g_act")
        g_in = sig("g_in")
        g_out = sig("g_out")
        bias_made = sig("bias_made")
        route_in, plan_ready = sig("route_in"), sig("plan_ready")
        select_ready, chosen_ready, down_ready = sig("select_ready"), sig("chosen_ready"), sig("down_ready")

        block = ctx.enter_context(nc.Block())

        @block.sync
        def _(sp):
            def load_weight(at, name, src):
                sp.wait_ge(*weights.vacant(at, name))
                slot = weights.slot(at, name)
                n = W_WIDTH[name[0]]
                if name == ("down", 5) and at.part in ("layer", "middle"):
                    n = 2048
                sp.dma_start(W[:, slot, 0:n], src[:, 0:n]).then_inc(*weights.fills(at, name))

            def load_row(at, name, src):
                sp.wait_ge(*rows.vacant(at, name))
                slot = rows.slot(at, name)
                sp.dma_start(R[:, slot, :], src).then_inc(*rows.fills(at, name))

            def row_source(at, name, turn):
                n = R_LOADS[at.part].index(name)
                if name[0] in PER_PARTITION:
                    src = ins["cols_" + at.part]
                    n = [r for r in R_LOADS[at.part] if r[0] in PER_PARTITION].index(name)
                    return src[turn, n] if turn is not None else src[n]
                src = ins["rows_" + at.part]
                src = src[turn, n:n + 1, :] if turn is not None else src[n:n + 1, :]
                return src.to_broadcast([P, 512])

            def stream(at, turn, after):
                src = ins["w_" + at.part]
                done = []

                def row(name):
                    load_row(at, name, row_source(at, name, turn))
                    done.append(name)

                for n, name in enumerate(W_LOADS[at.part]):
                    if name in R_LOADS[at.part]:
                        row(name)
                    load_weight(at, name, src[turn, n] if turn is not None else src[n])
                    for r in after.get(name, []):
                        row(r)
                assert done == R_LOADS[at.part], (done, R_LOADS[at.part])

            sp.dma_start(consts[:, :], ins["constants"]).then_inc(consts_in, 16)
            sp.dma_start(csil, ins["c_columns"]).then_inc(c_in, 16)
            sp.dma_start(x[:, :, :], ins["x"].rearrange("(t p) d -> p t d", p=P)).then_inc(x_in, 16)
            with sp.Fori(0, DEPTH) as l:
                at = Pass("layer", l)
                stream(at, l, {("ada", 11): [("lam", 0)],
                               ("gate", 5): [("gdiff", 0), ("gret", 0), ("gret", 1)],
                               ("out", 1): [("ln1", r) for r in LN_ROWS] + [("conv", 0)],
                               ("down", 5): [("ln2", r) for r in LN_ROWS]})
            at = Pass("middle")
            src = W_LOADS["middle"]
            after = {("qkv", 0): [("gconv", 0), ("gpar", 0)],
                     ("gout", 1): [("ln1", r) for r in LN_ROWS] + [("relb", 0), ("hot", 0), ("tmask", 0)],
                     ("down", 5): [("ln2", r) for r in LN_ROWS],
                     ("wkv", 0): [("sink", 0)],
                     ("wout", 1): [("ln3", r) for r in LN_ROWS]}
            stream(at, None, after)
            with sp.Fori(0, NE) as e:
                stream(Pass("expert", e), e, {})
            sp.wait_ge(*plan_ready.nth(Pass("middle"), 1))
            n_over = sp.value_load(plan[0:1, 0:1], min_val=0, max_val=OVER)
            with sp.If(n_over):
                with sp.Fori(0, n_over) as i:
                    e = sp.value_load(plan[0:1, bass.ds(1 + i, 1)], min_val=0, max_val=NE - 1)
                    at = Pass("over", i)
                    for n, name in enumerate(W_LOADS["over"]):
                        load_weight(at, name, ins["w_expert"][e, n])
            at = Pass("end")
            for name in R_LOADS["end"]:
                load_row(at, name, row_source(at, name, None))
            sp.wait_ge(*h_ready.nth(at, 1))
            sp.dma_start(out.rearrange("(t p) d -> p t d", p=P), x[:, :, :]).then_inc(out_written, 16)
            sp.wait_ge(out_written, 16)

        @block.gpsimd
        def _(pool):
            for s in weights.freed + rows.freed + psum.freed:
                pool.sem_inc(s, 1)
            at = Pass("middle")
            pool.wait_ge(*bias_made.nth(at, 1))
            pool.dma_start(spread.rearrange("h p m -> p h m"), relw).then_inc(bias_out, 16)
            pool.wait_ge(bias_out, 16)
            shifted = bass.AP(spread.tensor, P - 1, [[383, P], [P * 384, WQ_HEADS], [1, S]])
            pool.dma_start(wbias, shifted).then_inc(bias_in, 16)

        @block.tensor
        def _(pe):
            mm, turn_over = nc.tensor.matmul, nc.tensor.transpose
            at = None

            used = []

            def hand_back():
                while used:
                    w, job = used.pop()
                    pe.wait_ge(*psum.full(at, job))
                    pe.nop().then_inc(*weights.frees(at, w))

            def chunk(name, w, src, kt, width):
                pe.wait_ge(*weights.full(at, w))
                slot = weights.slot(at, w)
                wv = W[:, slot, 0:kt * width].rearrange("p (k n) -> p k n", k=kt)
                for t in range(NT):
                    yield
                    pe.wait_ge(*psum.vacant(at, name + (t,)))
                    bank = banks[psum.slot(at, name + (t,))]
                    for k in range(kt):
                        last = mm(bank[:, 0:width], src[:, k, t * P:(t + 1) * P], wv[:, k, :],
                                  start=k == 0, stop=k == kt - 1)
                        if k == 0:
                            hand_back()
                    last.then_inc(*psum.fills(at, name + (t,)))
                    if t == NT - 1:
                        used.append((w, name + (t,)))

            def run(*gens):
                for g in gens:
                    for _ in g:
                        pass

            def transposes(name, src, tiles, signal, first, waits_each=1):
                hand_back()
                for t in range(NT):
                    if signal is not None:
                        pe.wait_ge(*signal.nth(at, first + t * waits_each))
                    for q in range((tiles + 3) // 4):
                        pe.wait_ge(*psum.vacant(at, (name, t, q)))
                        bank = banks[psum.slot(at, (name, t, q))]
                        for i in range(min(4, tiles - 4 * q)):
                            f = (4 * q + i) * P
                            last = turn_over(bank[:, i * P:(i + 1) * P], src[:, t, f:f + P], ident)
                        last.then_inc(*psum.fills(at, (name, t, q)))

            def up(n_chunks):
                for c in range(n_chunks):
                    pe.wait_ge(*weights.full(at, ("up", c)))
                    slot = weights.slot(at, ("up", c))
                    wv = W[:, slot, :].rearrange("p (k g n) -> p k g n", k=KD, g=2)
                    for i in range(2):
                        pe.wait_ge(*psum.vacant(at, ("up", 2 * c + i)))
                        bank = banks[psum.slot(at, ("up", 2 * c + i))]
                        for g in range(2):
                            for k in range(KD):
                                last = mm(bank[:, g * S:(g + 1) * S], wv[:, k, g, i * P:(i + 1) * P],
                                          hT[:, k, :], start=k == 0, stop=k == KD - 1)
                                if k == 0:
                                    hand_back()
                        last.then_inc(*psum.fills(at, ("up", 2 * c + i)))
                    used.append((("up", c), ("up", 2 * c + 1)))

            def down(hid, tiles):
                jobs = [("down", t, n) for t in range(NT) for n in range(2)]
                acc = []
                for j in jobs:
                    pe.wait_ge(*psum.vacant(at, j))
                    acc.append(banks[psum.slot(at, j)])
                for c in range((tiles + 3) // 4):
                    pe.wait_ge(*weights.full(at, ("down", c)))
                    slot = weights.slot(at, ("down", c))
                    wv = W[:, slot, :].rearrange("p (k n) -> p k n", k=4)
                    for i in range(min(4, tiles - 4 * c)):
                        k = 4 * c + i
                        pe.wait_ge(*hid_ready.nth(at, k + 1))
                        for j, (_, t, n) in enumerate(jobs):
                            last = mm(acc[j][:, :], hid[:, k, t * P:(t + 1) * P],
                                      wv[:, i, n * 512:(n + 1) * 512], start=k == 0, stop=k == tiles - 1)
                            hand_back()
                            if k == tiles - 1:
                                last.then_inc(*psum.fills(at, jobs[j]))
                    if 4 * c + 4 < tiles:
                        last.then_inc(*weights.frees(at, ("down", c)))
                    else:
                        used.append((("down", c), jobs[-1]))
                        hand_back()

            def attend(kind, h_, t, qT, kT, maps):
                K = (t + 1) * P
                for m in range(maps):
                    pe.wait_ge(*psum.vacant(at, (kind + "s", h_, t, m)))
                    bank = banks[psum.slot(at, (kind + "s", h_, t, m))]
                    a, b = (m * 64, m * 64 + 64) if maps == 2 else (0, P)
                    last = mm(bank[:, 0:K], qT[a:b, t * P:(t + 1) * P], kT[a:b, 0:K],
                              start=True, stop=kind != "B")
                    if kind == "B":
                        for j in range(t + 1):
                            lhs = upto if j == t else ones
                            mm(bank[:, 0:K], lhs, forget[:, j, h_, 0:K], start=False, stop=False)
                            last = mm(bank[:, 0:K], forget_neg[:, j, h_, :],
                                      steps[:, P - j * P:P - j * P + K], start=False, stop=j == t)
                    last.then_inc(*psum.fills(at, (kind + "s", h_, t, m)))

            def attend_T(kind, h_, t, u, maps):
                pe.wait_ge(*probs.nth(at, u + 1))
                pe.wait_ge(*psum.vacant(at, (kind + "t", h_, t)))
                bank = banks[psum.slot(at, (kind + "t", h_, t))]
                for m in range(maps):
                    for kt in range(t + 1):
                        i = m * (t + 1) + kt
                        last = turn_over(bank[:, i * P:(i + 1) * P],
                                         scores[:, u % 2, m, kt * P:(kt + 1) * P], ident)
                last.then_inc(*psum.fills(at, (kind + "t", h_, t)))

            def attend_out(kind, h_, t, u, v, maps):
                pe.wait_ge(*probsT_ready.nth(at, u + 1))
                pe.wait_ge(*psum.vacant(at, (kind + "o", h_, t)))
                bank = banks[psum.slot(at, (kind + "o", h_, t))]
                for m in range(maps):
                    for kt in range(t + 1):
                        vv = v(m, kt)
                        n = vv.shape[-1]
                        last = mm(bank[:, m * n:(m + 1) * n], probsT[:, u % 2, m * (t + 1) + kt, :], vv,
                                  start=kt == 0, stop=kt == t)
                last.then_inc(*psum.fills(at, (kind + "o", h_, t)))

            pe.wait_ge(consts_in, 16)
            with pe.Fori(0, DEPTH) as l:
                at = Pass("layer", l)
                pe.wait_ge(*c_ready.nth(at, 1))
                for c in range(12):
                    pe.wait_ge(*weights.full(at, ("ada", c)))
                    slot = weights.slot(at, ("ada", c))
                    wv = W[:, slot, :].rearrange("p (k n) -> p k n", k=KD)
                    pe.wait_ge(*psum.vacant(at, ("ada", c)))
                    bank = banks[psum.slot(at, ("ada", c))]
                    for k in range(KD):
                        last = mm(bank[:, :], cspread[:, k, :], wv[:, k, :], start=k == 0, stop=k == KD - 1)
                        if k == 0:
                            hand_back()
                    last.then_inc(*psum.fills(at, ("ada", c)))
                    used.append((("ada", c), ("ada", c)))
                transposes("hT", h, KD, h_ready, 1)
                pe.wait_ge(*hT_ready.nth(at, 4))
                for c in range(3):
                    run(chunk(("A", c), ("A", c), hT, KD, 512))
                run(chunk(("B", 0), ("B", 0), hT, KD, 512))
                pe.wait_ge(*zA_ready.nth(at, 6))
                transposes("aT", zA, 8, None, 0)
                run(chunk(("B", 1), ("B", 1), hT, KD, 512))
                run(chunk(("B", 2), ("B", 2), hT, KD, 512))
                run(chunk(("bf", 0), ("bf", 0), hT, KD, 4))

                def background():
                    for c in range(6):
                        yield from chunk(("C", c), ("C", c), hT, KD, 512)
                    for c in range(6):
                        yield from chunk(("gate", c), ("gate", c), hT, KD, 512)

                bg = background()
                next(bg)
                pe.wait_ge(*qkT_ready.nth(at, 4))
                u = 0
                for h_ in range(A_HEADS):
                    for t in range(NT):
                        attend("A", h_, t, aT[:, h_, :], aT[:, 4 + h_, :], 2)
                        next(bg)
                        attend_T("A", h_, t, u, 1)
                        if u:
                            ph, pt = divmod(u - 1, NT)
                            attend_out("A", ph, pt, u - 1, lambda m, kt: zA[:, kt, 1024 + ph * P:1024 + (ph + 1) * P], 1)
                        u += 1
                pe.wait_ge(*zB_ready.nth(at, 6))
                transposes("bT", zB, 8, None, 0)
                attend_out("A", 3, 1, u - 1, lambda m, kt: zA[:, kt, 1024 + 3 * P:1024 + 4 * P], 1)
                pe.wait_ge(*qkT_ready.nth(at, 8))
                pe.wait_ge(*forget_ready.nth(at, 1))
                for h_ in range(B_HEADS):
                    for t in range(NT):
                        attend("B", h_, t, bT[:, h_, :], bT[:, 4 + h_, :], 1)
                        next(bg)
                        attend_T("B", h_, t, u, 1)
                        if u > 8:
                            ph, pt = divmod(u - 9, NT)
                            attend_out("B", ph, pt, u - 1, lambda m, kt: zB[:, kt, 1024 + ph * P:1024 + (ph + 1) * P], 1)
                        u += 1
                pe.wait_ge(*zC_ready.nth(at, 2))
                attend_out("B", 3, 1, u - 1, lambda m, kt: zB[:, kt, 1024 + 3 * P:1024 + 4 * P], 1)
                transposes("cT", zCqk, 8, None, 0)
                next(bg)
                pe.wait_ge(*qkT_ready.nth(at, 12))
                for h_ in range(C_HEADS):
                    for j in range(NT):
                        pe.wait_ge(*psum.vacant(at, ("Cs", h_, j)))
                        bank = banks[psum.slot(at, ("Cs", h_, j))]
                        n = S - j * P
                        mm(bank[:, 0:n], cT[:, 4 + h_, j * P:(j + 1) * P], cT[:, h_, j * P:S],
                           start=True, stop=True).then_inc(*psum.fills(at, ("Cs", h_, j)))
                    next(bg, None)
                    pe.wait_ge(*retained.nth(at, 2 * h_ + 2))
                    flat = scores[:, h_ % 2, :, :].rearrange("p m k -> p (m k)")
                    for t in range(NT):
                        pe.wait_ge(*psum.vacant(at, ("Co", h_, t)))
                        bank = banks[psum.slot(at, ("Co", h_, t))]
                        for j in range(t + 1):
                            at_ = 256 if j else t * P
                            last = mm(bank[:, 0:C_DV], flat[:, at_:at_ + P],
                                      zCv[:, j, h_ * C_DV:(h_ + 1) * C_DV], start=j == 0, stop=j == t)
                        last.then_inc(*psum.fills(at, ("Co", h_, t)))
                for _ in bg:
                    pass
                transposes("yA", yA, 4, y_ready, 1)
                transposes("yB", yB, 4, y_ready, 3)
                transposes("yC", yC, 8, y_ready, 5)
                for b, (yT, kt, upto_) in enumerate(((yAT, 4, 2), (yBT, 4, 4), (yCT, 8, 8))):
                    pe.wait_ge(*yT_ready.nth(at, upto_))
                    for n in range(2):
                        run(chunk(("p", b, n), ("p" + "abc"[b], n), yT, kt, 512))
                transposes("mT", mix, KD, h_ready, 3)
                pe.wait_ge(*hT_ready.nth(at, 8))
                for n in range(2):
                    run(chunk(("out", n), ("out", n), mixT, KD, 512))
                transposes("h2T", h, KD, h_ready, 5)
                pe.wait_ge(*hT_ready.nth(at, 12))
                up(FF1 // 256)
                down(hid1, FF1 // P)

            at = Pass("middle")
            transposes("gxT", x, KD, h_ready, 1, 0)
            pe.wait_ge(*hT_ready.nth(at, 4))
            for c in range(4):
                pe.wait_ge(*weights.full(at, ("qkv", c)))
                slot = weights.slot(at, ("qkv", c))
                wv = W[:, slot, :].rearrange("p (k n) -> p k n", k=KD)
                for i in range(2):
                    pe.wait_ge(*psum.vacant(at, ("qkv", 2 * c + i)))
                    bank = banks[psum.slot(at, ("qkv", 2 * c + i))]
                    for g in range(2):
                        f = (2 * i + g) * P
                        for k in range(KD):
                            last = mm(bank[:, g * S:(g + 1) * S], wv[:, k, f:f + P], hT[:, k, :],
                                      start=k == 0, stop=k == KD - 1)
                            if k == 0:
                                hand_back()
                    last.then_inc(*psum.fills(at, ("qkv", 2 * c + i)))
                used.append((("qkv", c), ("qkv", 2 * c + 1)))
            for c in range(2):
                run(chunk(("z", c), ("z", c), hT, KD, 512))
            run(chunk(("ba", 0), ("ba", 0), hT, KD, 16))
            pe.wait_ge(*g_act.nth(at, 8))
            for t in range(NT):
                for q in range(2):
                    pe.wait_ge(*psum.vacant(at, ("vn", t, q)))
                    bank = banks[psum.slot(at, ("vn", t, q))]
                    for i in range(4):
                        last = turn_over(bank[:, i * P:(i + 1) * P], gT[:, 8 + 4 * q + i, t * P:(t + 1) * P], ident)
                    last.then_inc(*psum.fills(at, ("vn", t, q)))
            for p in range(4):
                pe.wait_ge(*g_out.nth(at, p + 1))
                pe.wait_ge(*psum.vacant(at, ("ss", p)))
                bank = banks[psum.slot(at, ("ss", p))]
                mm(bank[:, :], ones, gsq[:, 2 * p:2 * p + 2, :].rearrange("p a n -> p (a n)"),
                   start=True, stop=True).then_inc(*psum.fills(at, ("ss", p)))
            pe.wait_ge(*g_in.nth(at, 1))
            pe.wait_ge(*psum.vacant(at, ("cum", 0)))
            bank = banks[psum.slot(at, ("cum", 0))]
            mm(bank[:, 0:16], upto, decays, start=True, stop=True)
            mm(bank[:, 16:32], ones, decays, start=True, stop=True).then_inc(*psum.fills(at, ("cum", 0)))
            pe.wait_ge(*g_in.nth(at, 2))
            for t in range(NT):
                pe.wait_ge(*psum.vacant(at, ("kn", t)))
                bank = banks[psum.slot(at, ("kn", t))]
                for i in range(GK):
                    last = turn_over(bank[:, i * P:(i + 1) * P], gk[:, i, t * P:(t + 1) * P], ident)
                last.then_inc(*psum.fills(at, ("kn", t)))
            n_in, n_out = 2, 6
            for t in range(NT):
                tok = slice(t * P, (t + 1) * P)
                n_in += 1
                pe.wait_ge(*g_in.nth(at, n_in))
                for q in range(2):
                    pe.wait_ge(*psum.vacant(at, ("G", t, q)))
                    bank = banks[psum.slot(at, ("G", t, q))]
                    for i in range(4):
                        hh = 4 * q + i
                        mm(bank[:, i * P:(i + 1) * P], upto, gplus[:, hh, :], start=True, stop=False)
                        last = mm(bank[:, i * P:(i + 1) * P], gminus[:, hh, :], upto, start=False, stop=True)
                    last.then_inc(*psum.fills(at, ("G", t, q)))
                for name, rhs in (("kk", gk), ("qk", gq)):
                    pe.wait_ge(*psum.vacant(at, (name, t)))
                    bank = banks[psum.slot(at, (name, t))]
                    for i in range(GK):
                        last = mm(bank[:, i * P:(i + 1) * P], gk[:, i, tok], rhs[:, i, tok], start=True, stop=True)
                    last.then_inc(*psum.fills(at, (name, t)))
                n_in += 1
                pe.wait_ge(*g_in.nth(at, n_in))
                for name, src in (("DT", gdec), ("AT", gpair)):
                    for q in range(2):
                        pe.wait_ge(*psum.vacant(at, (name, t, q)))
                        bank = banks[psum.slot(at, (name, t, q))]
                        for i in range(4):
                            last = turn_over(bank[:, i * P:(i + 1) * P], src[:, 4 * q + i, :], ident)
                        last.then_inc(*psum.fills(at, (name, t, q)))
                for lv in range(LEVELS):
                    n_in += 1
                    pe.wait_ge(*g_in.nth(at, n_in))
                    for q in range(2):
                        pe.wait_ge(*psum.vacant(at, ("U", t, lv, q)))
                        bank = banks[psum.slot(at, ("U", t, lv, q))]
                        for i in range(4):
                            last = mm(bank[:, i * P:(i + 1) * P], gbT[:, 4 * q + i, :], gt[:, 4 * q + i, :],
                                      start=True, stop=True)
                        last.then_inc(*psum.fills(at, ("U", t, lv, q)))
                    for q in range(2):
                        n_out += 1
                        pe.wait_ge(*g_out.nth(at, n_out))
                        for name, lhs, rhs in (("V", gtT, gu), ("VT", gu, gtT)):
                            if name == "V" and lv == LEVELS - 1:
                                continue
                            pe.wait_ge(*psum.vacant(at, (name, t, lv, q)))
                            bank = banks[psum.slot(at, (name, t, lv, q))]
                            for i in range(4):
                                last = mm(bank[:, i * P:(i + 1) * P], lhs[:, 4 * q + i, :], rhs[:, 4 * q + i, :],
                                          start=True, stop=True)
                            last.then_inc(*psum.fills(at, (name, t, lv, q)))
                n_in += 1
                pe.wait_ge(*g_in.nth(at, n_in))
                if t:
                    for q in range(2):
                        pe.wait_ge(*psum.vacant(at, ("wT", t, q)))
                        bank = banks[psum.slot(at, ("wT", t, q))]
                        for i in range(4):
                            last = mm(bank[:, i * P:(i + 1) * P], gdec[:, 4 * q + i, :], gtT[:, 4 * q + i, :],
                                      start=True, stop=True)
                        last.then_inc(*psum.fills(at, ("wT", t, q)))
                    n_out += 2
                    pe.wait_ge(*g_out.nth(at, n_out))
                for q in range(2):
                    pe.wait_ge(*psum.vacant(at, ("vnew", t, q)))
                    bank = banks[psum.slot(at, ("vnew", t, q))]
                    for i in range(4):
                        hh = 4 * q + i
                        last = mm(bank[:, i * P:(i + 1) * P], gtT[:, hh, :], gvb[:, t, hh, :],
                                  start=True, stop=t == 0)
                        if t:
                            last = mm(bank[:, i * P:(i + 1) * P], gaT[:, hh, :], gst[:, hh, :],
                                      start=False, stop=True)
                    last.then_inc(*psum.fills(at, ("vnew", t, q)))
                n_in += 1
                pe.wait_ge(*g_in.nth(at, n_in))
                for q in range(2):
                    if t:
                        pe.wait_ge(*psum.vacant(at, ("oa", q)))
                        bank = banks[psum.slot(at, ("oa", q))]
                        for i in range(4):
                            hh = 4 * q + i
                            last = mm(bank[:, i * P:(i + 1) * P], gq[:, hh // 2, tok], gst[:, hh, :],
                                      start=True, stop=True)
                        last.then_inc(*psum.fills(at, ("oa", q)))
                    pe.wait_ge(*psum.vacant(at, ("ob", t, q)))
                    bank = banks[psum.slot(at, ("ob", t, q))]
                    for i in range(4):
                        hh = 4 * q + i
                        last = mm(bank[:, i * P:(i + 1) * P], gaq[:, hh, :], gvn[:, hh, :], start=True, stop=True)
                    last.then_inc(*psum.fills(at, ("ob", t, q)))
                    if not t:
                        pe.wait_ge(*psum.vacant(at, ("st", q)))
                        bank = banks[psum.slot(at, ("st", q))]
                        for i in range(4):
                            hh = 4 * q + i
                            last = mm(bank[:, i * P:(i + 1) * P], gdec[:, hh, :], gvn[:, hh, :],
                                      start=True, stop=True)
                        last.then_inc(*psum.fills(at, ("st", q)))
            transposes("goT", go, KD, y_ready, 1)
            pe.wait_ge(*yT_ready.nth(at, 4))
            for n in range(2):
                run(chunk(("gout", n), ("gout", n), goT, KD, 512))
            transposes("fxT", x, KD, h_ready, 2, 0)
            pe.wait_ge(*hT_ready.nth(at, 8))
            up(FF2 // 256)
            pe.wait_ge(*g_in.nth(at, n_in + 1))
            pe.wait_ge(*rows.full(at, ("hot", 0)))
            hot = rows.slot(at, ("hot", 0))
            for h_ in range(WQ_HEADS):
                pe.wait_ge(*psum.vacant(at, ("rel", h_)))
                bank = banks[psum.slot(at, ("rel", h_))]
                mm(bank[:, 0:384], relspread[0:BUCKETS, h_, :], R[0:BUCKETS, hot, 0:384],
                   start=True, stop=True).then_inc(*psum.fills(at, ("rel", h_)))
            down(hid2, FF2 // P)
            transposes("wxT", x, KD, h_ready, 3, 0)
            pe.wait_ge(*hT_ready.nth(at, 12))
            for c in range(2):
                run(chunk(("wq", c), ("wq", c), hT, KD, 512))
            run(chunk(("wkv", 0), ("wkv", 0), hT, KD, 256))
            pe.wait_ge(*zB_ready.nth(at, 1))
            transposes("wqT", wq, 8, None, 0)
            transposes("wkT", wkd, 2, None, 0)
            pe.wait_ge(*qkT_ready.nth(at, 6))
            u = 0

            def window_out(u):
                ph, pt = divmod(u, NT)
                g = ph // 4
                attend_out("W", ph, pt, u, lambda m, kt: wkv[:, kt, 128 + g * 64:192 + g * 64], 2)

            for hp in range(WQ_HEADS // 2):
                for t in range(NT):
                    attend("W", hp, t, wqT[:, hp, :], wkT[:, hp // 4, :], 2)
                    if u:
                        attend_T("W", (u - 1) // NT, (u - 1) % NT, u - 1, 2)
                    if u > 1:
                        window_out(u - 2)
                    u += 1
            attend_T("W", (u - 1) // NT, (u - 1) % NT, u - 1, 2)
            window_out(u - 2)
            window_out(u - 1)
            transposes("woT", wo, KD, y_ready, 3)
            pe.wait_ge(*yT_ready.nth(at, 8))
            for n in range(2):
                run(chunk(("wout", n), ("wout", n), woT, KD, 512))
            transposes("mxT", x, KD, h_ready, 4, 0)
            pe.wait_ge(*hT_ready.nth(at, 16))
            run(chunk(("router", 0), ("router", 0), hT, KD, NE))
            hand_back()
            pe.wait_ge(*route_in.nth(at, 1))
            pe.wait_ge(*psum.vacant(at, ("count", 0)))
            bank = banks[psum.slot(at, ("count", 0))]
            mm(bank[:, 0:NE], upto, places[:, 0, :], start=True, stop=True)
            mm(bank[:, NE:2 * NE], ones, places[:, 0, :], start=True, stop=False)
            mm(bank[:, NE:2 * NE], upto, places[:, 1, :], start=False, stop=True)
            mm(bank[:, 2 * NE:3 * NE], ones, places[:, 0, :], start=True, stop=False)
            mm(bank[:, 2 * NE:3 * NE], ones, places[:, 1, :], start=False,
               stop=True).then_inc(*psum.fills(at, ("count", 0)))

            def expert():
                pe.wait_ge(*select_ready.nth(at, 1))
                for q in range(2):
                    pe.wait_ge(*psum.vacant(at, ("chosen", q)))
                    bank = banks[psum.slot(at, ("chosen", q))]
                    for i in range(4):
                        f = (4 * q + i) * P
                        for t in range(NT):
                            last = mm(bank[:, i * P:(i + 1) * P], xin[:, t, f:f + P], select[:, t, :],
                                      start=t == 0, stop=t == NT - 1)
                    last.then_inc(*psum.fills(at, ("chosen", q)))
                pe.wait_ge(*select_ready.nth(at, 2))
                pe.wait_ge(*psum.vacant(at, ("weigh", 0)))
                bank = banks[psum.slot(at, ("weigh", 0))]
                for t in range(NT):
                    last = turn_over(bank[:, t * P:(t + 1) * P], weigh[:, t, :], ident)
                last.then_inc(*psum.fills(at, ("weigh", 0)))

                def hid_turn(c):
                    pe.wait_ge(*hid_ready.nth(at, c + 1))
                    pe.wait_ge(*psum.vacant(at, ("turn", c)))
                    bank = banks[psum.slot(at, ("turn", c))]
                    for i in range(2):
                        last = turn_over(bank[:, i * P:(i + 1) * P], hid_tok[:, c % 2, i * P:(i + 1) * P], ident)
                    last.then_inc(*psum.fills(at, ("turn", c)))

                pe.wait_ge(*chosen_ready.nth(at, 2))
                n = FFE // 256
                for c in range(n):
                    pe.wait_ge(*weights.full(at, ("up", c)))
                    slot = weights.slot(at, ("up", c))
                    pe.wait_ge(*psum.vacant(at, ("up", c)))
                    bank = banks[psum.slot(at, ("up", c))]
                    for k in range(KD):
                        last = mm(bank[:, :], chosenT[:, k, :], W[:, slot, k * 512:(k + 1) * 512],
                                  start=k == 0, stop=k == KD - 1)
                        if k == 0:
                            hand_back()
                    last.then_inc(*psum.fills(at, ("up", c)))
                    used.append((("up", c), ("up", c)))
                    if c:
                        hid_turn(c - 1)
                acc = []
                for half in range(2):
                    pe.wait_ge(*psum.vacant(at, ("down", half)))
                    acc.append(banks[psum.slot(at, ("down", half))])
                for k in range(FFE // P):
                    c, i = divmod(k, 4)
                    if i == 0:
                        pe.wait_ge(*weights.full(at, ("down", c)))
                        slot = weights.slot(at, ("down", c))
                    if k % 2 == 0:
                        pe.wait_ge(*down_ready.nth(at, k // 2 + 1))
                    for half in range(2):
                        at_ = i * D + half * 512
                        last = mm(acc[half][:, :], hidT[:, k, :], W[:, slot, at_:at_ + 512],
                                  start=k == 0, stop=k == FFE // P - 1)
                        hand_back()
                        if k == FFE // P - 1:
                            last.then_inc(*psum.fills(at, ("down", half)))
                    if k == 0:
                        hid_turn(n - 1)
                    if i == 3 and k < FFE // P - 1:
                        last.then_inc(*weights.frees(at, ("down", c)))
                used.append((("down", c), ("down", 1)))
                hand_back()
                for half in range(2):
                    pe.wait_ge(*chosen_ready.nth(at, 4 + half))
                    for t in range(NT):
                        pe.wait_ge(*psum.vacant(at, ("back", t, half)))
                        bank = banks[psum.slot(at, ("back", t, half))]
                        last = mm(bank[:, :], weighT[:, t, :], chosen_out[:, half, :], start=True, stop=True)
                        last.then_inc(*psum.fills(at, ("back", t, half)))

            with pe.Fori(0, NE) as e:
                at = Pass("expert", e)
                expert()
            pe.wait_ge(*plan_ready.nth(Pass("middle"), 1))
            n_over = pe.value_load(plan[0:1, 0:1], min_val=0, max_val=OVER)
            with pe.If(n_over):
                with pe.Fori(0, n_over) as i:
                    at = Pass("over", i)
                    expert()

        @block.scalar
        def _(act):
            a = Steps()
            do = nc.scalar.activation

            def evacuate(jobs, dst, signal, scale=None):
                for job in jobs:
                    act.wait_ge(*psum.full(a.at, job))
                    bank = banks[psum.slot(a.at, job)]
                    d = dst(job)
                    n = d.shape[1]
                    src = bank[:, 0:n * P].rearrange("p (a i) -> p a i", a=n)
                    do(d, src, ACT.Copy, scale=1.0 if scale is None else scale(job)
                       ).then_inc(*psum.frees(a.at, job))
                    act.wait_ge(*psum.vacated(a.at, job))
                    act.nop().then_inc(*signal.event(a.at))

            def tiles(name, n, dst, signal, scale=None, width=4):
                evacuate([(name, t, q) for t in range(NT) for q in range(n)],
                         lambda j: dst[:, 4 * j[2]:4 * j[2] + width, j[1] * P:(j[1] + 1) * P], signal, scale)

            def evict_probsT(kind, h_, t, u, maps):
                n = maps * (t + 1)
                evacuate([(kind + "t", h_, t)], lambda j: probsT[:, u % 2, 0:n, :], probsT_ready)

            def exps(u, t, maps, sink=False):
                act.wait_ge(*masked.nth(a.at, u + 1))
                K = (t + 1) * P
                b = u % 2
                if sink:
                    do(esink[:, b, :], esink[:, b, :], ACT.Exp).then_inc(act_done, 1)
                    act.wait_ge(act_done, a.count())
                for m in range(maps):
                    i = do(scores[:, b, m, 0:K], scores[:, b, m, 0:K], ACT.Exp,
                           bias=nmax[:, b, m:m + 1], accum_out=rsum[:, b, m:m + 1])
                    if m < maps - 1:
                        i.then_inc(act_done, 1)
                        act.wait_ge(act_done, a.count())
                    else:
                        i.then_inc(*exped.event(a.at))
                        act.wait_ge(*exped.last(a.at))

            def root(n):
                state["var"] += 1
                act.wait_ge(*var_ready.nth(a.at, state["var"]))
                do(inv[:, 0:n], inv[:, 0:n], ACT.Sqrt).then_inc(*std_ready.event(a.at))
                act.wait_ge(*std_ready.last(a.at))

            def hidden(n, func, conv):
                for j in range(n):
                    act.wait_ge(*psum.full(a.at, ("up", j)))
                    bank = banks[psum.slot(a.at, ("up", j))]
                    if conv:
                        act.wait_ge(*hid_pre.nth(a.at, j + 1))
                    if j >= 2:
                        act.wait_ge(*hid_ready.nth(a.at, j - 1))
                    src = work[:, (j % 2) * S:(j % 2 + 1) * S] if conv else bank[:, 0:S]
                    do(acted[:, j % 2, :], src, func).then_inc(*hid_act.event(a.at))
                    act.wait_ge(*hid_act.last(a.at))

            state = {"var": 0}
            a.enter("start")
            act.wait_ge(c_in, 16)
            do(csil, csil, ACT.Silu).then_inc(*c_silu.event(a.at))
            act.wait_ge(*c_silu.last(a.at))
            with act.Fori(0, DEPTH) as l:
                a.enter("layer", l)
                state["var"] = 0
                act.wait_ge(*lam_dots.nth(a.at, 1))
                do(lam[:, 0:2], lam[:, 0:2], ACT.Exp).then_inc(*lam_exps.event(a.at))
                act.wait_ge(*lam_exps.last(a.at))
                tiles("hT", 2, hT, hT_ready)
                tiles("aT", 2, aT, qkT_ready)
                act.wait_ge(*forget_pre.nth(a.at, 1))
                do(tmp[:, 0:8], tmp[:, 0:8], ACT.Exp).then_inc(*forget_exp.event(a.at))
                act.wait_ge(*forget_exp.last(a.at))
                act.wait_ge(*forget_pre.nth(a.at, 2))
                do(tmp[:, 0:8], tmp[:, 0:8], ACT.Ln).then_inc(*forget_ln.event(a.at))
                act.wait_ge(*forget_ln.last(a.at))
                for u in range(8):
                    exps(u, u % NT, 2)
                    evict_probsT("A", u // NT, u % NT, u, 1)
                tiles("bT", 2, bT, qkT_ready, scale=lambda j: B_DH ** -0.5 if j[2] == 0 else 1.0)
                for u in range(8, 16):
                    exps(u, u % NT, 1)
                    evict_probsT("B", (u - 8) // NT, u % NT, u, 1)
                tiles("cT", 2, cT, qkT_ready)
                act.wait_ge(*gate_pre.nth(a.at, 1))
                do(zCg, zCg, ACT.Silu).then_inc(*gate_done.event(a.at))
                act.wait_ge(*gate_done.last(a.at))
                for n, g in enumerate((gA, gB, gC)):
                    act.wait_ge(*gate_pre.nth(a.at, 2 + n))
                    do(g[:, :, :], g[:, :, :], ACT.Sigmoid).then_inc(*gate_done.event(a.at))
                    act.wait_ge(*gate_done.last(a.at))
                root(8)
                root(8)
                tiles("yA", 1, yAT, yT_ready)
                tiles("yB", 1, yBT, yT_ready)
                tiles("yC", 2, yCT, yT_ready)
                tiles("mT", 2, mixT, hT_ready)
                root(2)
                tiles("h2T", 2, hT, hT_ready)
                hidden(FF1 // P, ACT.Gelu, True)
                root(2)
                act.nop().then_inc(act_done, 1)
                act.wait_ge(act_done, a.count())
                act.sem_clear(act_done)
            a.enter("middle")
            state["var"] = 0
            tiles("gxT", 2, hT, hT_ready)
            for p in range(8):
                act.wait_ge(*g_pre.nth(a.at, p + 1))
                do(gT[:, 2 * p:2 * p + 2, :], gT[:, 2 * p:2 * p + 2, :], ACT.Silu).then_inc(*g_act.event(a.at))
                act.wait_ge(*g_act.last(a.at))
            for p in range(4):
                do(gsq[:, 2 * p:2 * p + 2, :], gT[:, 2 * p:2 * p + 2, :], ACT.Square).then_inc(*g_out.event(a.at))
                act.wait_ge(*g_out.last(a.at))
            act.wait_ge(*g_pre.nth(a.at, 9))
            do(beta, beta, ACT.Sigmoid).then_inc(act_done, 1)
            act.wait_ge(act_done, a.count())
            do(tmp[:, 0:16], tmp[:, 0:16], ACT.Exp).then_inc(act_done, 1)
            act.wait_ge(act_done, a.count())
            do(cums[:, 0:8], cums[:, 0:8], ACT.Exp).then_inc(*g_act.event(a.at))
            act.wait_ge(*g_act.last(a.at))
            act.wait_ge(*g_pre.nth(a.at, 10))
            do(tmp[:, 0:16], tmp[:, 0:16], ACT.Ln).then_inc(*g_act.event(a.at))
            act.wait_ge(*g_act.last(a.at))
            act.wait_ge(*g_pre.nth(a.at, 11))
            do(gsq[:, :, :], gsq[:, :, :], ACT.Sqrt).then_inc(*g_act.event(a.at))
            act.wait_ge(*g_act.last(a.at))
            evacuate([("kn", t) for t in range(NT)], lambda j: gkn[:, j[1], :, :], g_out)
            act.wait_ge(*g_pre.nth(a.at, 12))
            do(egc, cums[:, 0:16], ACT.Exp).then_inc(act_done, 1)
            act.wait_ge(act_done, a.count())
            do(egl, egl, ACT.Exp).then_inc(*g_act.event(a.at))
            act.wait_ge(*g_act.last(a.at))
            n_pre = 12
            for t in range(NT):
                n_pre += 1
                act.wait_ge(*g_pre.nth(a.at, n_pre))
                do(gdec[:, :, :], gdec[:, :, :], ACT.Exp).then_inc(*g_act.event(a.at))
                act.wait_ge(*g_act.last(a.at))
                evacuate([("DT", t, q) for q in range(2)], lambda j: gaq[:, 4 * j[2]:4 * j[2] + 4, :], g_act)
                evacuate([("AT", t, q) for q in range(2)], lambda j: gaT[:, 4 * j[2]:4 * j[2] + 4, :], g_act)
                for lv in range(LEVELS):
                    evacuate([("U", t, lv, q) for q in range(2)], lambda j: gu[:, 4 * j[3]:4 * j[3] + 4, :], g_out)
                if t:
                    evacuate([("wT", t, q) for q in range(2)], lambda j: gaT[:, 4 * j[2]:4 * j[2] + 4, :], g_out,
                             scale=lambda j: -1.0)
            act.wait_ge(*gate_pre.nth(a.at, 1))
            do(gz[:, :, :], gz[:, :, :], ACT.Silu).then_inc(*gate_done.event(a.at))
            act.wait_ge(*gate_done.last(a.at))
            state["var"] += 1
            act.wait_ge(*var_ready.nth(a.at, state["var"]))
            do(tmp[:, 0:16], tmp[:, 0:16], ACT.Sqrt).then_inc(*std_ready.event(a.at))
            act.wait_ge(*std_ready.last(a.at))
            tiles("goT", 2, goT, yT_ready)
            root(2)
            tiles("fxT", 2, hT, hT_ready)
            hidden(FF2 // P, ACT.Silu, False)
            root(2)
            tiles("wxT", 2, hT, hT_ready)
            tiles("wqT", 2, wqT, qkT_ready)
            tiles("wkT", 1, wkT, qkT_ready, width=2)
            for u in range(16):
                exps(u, u % NT, 2, sink=True)
                if u:
                    evict_probsT("W", (u - 1) // NT, (u - 1) % NT, u - 1, 2)
            evict_probsT("W", 7, 1, 15, 2)
            tiles("woT", 2, woT, yT_ready)
            root(2)
            tiles("mxT", 2, hT, hT_ready)
            act.wait_ge(*g_pre.nth(a.at, n_pre + 1))
            do(tmp[:, 0:16], tmp[:, 0:16], ACT.Exp).then_inc(*g_act.event(a.at))
            act.wait_ge(*g_act.last(a.at))
            act.nop().then_inc(act_done, 1)
            act.wait_ge(act_done, a.count())
            act.sem_clear(act_done)

            def expert():
                evacuate([("chosen", q) for q in range(2)], lambda j: chosenT[:, 4 * j[1]:4 * j[1] + 4, :],
                         chosen_ready)
                evacuate([("weigh", 0)], lambda j: weighT, chosen_ready)
                n = FFE // 256
                for c in range(n):
                    act.wait_ge(*psum.full(a.at, ("up", c)))
                    bank = banks[psum.slot(a.at, ("up", c))]
                    if c >= 2:
                        act.wait_ge(*hid_ready.nth(a.at, c - 1))
                    do(acted[:, c % 2, :], bank[:, 0:S], ACT.Silu).then_inc(*hid_act.event(a.at))
                    act.wait_ge(*hid_act.last(a.at))
                    if c:
                        evacuate([("turn", c - 1)], lambda j: hidT[:, 2 * j[1]:2 * j[1] + 2, :], down_ready)
                evacuate([("turn", n - 1)], lambda j: hidT[:, 2 * j[1]:2 * j[1] + 2, :], down_ready)
                evacuate([("down", half) for half in range(2)],
                         lambda j: chosen_out[:, j[1], :].rearrange("p (a i) -> p a i", a=4), chosen_ready)

            with act.Fori(0, NE) as e:
                a.enter("expert", e)
                expert()
            act.wait_ge(*plan_ready.nth(Pass("middle"), 1))
            n_over = act.value_load(plan[0:1, 0:1], min_val=0, max_val=OVER)
            with act.If(n_over):
                with act.Fori(0, n_over) as i:
                    a.enter("over", i)
                    expert()
            a.enter("end")
            state["var"] = 0
            root(2)

        @block.vector
        def _(dve):
            v = Steps()
            V = nc.vector
            tt, ts, stt = V.tensor_tensor, V.tensor_scalar, V.scalar_tensor_tensor

            def add_row(job, r, dst, width=512, plus=None):
                dve.wait_ge(*psum.full(v.at, job))
                bank = banks[psum.slot(v.at, job)]
                if plus is None:
                    tt(dst, bank[:, 0:width], r[:, 0:width], ALU.add).then_inc(*psum.frees(v.at, job))
                    dve.wait_ge(*psum.vacated(v.at, job))
                else:
                    stt(dst, bank[:, 0:width], plus, r[:, 0:width], ALU.add, ALU.add).then_inc(*psum.frees(v.at, job))
                    dve.wait_ge(*psum.vacated(v.at, job))

            def chunk_in(kind, c, dst):
                dve.wait_ge(*rows.full(v.at, (kind, c)))
                r = R[:, rows.slot(v.at, (kind, c)), :]
                for t in range(NT):
                    add_row((kind, c, t), r, dst(t))
                dve.nop().then_inc(*rows.frees(v.at, (kind, c)))

            def std(n):
                state["std"] += 1
                dve.wait_ge(*std_ready.nth(v.at, state["std"]))
                V.reciprocal(inv[:, 0:n], inv[:, 0:n]).then_inc(dve_done, 1)
                dve.wait_ge(dve_done, v.count())

            def layernorm(name):
                for t in range(NT):
                    for n in range(2):
                        V.bn_stats(stats[:, 2 * t + n, :], x[:, t, n * 512:(n + 1) * 512]).then_inc(dve_done, 1)
                        dve.wait_ge(dve_done, v.count())
                    V.bn_aggr(meanvar[:, t, :], stats[:, 2 * t:2 * t + 2, :]).then_inc(dve_done, 1)
                    dve.wait_ge(dve_done, v.count())
                ts(inv[:, 0:2], meanvar[:, 0:2, 1], EPS, None, ALU.add).then_inc(*var_ready.event(v.at))
                dve.wait_ge(*var_ready.last(v.at))
                std(2)
                for t in range(NT):
                    ts(x[:, t, :], x[:, t, :], meanvar[:, t, 0:1], inv[:, t:t + 1], ALU.subtract, ALU.mult).then_inc(dve_done, 1)
                    dve.wait_ge(dve_done, v.count())
                for n in range(2):
                    dve.wait_ge(*rows.full(v.at, (name, f"g{n}")))
                    g = R[:, rows.slot(v.at, (name, f"g{n}")), :]
                    dve.wait_ge(*rows.full(v.at, (name, f"b{n}")))
                    b = R[:, rows.slot(v.at, (name, f"b{n}")), :]
                    half = x[:, :, n * 512:(n + 1) * 512]
                    tt(half, half, g.unsqueeze(1).to_broadcast([P, NT, 512]), ALU.mult).then_inc(dve_done, 1)
                    dve.wait_ge(dve_done, v.count())
                    tt(half, half, b.unsqueeze(1).to_broadcast([P, NT, 512]), ALU.add).then_inc(dve_done, 1)
                    dve.wait_ge(dve_done, v.count())
                    dve.nop().then_inc(*rows.frees(v.at, (name, f"g{n}")))
                    dve.nop().then_inc(*rows.frees(v.at, (name, f"b{n}")))

            def modulate(shift, scale):
                for t in range(NT):
                    ht = h[:, t, :].rearrange("p (a n) -> p a n", a=2)
                    xt = x[:, t, :].rearrange("p (a n) -> p a n", a=2)
                    tt(ht, xt, mod[:, scale:scale + 2, :], ALU.mult).then_inc(dve_done, 1)
                    dve.wait_ge(dve_done, v.count())
                    tt(ht, ht, mod[:, shift:shift + 2, :], ALU.add).then_inc(*h_ready.event(v.at))
                    dve.wait_ge(*h_ready.last(v.at))

            def residual(jobs, gate, alpha):
                for job in jobs:
                    t, n = (job[2], job[1]) if job[0] != "down" else (job[1], job[2])
                    dve.wait_ge(*psum.full(v.at, job))
                    bank = banks[psum.slot(v.at, job)]
                    dst = x[:, t, n * 512:(n + 1) * 512]
                    if gate is None:
                        stt(dst, dst, alpha, bank[:, :], ALU.mult, ALU.add).then_inc(*psum.frees(v.at, job))
                        dve.wait_ge(*psum.vacated(v.at, job))
                    else:
                        tt(work[:, 0:512], bank[:, :], mod[:, gate + n, :], ALU.mult).then_inc(*psum.frees(v.at, job))
                        dve.wait_ge(*psum.vacated(v.at, job))
                        stt(dst, dst, alpha, work[:, 0:512], ALU.mult, ALU.add).then_inc(dve_done, 1)
                        dve.wait_ge(dve_done, v.count())

            def outs(name):
                return [(name, n, t) for n in range(2) for t in range(NT)]

            DOWN = [("down", t, n) for t in range(NT) for n in range(2)]

            def finish_hidden(j, hid, conv):
                dve.wait_ge(*hid_act.nth(v.at, j + 1))
                dve.wait_ge(*psum.full(v.at, ("up", j)))
                bank = banks[psum.slot(v.at, ("up", j))]
                tt(hid[:, j, :], acted[:, j % 2, :], bank[:, S:2 * S], ALU.mult).then_inc(*psum.frees(v.at, ("up", j)))
                dve.wait_ge(*psum.vacated(v.at, ("up", j)))
                dve.nop().then_inc(*hid_ready.event(v.at))

            def hidden(n, hid):
                for j in range(n):
                    finish_hidden(j, hid, False)

            def hidden_conv(n, hid, taps):
                for j in range(n):
                    dve.wait_ge(*psum.full(v.at, ("up", j)))
                    u = banks[psum.slot(v.at, ("up", j))]
                    c = work[:, (j % 2) * S:(j % 2 + 1) * S]
                    ts(c, u[:, 0:S], taps[:, 2 * n + j:2 * n + j + 1], taps[:, 3 * n + j:3 * n + j + 1], ALU.mult, ALU.add).then_inc(dve_done, 1)
                    dve.wait_ge(dve_done, v.count())
                    stt(c[:, 1:S], u[:, 0:S - 1], taps[:, n + j:n + j + 1], c[:, 1:S], ALU.mult, ALU.add).then_inc(dve_done, 1)
                    dve.wait_ge(dve_done, v.count())
                    stt(c[:, 2:S], u[:, 0:S - 2], taps[:, j:j + 1], c[:, 2:S], ALU.mult, ALU.add).then_inc(*hid_pre.event(v.at))
                    dve.wait_ge(*hid_pre.last(v.at))
                    if j:
                        finish_hidden(j - 1, hid, True)
                finish_hidden(n - 1, hid, True)

            def mask(kind, h_, t, u, maps, scale, bias):
                K = (t + 1) * P
                b = u % 2
                for m in range(maps):
                    job = (kind + "s", h_, t, m)
                    dve.wait_ge(*psum.full(v.at, job))
                    bank = banks[psum.slot(v.at, job)]
                    stt(scores[:, b, m, 0:K], bank[:, 0:K], scale, bias(m, K), ALU.mult, ALU.add).then_inc(*psum.frees(v.at, job))
                    dve.wait_ge(*psum.vacated(v.at, job))
                if kind != "W":
                    V.reduce_max(nmax[:, b, 0:maps], scores[:, b, 0:maps, 0:K], axis=AX, negate=True).then_inc(*masked.event(v.at))
                    dve.wait_ge(*masked.last(v.at))
                else:
                    V.reduce_max(nmax[:, b, :], scores[:, b, :, 0:K], axis=AX).then_inc(dve_done, 1)
                    dve.wait_ge(dve_done, v.count())
                    sink = sinks[:, 2 * h_:2 * h_ + 2]
                    tt(nmax[:, b, :], nmax[:, b, :], sink, ALU.max).then_inc(dve_done, 1)
                    dve.wait_ge(dve_done, v.count())
                    ts(nmax[:, b, :], nmax[:, b, :], -1.0, None, ALU.mult).then_inc(dve_done, 1)
                    dve.wait_ge(dve_done, v.count())
                    tt(esink[:, b, :], sink, nmax[:, b, :], ALU.add).then_inc(*masked.event(v.at))
                    dve.wait_ge(*masked.last(v.at))

            state = {"std": 0}
            v.enter("start")
            dve.wait_ge(*c_silu.nth(v.at, 1))
            dve.wait_ge(consts_in, 16)
            dve.wait_ge(x_in, 16)
            dve.nop().then_inc(dve_done, 1)
            dve.wait_ge(dve_done, v.count())
            dve.sem_clear(dve_done)
            with dve.Fori(0, DEPTH) as l:
                v.enter("layer", l)
                state["std"] = 0
                V.tensor_copy(cspread, csil.unsqueeze(2).to_broadcast([P, KD, P])).then_inc(*c_ready.event(v.at))
                dve.wait_ge(*c_ready.last(v.at))
                for c in range(12):
                    dve.wait_ge(*rows.full(v.at, ("ada", c)))
                    r = R[:, rows.slot(v.at, ("ada", c)), :]
                    add_row(("ada", c), r, mod[:, c, :], plus=1.0 if c in (2, 3, 8, 9) else None)
                    dve.nop().then_inc(*rows.frees(v.at, ("ada", c)))
                    if c == 3:
                        modulate(0, 2)
                dve.wait_ge(*rows.full(v.at, ("lam", 0)))
                r = R[:, rows.slot(v.at, ("lam", 0)), :]
                pairs = r[:, 0:256].rearrange("p (a b n) -> p a b n", a=2, b=2)
                dots = work[:, 0:128].rearrange("p (a n) -> p a n", a=2)
                tt(dots, pairs[:, :, 0, :], pairs[:, :, 1, :], ALU.mult).then_inc(dve_done, 1)
                dve.wait_ge(dve_done, v.count())
                V.reduce_sum(lam[:, 0:2], dots, axis=AX).then_inc(*lam_dots.event(v.at))
                dve.wait_ge(*lam_dots.last(v.at))
                dve.wait_ge(*lam_exps.nth(v.at, 1))
                tt(lam[:, 2:3], lam[:, 1:2], lam[:, 0:1], ALU.subtract).then_inc(dve_done, 1)
                dve.wait_ge(dve_done, v.count())
                tt(lam[:, 2:3], lam[:, 2:3], r[:, 256:257], ALU.subtract).then_inc(dve_done, 1)
                dve.wait_ge(dve_done, v.count())
                V.tensor_copy(lam[:, 3:4], r[:, 257:258]).then_inc(dve_done, 1)
                dve.wait_ge(dve_done, v.count())
                dve.nop().then_inc(*rows.frees(v.at, ("lam", 0)))

                def take_chunk(kind, c, dst, signal):
                    dve.wait_ge(*rows.full(v.at, (kind, c)))
                    r = R[:, rows.slot(v.at, (kind, c)), :]
                    for t in range(NT):
                        add_row((kind, c, t), r, dst(t))
                        if signal is not None:
                            dve.nop().then_inc(*signal.event(v.at))
                    dve.nop().then_inc(*rows.frees(v.at, (kind, c)))

                for c in range(3):
                    take_chunk("A", c, lambda t: zA[:, t, c * 512:(c + 1) * 512], zA_ready)
                for c in range(3):
                    take_chunk("B", c, lambda t: zB[:, t, c * 512:(c + 1) * 512], zB_ready)
                dve.wait_ge(*rows.full(v.at, ("bf", 0)))
                r = R[:, rows.slot(v.at, ("bf", 0)), :]
                for t in range(NT):
                    add_row(("bf", 0, t), r, logf[:, 4 * t:4 * t + 4], width=4)
                dve.nop().then_inc(*rows.frees(v.at, ("bf", 0)))
                f8, t8 = logf[:, 0:8], tmp[:, 0:8]
                stt(t8, f8, -1.0, f8, ALU.mult, ALU.min).then_inc(dve_done, 1)
                dve.wait_ge(dve_done, v.count())
                dve.nop().then_inc(*forget_pre.event(v.at))
                dve.wait_ge(*forget_exp.nth(v.at, 1))
                ts(t8, t8, 1.0, None, ALU.add).then_inc(dve_done, 1)
                dve.wait_ge(dve_done, v.count())
                dve.nop().then_inc(*forget_pre.event(v.at))
                dve.wait_ge(*forget_ln.nth(v.at, 1))
                stt(f8, f8, 0.0, t8, ALU.min, ALU.subtract).then_inc(dve_done, 1)
                dve.wait_ge(dve_done, v.count())
                f3 = f8.rearrange("p (t h) -> p t h", t=NT)
                for t in range(NT):
                    V.tensor_copy(forget[:, t, :, :], f3[:, t, :].unsqueeze(2).to_broadcast([P, B_HEADS, S])).then_inc(dve_done, 1)
                    dve.wait_ge(dve_done, v.count())
                for t in range(NT):
                    i = ts(forget_neg[:, t, :, :], f3[:, t, :].unsqueeze(2).to_broadcast([P, B_HEADS, P]),
                           -1.0, None, ALU.mult)
                    if t == 0:
                        i.then_inc(dve_done, 1)
                        dve.wait_ge(dve_done, v.count())
                    else:
                        i.then_inc(*forget_ready.event(v.at))
                        dve.wait_ge(*forget_ready.last(v.at))

                def background():
                    def one(kind, c, dst):
                        dve.wait_ge(*rows.full(v.at, (kind, c)))
                        r = R[:, rows.slot(v.at, (kind, c)), :]
                        for t in range(NT):
                            add_row((kind, c, t), r, dst(t))
                            if t == NT - 1:
                                dve.nop().then_inc(*rows.frees(v.at, (kind, c)))
                                if kind == "C" and c == 5:
                                    dve.nop().then_inc(*gate_pre.event(v.at))
                                if kind == "gate" and c % 2:
                                    dve.nop().then_inc(*gate_pre.event(v.at))
                            yield
                    for c in range(6):
                        part = (zCqk, zCv, zCg)[c // 2]
                        yield from one("C", c, lambda t: part[:, t, (c % 2) * 512:(c % 2 + 1) * 512])
                    for c in range(6):
                        g = (gA, gB, gC)[c // 2]
                        yield from one("gate", c, lambda t: g[:, t, (c % 2) * 512:(c % 2 + 1) * 512])

                bg = background()

                def a_out(u):
                    job = ("Ao", u // NT, u % NT)
                    dve.wait_ge(*psum.full(v.at, job))
                    bank = banks[psum.slot(v.at, job)]
                    V.tensor_copy(yA[:, u % NT, (u // NT) * P:(u // NT + 1) * P], bank[:, 0:P]).then_inc(*psum.frees(v.at, job))
                    dve.wait_ge(*psum.vacated(v.at, job))

                def b_out(u):
                    job = ("Bo", (u - 8) // NT, u % NT)
                    dve.wait_ge(*psum.full(v.at, job))
                    bank = banks[psum.slot(v.at, job)]
                    hh = (u - 8) // NT
                    ts(yB[:, u % NT, hh * P:(hh + 1) * P], bank[:, 0:P],
                                         rinv[:, u % 3, 0:1], None, ALU.mult).then_inc(*psum.frees(v.at, job))
                    dve.wait_ge(*psum.vacated(v.at, job))

                for u in range(8):
                    h_, t = divmod(u, NT)
                    K, b = (t + 1) * P, u % 2
                    mask("A", h_, t, u, 2, A_DQK ** -0.5, lambda m, K: blocks[:, 2 * P - K:2 * P])
                    dve.wait_ge(*exped.nth(v.at, u + 1))
                    V.reciprocal(rsum[:, b, :], rsum[:, b, :]).then_inc(dve_done, 1)
                    dve.wait_ge(dve_done, v.count())
                    tt(rsum[:, b, 1:2], rsum[:, b, 1:2], lam[:, 2:3], ALU.mult).then_inc(dve_done, 1)
                    dve.wait_ge(dve_done, v.count())
                    ts(scores[:, b, 1, 0:K], scores[:, b, 1, 0:K], rsum[:, b, 1:2], None, ALU.mult).then_inc(dve_done, 1)
                    dve.wait_ge(dve_done, v.count())
                    stt(scores[:, b, 0, 0:K], scores[:, b, 0, 0:K], rsum[:, b, 0:1],
                                      scores[:, b, 1, 0:K], ALU.mult, ALU.add).then_inc(*probs.event(v.at))
                    dve.wait_ge(*probs.last(v.at))
                    next(bg)
                    if u:
                        a_out(u - 1)
                a_out(7)

                def rotate(t):
                    for s in range(2):
                        z = zCqk[:, t, s * 512:(s + 1) * 512].rearrange("p (h f) -> p h f", h=C_HEADS)
                        t1, t2 = z[:, :, 0:64], z[:, :, 64:128]
                        w = [work[:, i * 256:(i + 1) * 256].rearrange("p (h f) -> p h f", h=C_HEADS) for i in range(3)]
                        cs = cos[:, t, :].unsqueeze(1).to_broadcast([P, C_HEADS, 64])
                        sn = sin[:, t, :].unsqueeze(1).to_broadcast([P, C_HEADS, 64])
                        tt(w[0], t1, cs, ALU.mult).then_inc(dve_done, 1)
                        dve.wait_ge(dve_done, v.count())
                        tt(w[1], t2, sn, ALU.mult).then_inc(dve_done, 1)
                        dve.wait_ge(dve_done, v.count())
                        tt(w[2], t1, sn, ALU.mult).then_inc(dve_done, 1)
                        dve.wait_ge(dve_done, v.count())
                        tt(t1, w[0], w[1], ALU.subtract).then_inc(dve_done, 1)
                        dve.wait_ge(dve_done, v.count())
                        tt(w[0], t2, cs, ALU.mult).then_inc(dve_done, 1)
                        dve.wait_ge(dve_done, v.count())
                        tt(t2, w[0], w[2], ALU.add).then_inc(dve_done, 1)
                        dve.wait_ge(dve_done, v.count())

                for u in range(8, 16):
                    h_, t = divmod(u - 8, NT)
                    b = u % 2
                    mask("B", h_, t, u, 1, 1.0, lambda m, K: causal[:, 2 * P - K:2 * P])
                    dve.wait_ge(*exped.nth(v.at, u + 1))
                    V.reciprocal(rinv[:, u % 3, 0:1], rsum[:, b, 0:1]).then_inc(*probs.event(v.at))
                    dve.wait_ge(*probs.last(v.at))
                    next(bg)
                    if u > 8:
                        b_out(u - 1)
                    if u in (9, 10):
                        rotate(u - 9)
                        dve.nop().then_inc(*zC_ready.event(v.at))
                b_out(15)
                next(bg)
                for h_ in range(C_HEADS):
                    flat = scores[:, h_ % 2, :, :].rearrange("p m k -> p (m k)")
                    for j in range(NT):
                        job = ("Cs", h_, j)
                        dve.wait_ge(*psum.full(v.at, job))
                        bank = banks[psum.slot(v.at, job)]
                        n, o = S - j * P, j * S
                        tt(flat[:, o:o + n], bank[:, 0:n], decay[:, h_, 0:n], ALU.mult).then_inc(*psum.frees(v.at, job))
                        dve.wait_ge(*psum.vacated(v.at, job))
                        dve.nop().then_inc(*retained.event(v.at))
                    next(bg, None)
                    for t in range(NT):
                        job = ("Co", h_, t)
                        dve.wait_ge(*psum.full(v.at, job))
                        bank = banks[psum.slot(v.at, job)]
                        V.bn_stats(stats[:, 0, :], bank[:, 0:C_DV]).then_inc(dve_done, 1)
                        dve.wait_ge(dve_done, v.count())
                        V.bn_aggr(meanvar[:, 4 * t + h_, :], stats[:, 0, :]).then_inc(dve_done, 1)
                        dve.wait_ge(dve_done, v.count())
                        V.tensor_copy(yC[:, t, h_ * C_DV:(h_ + 1) * C_DV], bank[:, 0:C_DV]).then_inc(*psum.frees(v.at, job))
                        dve.wait_ge(*psum.vacated(v.at, job))
                for _ in bg:
                    pass
                for t in range(NT):
                    sq = work[:, 0:512]
                    tt(sq, yA[:, t, :], yA[:, t, :], ALU.mult).then_inc(dve_done, 1)
                    dve.wait_ge(dve_done, v.count())
                    V.reduce_sum(inv[:, 4 * t:4 * t + 4], sq.rearrange("p (h f) -> p h f", h=A_HEADS), axis=AX).then_inc(dve_done, 1)
                    dve.wait_ge(dve_done, v.count())
                ts(inv, inv, 1.0 / P, EPS, ALU.mult, ALU.add).then_inc(*var_ready.event(v.at))
                dve.wait_ge(*var_ready.last(v.at))
                std(8)
                dve.wait_ge(*rows.full(v.at, ("gdiff", 0)))
                g = R[:, rows.slot(v.at, ("gdiff", 0)), :]
                for t in range(NT):
                    ya = yA[:, t, :].rearrange("p (h f) -> p h f", h=A_HEADS)
                    tt(ya, ya, inv[:, 4 * t:4 * t + 4].unsqueeze(2).to_broadcast([P, A_HEADS, P]), ALU.mult).then_inc(dve_done, 1)
                    dve.wait_ge(dve_done, v.count())
                    stt(yA[:, t, :], yA[:, t, :], lam[:, 3:4], g, ALU.mult, ALU.mult).then_inc(*y_ready.event(v.at))
                    dve.wait_ge(*y_ready.last(v.at))
                dve.nop().then_inc(*rows.frees(v.at, ("gdiff", 0)))
                dve.nop().then_inc(*y_ready.event(v.at))
                dve.nop().then_inc(*y_ready.event(v.at))
                ts(inv, meanvar[:, 0:8, 1], EPS, None, ALU.add).then_inc(*var_ready.event(v.at))
                dve.wait_ge(*var_ready.last(v.at))
                std(8)
                dve.wait_ge(*gate_done.nth(v.at, 1))
                dve.wait_ge(*rows.full(v.at, ("gret", 0)))
                g0 = R[:, rows.slot(v.at, ("gret", 0)), :]
                dve.wait_ge(*rows.full(v.at, ("gret", 1)))
                g1 = R[:, rows.slot(v.at, ("gret", 1)), :]
                for t in range(NT):
                    for h_ in range(C_HEADS):
                        yc = yC[:, t, h_ * C_DV:(h_ + 1) * C_DV]
                        ts(yc, yc, meanvar[:, 4 * t + h_, 0:1], inv[:, 4 * t + h_:4 * t + h_ + 1],
                             ALU.subtract, ALU.mult).then_inc(dve_done, 1)
                        dve.wait_ge(dve_done, v.count())
                    for n, g in enumerate((g0, g1)):
                        yc = yC[:, t, n * 512:(n + 1) * 512]
                        tt(yc, yc, g, ALU.mult).then_inc(dve_done, 1)
                        dve.wait_ge(dve_done, v.count())
                    tt(yC[:, t, :], yC[:, t, :], zCg[:, t, :], ALU.mult).then_inc(*y_ready.event(v.at))
                    dve.wait_ge(*y_ready.last(v.at))
                dve.nop().then_inc(*rows.frees(v.at, ("gret", 0)))
                dve.nop().then_inc(*rows.frees(v.at, ("gret", 1)))
                for b_, g in enumerate((gA, gB, gC)):
                    dve.wait_ge(*gate_done.nth(v.at, 2 + b_))
                    for n in range(2):
                        for t in range(NT):
                            job = ("p", b_, n, t)
                            dve.wait_ge(*psum.full(v.at, job))
                            bank = banks[psum.slot(v.at, job)]
                            cols = slice(n * 512, (n + 1) * 512)
                            if b_ == 0:
                                tt(mix[:, t, cols], bank[:, :], g[:, t, cols], ALU.mult).then_inc(*psum.frees(v.at, job))
                                dve.wait_ge(*psum.vacated(v.at, job))
                            else:
                                tt(work[:, 0:512], bank[:, :], g[:, t, cols], ALU.mult).then_inc(*psum.frees(v.at, job))
                                dve.wait_ge(*psum.vacated(v.at, job))
                                tt(mix[:, t, cols], mix[:, t, cols], work[:, 0:512], ALU.add).then_inc(dve_done, 1)
                                dve.wait_ge(dve_done, v.count())
                dve.nop().then_inc(*h_ready.event(v.at))
                dve.nop().then_inc(*h_ready.event(v.at))
                residual(outs("out"), 4, ALPHA)
                layernorm("ln1")
                modulate(6, 8)
                dve.wait_ge(*rows.full(v.at, ("conv", 0)))
                taps = R[:, rows.slot(v.at, ("conv", 0)), :]
                hidden_conv(FF1 // P, hid1, taps)
                dve.nop().then_inc(*rows.frees(v.at, ("conv", 0)))
                residual(DOWN, 10, ALPHA)
                layernorm("ln2")
                dve.nop().then_inc(dve_done, 1)
                dve.wait_ge(dve_done, v.count())
                dve.sem_clear(dve_done)

            v.enter("middle")
            state["std"] = 0
            dve.nop().then_inc(*h_ready.event(v.at))
            dve.wait_ge(*rows.full(v.at, ("gconv", 0)))
            taps = R[:, rows.slot(v.at, ("gconv", 0)), :]
            for p in range(8):
                dve.wait_ge(*psum.full(v.at, ("qkv", p)))
                u = banks[psum.slot(v.at, ("qkv", p))]
                for g in range(2):
                    f = 2 * p + g
                    c, s = gT[:, f, :], u[:, g * S:(g + 1) * S]
                    ts(c, s, taps[:, 48 + f:49 + f], None, ALU.mult).then_inc(dve_done, 1)
                    dve.wait_ge(dve_done, v.count())
                    for back in range(1, GDN_TAPS):
                        tap = 16 * (GDN_TAPS - 1 - back) + f
                        i = stt(c[:, back:S], s[:, 0:S - back], taps[:, tap:tap + 1], c[:, back:S], ALU.mult, ALU.add)
                        if g == 1 and back == GDN_TAPS - 1:
                            i.then_inc(*psum.frees(v.at, ("qkv", p)))
                            dve.wait_ge(*psum.vacated(v.at, ("qkv", p)))
                            dve.nop().then_inc(*g_pre.event(v.at))
                        else:
                            i.then_inc(dve_done, 1)
                            dve.wait_ge(dve_done, v.count())
            dve.nop().then_inc(*rows.frees(v.at, ("gconv", 0)))
            for c in range(2):
                for t in range(NT):
                    dve.wait_ge(*psum.full(v.at, ("z", c, t)))
                    bank = banks[psum.slot(v.at, ("z", c, t))]
                    V.tensor_copy(gz[:, t, c * 512:(c + 1) * 512], bank[:, :]).then_inc(*psum.frees(v.at, ("z", c, t)))
                    dve.wait_ge(*psum.vacated(v.at, ("z", c, t)))
            dve.nop().then_inc(*gate_pre.event(v.at))
            dve.wait_ge(*rows.full(v.at, ("gpar", 0)))
            par = R[:, rows.slot(v.at, ("gpar", 0)), :]
            d16 = decays.rearrange("p (t h) -> p t h", t=NT)
            b16 = beta.rearrange("p (t h) -> p t h", t=NT)
            for t in range(NT):
                dve.wait_ge(*psum.full(v.at, ("ba", 0, t)))
                bank = banks[psum.slot(v.at, ("ba", 0, t))]
                V.tensor_copy(b16[:, t, :], bank[:, 0:8]).then_inc(dve_done, 1)
                dve.wait_ge(dve_done, v.count())
                tt(d16[:, t, :], bank[:, 8:16], par[:, 8:16], ALU.add).then_inc(*psum.frees(v.at, ("ba", 0, t)))
                dve.wait_ge(*psum.vacated(v.at, ("ba", 0, t)))
            V.tensor_copy(cums[:, 0:8], par[:, 0:8]).then_inc(dve_done, 1)
            dve.wait_ge(dve_done, v.count())
            V.tensor_copy(nw, par[:, 16:144]).then_inc(dve_done, 1)
            dve.wait_ge(dve_done, v.count())
            dve.nop().then_inc(*rows.frees(v.at, ("gpar", 0)))
            t16 = tmp[:, 0:16]
            stt(t16, decays, -1.0, decays, ALU.mult, ALU.min).then_inc(dve_done, 1)
            dve.wait_ge(dve_done, v.count())
            dve.nop().then_inc(*g_pre.event(v.at))
            dve.wait_ge(*g_act.nth(v.at, 9))
            ts(t16, t16, 1.0, None, ALU.add).then_inc(dve_done, 1)
            dve.wait_ge(dve_done, v.count())
            dve.nop().then_inc(*g_pre.event(v.at))
            dve.wait_ge(*g_act.nth(v.at, 10))
            stt(decays, decays, 0.0, t16, ALU.max, ALU.add).then_inc(dve_done, 1)
            dve.wait_ge(dve_done, v.count())
            tt(d16, d16, cums[:, 0:8].unsqueeze(1).to_broadcast([P, NT, GV]), ALU.mult).then_inc(dve_done, 1)
            dve.wait_ge(dve_done, v.count())
            ts(decays, decays, -1.0, None, ALU.mult).then_inc(*g_in.event(v.at))
            dve.wait_ge(*g_in.last(v.at))
            for t in range(NT):
                for q in range(2):
                    dve.wait_ge(*psum.full(v.at, ("vn", t, q)))
                    bank = banks[psum.slot(v.at, ("vn", t, q))]
                    tt(gvb[:, t, 4 * q:4 * q + 4, :], bank[:, :].rearrange("p (a i) -> p a i", a=4),
                              b16[:, t, 4 * q:4 * q + 4].unsqueeze(2).to_broadcast([P, 4, P]), ALU.mult).then_inc(*psum.frees(v.at, ("vn", t, q)))
                    dve.wait_ge(*psum.vacated(v.at, ("vn", t, q)))
            for p in range(4):
                dve.wait_ge(*psum.full(v.at, ("ss", p)))
                bank = banks[psum.slot(v.at, ("ss", p))]
                ts(gsq[:, 2 * p:2 * p + 2, :].rearrange("p a n -> p (a n)"), bank[:, :],
                                           GDN_EPS, None, ALU.add).then_inc(*psum.frees(v.at, ("ss", p)))
                dve.wait_ge(*psum.vacated(v.at, ("ss", p)))
            dve.nop().then_inc(*g_pre.event(v.at))
            dve.wait_ge(*g_act.nth(v.at, 11))
            V.reciprocal(gsq[:, :, :], gsq[:, :, :]).then_inc(dve_done, 1)
            dve.wait_ge(dve_done, v.count())
            stt(gq, gq, GD ** -0.5, gsq[:, 0:4, :], ALU.mult, ALU.mult).then_inc(dve_done, 1)
            dve.wait_ge(dve_done, v.count())
            tt(gk, gk, gsq[:, 4:8, :], ALU.mult).then_inc(*g_in.event(v.at))
            dve.wait_ge(*g_in.last(v.at))
            dve.wait_ge(*psum.full(v.at, ("cum", 0)))
            bank = banks[psum.slot(v.at, ("cum", 0))]
            V.tensor_copy(cums, bank[:, 0:32]).then_inc(dve_done, 1)
            dve.wait_ge(dve_done, v.count())
            tt(egl, cums[:, 16:32], cums[:, 0:16], ALU.subtract).then_inc(*psum.frees(v.at, ("cum", 0)))
            dve.wait_ge(*psum.vacated(v.at, ("cum", 0)))
            dve.nop().then_inc(*g_pre.event(v.at))
            dve.wait_ge(*g_act.nth(v.at, 12))
            n_act = 12
            e16 = egc.rearrange("p (t h) -> p t h", t=NT)
            l16 = egl.rearrange("p (t h) -> p t h", t=NT)

            def spread8(col):
                return col.unsqueeze(2).to_broadcast([P, GV, P])

            def pairs8(t):
                return gkn[:, t, :, :].unsqueeze(2).to_broadcast([P, GK, 2, P])

            def split8(m):
                return m.rearrange("p (a b) i -> p a b i", b=2)

            for t in range(NT):
                V.tensor_copy(gplus, spread8(d16[:, t, :])).then_inc(dve_done, 1)
                dve.wait_ge(dve_done, v.count())
                ts(gminus, spread8(d16[:, t, :]), -1.0, None, ALU.mult).then_inc(*g_in.event(v.at))
                dve.wait_ge(*g_in.last(v.at))
                for q in range(2):
                    dve.wait_ge(*psum.full(v.at, ("G", t, q)))
                    bank = banks[psum.slot(v.at, ("G", t, q))]
                    tt(gdec[:, 4 * q:4 * q + 4, :], bank[:, :].rearrange("p (a i) -> p a i", a=4),
                              causal[:, P:2 * P].unsqueeze(1).to_broadcast([P, 4, P]), ALU.add).then_inc(*psum.frees(v.at, ("G", t, q)))
                    dve.wait_ge(*psum.vacated(v.at, ("G", t, q)))
                dve.nop().then_inc(*g_pre.event(v.at))
                n_act += 1
                dve.wait_ge(*g_act.nth(v.at, n_act))
                dve.wait_ge(*psum.full(v.at, ("kk", t)))
                bank = banks[psum.slot(v.at, ("kk", t))]
                kk = bank[:, :].rearrange("p (a i) -> p a i", a=4)
                for half in range(2):
                    i = tt(split8(gpair)[:, :, half, :], kk, split8(gdec)[:, :, half, :], ALU.mult)
                    if half == 0:
                        i.then_inc(dve_done, 1)
                        dve.wait_ge(dve_done, v.count())
                    else:
                        i.then_inc(*psum.frees(v.at, ("kk", t)))
                        dve.wait_ge(*psum.vacated(v.at, ("kk", t)))
                tt(gpair, gpair, const("strict").unsqueeze(1).to_broadcast([P, GV, P]), ALU.mult).then_inc(dve_done, 1)
                dve.wait_ge(dve_done, v.count())
                tt(gpair, gpair, spread8(b16[:, t, :]), ALU.mult).then_inc(*g_in.event(v.at))
                dve.wait_ge(*g_in.last(v.at))
                n_act += 2
                dve.wait_ge(*g_act.nth(v.at, n_act))
                dve.wait_ge(*psum.full(v.at, ("qk", t)))
                bank = banks[psum.slot(v.at, ("qk", t))]
                qk = bank[:, :].rearrange("p (a i) -> p a i", a=4)
                for half in range(2):
                    g = split8(gaq)[:, :, half, :]
                    i = tt(g, qk, g, ALU.mult)
                    if half == 0:
                        i.then_inc(dve_done, 1)
                        dve.wait_ge(dve_done, v.count())
                    else:
                        i.then_inc(*psum.frees(v.at, ("qk", t)))
                        dve.wait_ge(*psum.vacated(v.at, ("qk", t)))
                n_act += 2
                dve.wait_ge(*g_act.nth(v.at, n_act))
                eye = ident.unsqueeze(1).to_broadcast([P, GV, P])
                V.tensor_copy(gt, eye).then_inc(dve_done, 1)
                dve.wait_ge(dve_done, v.count())
                V.tensor_copy(gtT, eye).then_inc(dve_done, 1)
                dve.wait_ge(dve_done, v.count())
                for lv in range(LEVELS):
                    tt(gbT, gaT, levels[:, lv, :].unsqueeze(1).to_broadcast([P, GV, P]), ALU.mult).then_inc(*g_in.event(v.at))
                    dve.wait_ge(*g_in.last(v.at))
                    for q in range(2):
                        for name, m in (("V", gt), ("VT", gtT)):
                            if name == "V" and lv == LEVELS - 1:
                                continue
                            job = (name, t, lv, q)
                            dve.wait_ge(*psum.full(v.at, job))
                            bank = banks[psum.slot(v.at, job)]
                            if name == "V":
                                dve.wait_ge(*psum.full(v.at, ("VT", t, lv, q)))
                            mq = m[:, 4 * q:4 * q + 4, :]
                            tt(mq, mq, bank[:, :].rearrange("p (a i) -> p a i", a=4), ALU.subtract).then_inc(*psum.frees(v.at, job))
                            dve.wait_ge(*psum.vacated(v.at, job))
                if t:
                    tt(split8(gdec), pairs8(t), split8(spread8(e16[:, t, :])), ALU.mult).then_inc(dve_done, 1)
                    dve.wait_ge(dve_done, v.count())
                    tt(gdec, gdec, spread8(b16[:, t, :]), ALU.mult).then_inc(*g_in.event(v.at))
                    dve.wait_ge(*g_in.last(v.at))
                else:
                    g_out_wait = 6
                    dve.wait_ge(*g_out.nth(v.at, g_out_wait))
                    tt(split8(gdec), pairs8(t), split8(spread8(l16[:, t, :])), ALU.mult).then_inc(*g_in.event(v.at))
                    dve.wait_ge(*g_in.last(v.at))
                for q in range(2):
                    dve.wait_ge(*psum.full(v.at, ("vnew", t, q)))
                    bank = banks[psum.slot(v.at, ("vnew", t, q))]
                    V.tensor_copy(gvn[:, 4 * q:4 * q + 4, :],
                                                              bank[:, :].rearrange("p (a i) -> p a i", a=4)).then_inc(*psum.frees(v.at, ("vnew", t, q)))
                    dve.wait_ge(*psum.vacated(v.at, ("vnew", t, q)))
                dve.nop().then_inc(*g_in.event(v.at))
                for q in range(2):
                    cols = go[:, t, q * 512:(q + 1) * 512]
                    c4 = cols.rearrange("p (a i) -> p a i", a=4)
                    if t:
                        dve.wait_ge(*psum.full(v.at, ("oa", q)))
                        bank = banks[psum.slot(v.at, ("oa", q))]
                        tt(c4, bank[:, :].rearrange("p (a i) -> p a i", a=4),
                                                   e16[:, t, 4 * q:4 * q + 4].unsqueeze(2).to_broadcast([P, 4, P]), ALU.mult).then_inc(*psum.frees(v.at, ("oa", q)))
                        dve.wait_ge(*psum.vacated(v.at, ("oa", q)))
                        dve.wait_ge(*psum.full(v.at, ("ob", t, q)))
                        bank = banks[psum.slot(v.at, ("ob", t, q))]
                        tt(cols, cols, bank[:, :], ALU.add).then_inc(*psum.frees(v.at, ("ob", t, q)))
                        dve.wait_ge(*psum.vacated(v.at, ("ob", t, q)))
                    else:
                        dve.wait_ge(*psum.full(v.at, ("ob", t, q)))
                        bank = banks[psum.slot(v.at, ("ob", t, q))]
                        V.tensor_copy(cols, bank[:, :]).then_inc(*psum.frees(v.at, ("ob", t, q)))
                        dve.wait_ge(*psum.vacated(v.at, ("ob", t, q)))
                        dve.wait_ge(*psum.full(v.at, ("st", q)))
                        bank = banks[psum.slot(v.at, ("st", q))]
                        V.tensor_copy(gst[:, 4 * q:4 * q + 4, :],
                                                             bank[:, :].rearrange("p (a i) -> p a i", a=4)).then_inc(*psum.frees(v.at, ("st", q)))
                        dve.wait_ge(*psum.vacated(v.at, ("st", q)))
            for t in range(NT):
                tt(work[:, :], go[:, t, :], go[:, t, :], ALU.mult).then_inc(dve_done, 1)
                dve.wait_ge(dve_done, v.count())
                V.reduce_sum(tmp[:, 8 * t:8 * t + 8], work[:, :].rearrange("p (h f) -> p h f", h=GV), axis=AX).then_inc(dve_done, 1)
                dve.wait_ge(dve_done, v.count())
            ts(t16, t16, 1.0 / P, GDN_EPS, ALU.mult, ALU.add).then_inc(*var_ready.event(v.at))
            dve.wait_ge(*var_ready.last(v.at))
            state["std"] += 1
            dve.wait_ge(*std_ready.nth(v.at, state["std"]))
            V.reciprocal(t16, t16).then_inc(dve_done, 1)
            dve.wait_ge(dve_done, v.count())
            dve.wait_ge(*gate_done.nth(v.at, 1))
            for t in range(NT):
                o3 = go[:, t, :].rearrange("p (h f) -> p h f", h=GV)
                tt(o3, o3, t16[:, 8 * t:8 * t + 8].unsqueeze(2).to_broadcast([P, GV, P]), ALU.mult).then_inc(dve_done, 1)
                dve.wait_ge(dve_done, v.count())
                tt(o3, o3, nw.unsqueeze(1).to_broadcast([P, GV, P]), ALU.mult).then_inc(dve_done, 1)
                dve.wait_ge(dve_done, v.count())
                tt(go[:, t, :], go[:, t, :], gz[:, t, :], ALU.mult).then_inc(*y_ready.event(v.at))
                dve.wait_ge(*y_ready.last(v.at))
            residual(outs("gout"), None, ALPHA)
            layernorm("ln1")
            dve.nop().then_inc(*h_ready.event(v.at))
            dve.wait_ge(*rows.full(v.at, ("relb", 0)))
            r = R[:, rows.slot(v.at, ("relb", 0)), :]
            V.tensor_copy(relspread[0:BUCKETS, :, :], r[0:BUCKETS, 0:WQ_HEADS].unsqueeze(2)
                                       .to_broadcast([BUCKETS, WQ_HEADS, P])).then_inc(*g_in.event(v.at))
            dve.wait_ge(*g_in.last(v.at))
            dve.nop().then_inc(*rows.frees(v.at, ("relb", 0)))
            hidden(FF2 // P, hid2)
            dve.wait_ge(*rows.full(v.at, ("tmask", 0)))
            r = R[:, rows.slot(v.at, ("tmask", 0)), :]
            for h_ in range(WQ_HEADS):
                add_row(("rel", h_), r, relw[:, h_, :], width=384)
            dve.nop().then_inc(*bias_made.event(v.at))
            dve.nop().then_inc(*rows.frees(v.at, ("tmask", 0)))
            dve.nop().then_inc(*rows.frees(v.at, ("hot", 0)))
            residual(DOWN, None, ALPHA)
            layernorm("ln2")
            dve.nop().then_inc(*h_ready.event(v.at))
            for c in range(2):
                chunk_in("wq", c, lambda t: wq[:, t, c * 512:(c + 1) * 512])
            dve.wait_ge(*rows.full(v.at, ("wkv", 0)))
            r = R[:, rows.slot(v.at, ("wkv", 0)), :]
            for t in range(NT):
                add_row(("wkv", 0, t), r, wkv[:, t, :], width=256)
            dve.nop().then_inc(*rows.frees(v.at, ("wkv", 0)))
            for t in range(NT):
                i = V.tensor_copy(wkd[:, t, :].rearrange("p (g d f) -> p g d f", g=2, d=2),
                                  wkv[:, t, 0:128].rearrange("p (g f) -> p g f", g=2).unsqueeze(2)
                                  .to_broadcast([P, 2, 2, WD]))
                if t == 0:
                    i.then_inc(dve_done, 1)
                    dve.wait_ge(dve_done, v.count())
                else:
                    i.then_inc(*zB_ready.event(v.at))
                    dve.wait_ge(*zB_ready.last(v.at))
            dve.wait_ge(*rows.full(v.at, ("sink", 0)))
            sinks = R[:, rows.slot(v.at, ("sink", 0)), :]
            dve.wait_ge(bias_in, 16)

            def w_out(u):
                hp, t = divmod(u, NT)
                dve.wait_ge(*psum.full(v.at, ("Wo", hp, t)))
                bank = banks[psum.slot(v.at, ("Wo", hp, t))]
                tt(wo[:, t, hp * P:(hp + 1) * P].rearrange("p (m f) -> p m f", m=2),
                          bank[:, 0:P].rearrange("p (m f) -> p m f", m=2),
                          rinv[:, u % 3, :].unsqueeze(2).to_broadcast([P, 2, WD]), ALU.mult).then_inc(*psum.frees(v.at, ("Wo", hp, t)))
                dve.wait_ge(*psum.vacated(v.at, ("Wo", hp, t)))

            for u in range(16):
                hp, t = divmod(u, NT)
                b = u % 2
                mask("W", hp, t, u, 2, WD ** -0.5, lambda m, K: wbias[:, 2 * hp + m, 2 * P - K:2 * P])
                dve.wait_ge(*exped.nth(v.at, u + 1))
                tt(rsum[:, b, :], rsum[:, b, :], esink[:, b, :], ALU.add).then_inc(dve_done, 1)
                dve.wait_ge(dve_done, v.count())
                V.reciprocal(rinv[:, u % 3, :], rsum[:, b, :]).then_inc(*probs.event(v.at))
                dve.wait_ge(*probs.last(v.at))
                if u > 1:
                    w_out(u - 2)
            w_out(14)
            w_out(15)
            dve.nop().then_inc(*rows.frees(v.at, ("sink", 0)))
            dve.nop().then_inc(*y_ready.event(v.at))
            dve.nop().then_inc(*y_ready.event(v.at))
            residual(outs("wout"), None, ALPHA)
            layernorm("ln3")
            dve.nop().then_inc(*h_ready.event(v.at))
            lg = small[:, 60:76].rearrange("p (t e) -> p t e", t=NT)
            tm = tmp[:, 0:16].rearrange("p (t e) -> p t e", t=NT)
            for t in range(NT):
                dve.wait_ge(*psum.full(v.at, ("router", 0, t)))
                bank = banks[psum.slot(v.at, ("router", 0, t))]
                V.tensor_copy(lg[:, t, :], bank[:, 0:NE]).then_inc(*psum.frees(v.at, ("router", 0, t)))
                dve.wait_ge(*psum.vacated(v.at, ("router", 0, t)))
            V.reduce_max(nmax[:, 0, :], lg, axis=AX).then_inc(dve_done, 1)
            dve.wait_ge(dve_done, v.count())
            tt(tm, lg, nmax[:, 0, :].unsqueeze(2).to_broadcast([P, NT, NE]), ALU.subtract).then_inc(dve_done, 1)
            dve.wait_ge(dve_done, v.count())
            dve.nop().then_inc(*g_pre.event(v.at))
            dve.wait_ge(*g_act.nth(v.at, n_act + 1))
            for t in range(NT):
                other = lg[:, t, :].unsqueeze(1).to_broadcast([P, NE, NE])
                own = lg[:, t, :].unsqueeze(2).to_broadcast([P, NE, NE])
                gt_, eq = [work[:, i * 64:(i + 1) * 64].rearrange("p (a b) -> p a b", a=NE) for i in range(2)]
                tt(gt_, other, own, ALU.is_gt).then_inc(dve_done, 1)
                dve.wait_ge(dve_done, v.count())
                tt(eq, other, own, ALU.is_equal).then_inc(dve_done, 1)
                dve.wait_ge(dve_done, v.count())
                tt(eq, eq, below, ALU.mult).then_inc(dve_done, 1)
                dve.wait_ge(dve_done, v.count())
                tt(gt_, gt_, eq, ALU.add).then_inc(dve_done, 1)
                dve.wait_ge(dve_done, v.count())
                V.reduce_sum(gates[:, t, :], gt_, axis=AX).then_inc(dve_done, 1)
                dve.wait_ge(dve_done, v.count())
            ts(places, gates, 2.0, None, ALU.is_lt).then_inc(*route_in.event(v.at))
            dve.wait_ge(*route_in.last(v.at))
            tt(gates, places, tm, ALU.mult).then_inc(dve_done, 1)
            dve.wait_ge(dve_done, v.count())
            V.reduce_sum(nmax[:, 0, :], gates, axis=AX).then_inc(dve_done, 1)
            dve.wait_ge(dve_done, v.count())
            V.reciprocal(nmax[:, 0, :], nmax[:, 0, :]).then_inc(dve_done, 1)
            dve.wait_ge(dve_done, v.count())
            tt(gates, gates, nmax[:, 0, :].unsqueeze(2).to_broadcast([P, NT, NE]), ALU.mult).then_inc(dve_done, 1)
            dve.wait_ge(dve_done, v.count())
            counts = work[:, 0:3 * NE].rearrange("p (a e) -> p a e", a=3)
            dve.wait_ge(*psum.full(v.at, ("count", 0)))
            bank = banks[psum.slot(v.at, ("count", 0))]
            V.tensor_copy(work[:, 0:3 * NE], bank[:, 0:3 * NE]).then_inc(*psum.frees(v.at, ("count", 0)))
            dve.wait_ge(*psum.vacated(v.at, ("count", 0)))
            tt(places, places, counts[:, 0:NT, :], ALU.mult).then_inc(dve_done, 1)
            dve.wait_ge(dve_done, v.count())
            ts(places, places, -1.0, None, ALU.add).then_inc(dve_done, 1)
            dve.wait_ge(dve_done, v.count())
            more, number = work[:, 64:64 + NE], work[:, 72:72 + NE]
            hits = work[:, 128:128 + OVER * NE].rearrange("p (i e) -> p i e", i=OVER)
            listed = work[:, 200:201 + OVER]
            ts(more, counts[:, 2, :], P + 0.5, None, ALU.is_gt).then_inc(dve_done, 1)
            dve.wait_ge(dve_done, v.count())
            V.reduce_sum(listed[:, 0:1], more, axis=AX).then_inc(dve_done, 1)
            dve.wait_ge(dve_done, v.count())
            more_all = more.unsqueeze(1).to_broadcast([P, NE, NE])
            before = work[:, 256:256 + NE * NE].rearrange("p (a b) -> p a b", a=NE)
            tt(before, more_all, below, ALU.mult).then_inc(dve_done, 1)
            dve.wait_ge(dve_done, v.count())
            V.reduce_sum(number, before, axis=AX).then_inc(dve_done, 1)
            dve.wait_ge(dve_done, v.count())
            index = const("slots")
            tt(hits, number.unsqueeze(1).to_broadcast([P, OVER, NE]),
               index[:, 0:OVER].unsqueeze(2).to_broadcast([P, OVER, NE]), ALU.is_equal).then_inc(dve_done, 1)
            dve.wait_ge(dve_done, v.count())
            tt(hits, hits, more.unsqueeze(1).to_broadcast([P, OVER, NE]), ALU.mult).then_inc(dve_done, 1)
            dve.wait_ge(dve_done, v.count())
            tt(hits, hits, index[:, 0:NE].unsqueeze(1).to_broadcast([P, OVER, NE]), ALU.mult).then_inc(dve_done, 1)
            dve.wait_ge(dve_done, v.count())
            V.reduce_sum(listed[:, 1:1 + OVER], hits, axis=AX).then_inc(dve_done, 1)
            dve.wait_ge(dve_done, v.count())
            V.tensor_copy(plan[:, :], listed).then_inc(*plan_ready.event(v.at))
            dve.wait_ge(*plan_ready.last(v.at))
            V.tensor_copy(xin[:, :, :], x[:, :, :]).then_inc(dve_done, 1)
            dve.wait_ge(dve_done, v.count())
            ts(x[:, :, :], x[:, :, :], ALPHA, None, ALU.mult).then_inc(dve_done, 1)
            dve.wait_ge(dve_done, v.count())
            dve.nop().then_inc(dve_done, 1)
            dve.wait_ge(dve_done, v.count())
            dve.sem_clear(dve_done)

            def expert(e, block):
                slots = index[:, block * P:(block + 1) * P]
                V.tensor_copy(now, route[:, :, :, bass.ds(e, 1)].rearrange("p a t e -> p a (t e)")
                              ).then_inc(dve_done, 1)
                dve.wait_ge(dve_done, v.count())
                for t in range(NT):
                    i = ts(select[:, t, :], slots, now[:, 1, t:t + 1], None, ALU.is_equal)
                    if t < NT - 1:
                        i.then_inc(dve_done, 1)
                        dve.wait_ge(dve_done, v.count())
                    else:
                        i.then_inc(*select_ready.event(v.at))
                        dve.wait_ge(*select_ready.last(v.at))
                for t in range(NT):
                    i = ts(weigh[:, t, :], slots, now[:, 1, t:t + 1], now[:, 0, t:t + 1], ALU.is_equal, ALU.mult)
                    if t < NT - 1:
                        i.then_inc(dve_done, 1)
                        dve.wait_ge(dve_done, v.count())
                    else:
                        i.then_inc(*select_ready.event(v.at))
                        dve.wait_ge(*select_ready.last(v.at))
                for c in range(FFE // 256):
                    dve.wait_ge(*hid_act.nth(v.at, c + 1))
                    dve.wait_ge(*psum.full(v.at, ("up", c)))
                    bank = banks[psum.slot(v.at, ("up", c))]
                    tt(hid_tok[:, c % 2, :], acted[:, c % 2, :], bank[:, S:2 * S], ALU.mult
                       ).then_inc(*psum.frees(v.at, ("up", c)))
                    dve.wait_ge(*psum.vacated(v.at, ("up", c)))
                    dve.nop().then_inc(*hid_ready.event(v.at))
                for half in range(2):
                    for t in range(NT):
                        dve.wait_ge(*psum.full(v.at, ("back", t, half)))
                        bank = banks[psum.slot(v.at, ("back", t, half))]
                        dst = x[:, t, half * 512:(half + 1) * 512]
                        tt(dst, dst, bank[:, :], ALU.add).then_inc(*psum.frees(v.at, ("back", t, half)))
                        dve.wait_ge(*psum.vacated(v.at, ("back", t, half)))
                dve.nop().then_inc(dve_done, 1)
                dve.wait_ge(dve_done, v.count())
                dve.sem_clear(dve_done)

            with dve.Fori(0, NE) as e:
                v.enter("expert", e)
                expert(e, 0)
            n_over = dve.value_load(plan[0:1, 0:1], min_val=0, max_val=OVER)
            with dve.If(n_over):
                with dve.Fori(0, n_over) as i:
                    e = dve.value_load(plan[0:1, bass.ds(1 + i, 1)], min_val=0, max_val=NE - 1)
                    v.enter("over", i)
                    expert(e, 1)
            v.enter("end")
            state["std"] = 0
            layernorm("ln4")
            dve.nop().then_inc(*h_ready.event(v.at))

        jobs = {p: len(n) for p, n in psum.order.items()}
        given = {s.name: s.seen for s in signals}
        return jobs, given


def _columns(w, width=512):
    K, N = w.shape
    return [w[:, c:c + width].reshape(K // P, P, -1).transpose(1, 0, 2).reshape(P, -1)
            for c in range(0, N, width)]


def _pairs(a, b):
    F = a.shape[1]
    both = np.stack([a.reshape(KD, P, F // 256, 256), b.reshape(KD, P, F // 256, 256)], 3)
    return list(both.transpose(2, 1, 0, 3, 4).reshape(F // 256, P, 4096))


def _down(w):
    t = w.reshape(-1, P, D)
    return [t[c:c + 4].transpose(1, 0, 2).reshape(P, -1) for c in range(0, len(t), 4)]


def _pack(slots, width=4096):
    out = np.zeros((len(slots), P, width), np.float32)
    for i, s in enumerate(slots):
        out[i, :, :s.shape[1]] = s
    return out


def _row(*parts):
    r = np.zeros(512, np.float32)
    at = 0
    for p in parts:
        p = np.asarray(p).reshape(-1)
        r[at:at + len(p)] = p
        at += len(p)
    return r


def pack(i):
    arrays = {"constants": constants(), "x": i["x"].reshape(S, D),
              "c_columns": np.ascontiguousarray(i["c"].reshape(KD, P).T)}
    w, r, c = [], [], []
    for l in range(DEPTH):
        w_in, b_in = i["w_in"][l], i["b_in"][l]
        bf = 3072
        cuts = [(0, 1536), (1536, 3072), (bf, bf + 4), (bf + 4, bf + 3076), (bf + 3076, bf + 6148)]
        slots = _columns(i["w_ada"][l])
        bias = [_row(b) for b in i["b_ada"][l].reshape(12, 512)]
        init = 0.8 - 0.6 * math.exp(-0.3 * l)
        bias.append(_row(i["lam_q1"][l], i["lam_k1"][l], i["lam_q2"][l], i["lam_k2"][l],
                         np.array([init, 1.0 - init], np.float32)))
        for a, b in cuts:
            slots += _columns(w_in[:, a:b])
            bias += [_row(b_in[n:min(n + 512, b)]) for n in range(a, b, 512)]
        for name in ("w_pa", "w_pb", "w_pc", "w_out"):
            slots += _columns(i[name][l])
        slots += _pairs(i["w_up"][l][:, :FF1], i["w_up"][l][:, FF1:]) + _down(i["w_down"][l])
        bias += [_row(i["g_diff"][l])] + [_row(g) for g in i["g_ret"][l].reshape(2, 512)]

        def ln(g, b):
            return [_row(g[:512]), _row(b[:512]), _row(g[512:]), _row(b[512:])]

        bias += ln(i["ln_g"][l, 0], i["ln_b"][l, 0]) + [_row()] + ln(i["ln_g"][l, 1], i["ln_b"][l, 1])
        taps = np.zeros((P, 512), np.float32)
        nf = FF1 // P
        for n, a in enumerate([*i["w_conv"][l], i["b_conv"][l]]):
            taps[:, n * nf:(n + 1) * nf] = a.reshape(nf, P).T
        w.append(_pack(slots))
        r.append(np.stack(bias))
        c.append(taps[None])
    arrays["w_layer"], arrays["rows_layer"], arrays["cols_layer"] = np.stack(w), np.stack(r), np.stack(c)

    g = i["a_w_in_2"][0]
    slots = _columns(g[:, :2048]) + _columns(g[:, 2048:3072]) + _columns(g[:, 3072:])
    slots += _columns(i["a_w_out_2"][0])
    slots += _pairs(i["ffn_w_gate_2"][0], i["ffn_w_up_2"][0]) + _down(i["ffn_w_down_2"][0])
    slots += _columns(i["b_w_in_2"][0][:, :1024]) + _columns(i["b_w_in_2"][0][:, 1024:])
    slots += _columns(i["b_w_out_2"][0]) + _columns(i["moe_router_2"][0])
    arrays["w_middle"] = _pack(slots)
    hot, mask = bias_tables()
    lng, lnb = i["ln_g_2"], i["ln_b_2"]
    bias = [_row(), _row(i["a_a_log_2"][0], i["a_dt_bias_2"][0], i["a_norm_w_2"][0])]
    bias += ln(lng[0, 0], lnb[0, 0]) + [_row(), _row(), mask] + ln(lng[0, 1], lnb[0, 1])
    b = i["b_b_in_2"][0]
    bias += [_row(b[:512]), _row(b[512:1024]), _row(b[1024:]), _row(i["b_sinks_2"][0])]
    bias += ln(lng[1, 0], lnb[1, 0])
    arrays["rows_middle"] = np.stack(bias)
    gconv = np.zeros((P, 512), np.float32)
    for n in range(GDN_TAPS):
        gconv[:, 16 * n:16 * n + 16] = i["a_conv_w_2"][0][n].reshape(16, P).T
    relb = np.zeros((P, 512), np.float32)
    relb[:BUCKETS, :WQ_HEADS] = i["rel_bias_2"]
    arrays["cols_middle"] = np.stack([gconv, relb, hot])
    arrays["rows_end"] = np.stack(ln(lng[1, 1], lnb[1, 1]))
    e = np.empty((NE, len(W_LOADS["expert"]), P, 4096), np.float32)
    for n in range(NE):
        for k, s in enumerate(_pairs(i["moe_w_gate_2"][0, n], i["moe_w_up_2"][0, n])
                              + _down(i["moe_w_down_2"][0, n])):
            e[n, k] = s
    arrays["w_expert"] = e
    return arrays


def kernel(**inputs):
    import concourse.bacc as bacc
    from concourse.bass_utils import run_bass_kernel_spmd

    arrays = pack({k: np.asarray(a) for k, a in inputs.items()})
    nc = bacc.Bacc("TRN2", target_bir_lowering=False, num_devices=1)
    ins = {n: nc.dram_tensor("in_" + n, a.shape, F32, kind="ExternalInput").ap() for n, a in arrays.items()}
    out = nc.dram_tensor("out_x", (S, D), F32, kind="ExternalOutput").ap()
    program(nc, ins, out)
    r = run_bass_kernel_spmd(nc, [{"in_" + n: a for n, a in arrays.items()}], core_ids=[0])
    return r.results[0]["out_x"].reshape(1, S, D)
```

```python
from contextlib import ExitStack
import math

import numpy as np
import concourse.bass as bass
from concourse import mybir

ALU = mybir.AluOpType
ACT = mybir.ActivationFunctionType
F32 = mybir.dt.float32
F32R = mybir.dt.float32r
AX = mybir.AxisListType.X

P = 128
S = 256
NT = S // P
D = 1024
KD = D // P
DEPTH = 2
ALPHA = (2 * DEPTH) ** 0.25
EPS = 1e-5
CHUNK = 64
A_HEADS, A_DQK = 4, 64
B_HEADS, B_DH = 4, 128
C_HEADS, C_DK, C_DV = 4, 128, 256
FF1 = 2816
GK, GV, GD = 4, 8, 128
GDN_EPS = 1e-6
GDN_TAPS = 4
LEVELS = 7
WQ_HEADS, WKV_HEADS, WD = 16, 2, 64
WINDOW = 128
BUCKETS, MAX_DIST = 32, 128
FF2 = 2816
NE = 8
FFE = 3584
NEG = -1.0e30

PASSES = (("start", 1), ("layer", DEPTH), ("middle", 1), ("expert", NE), ("over", None), ("end", 1))
OVER = 2 * S // (P + 1)

def _halves(kind, n, halves=2):
    return [(kind, c, i) for c in range(n) for i in range(halves)]


def _layer_loads():
    loads = _halves("ada", 4)
    for n in range(6):
        kind, c = ("A", n) if n < 3 else ("B", n - 3)
        loads += [(kind, c, 0), ("ada", 4 + n, 0), (kind, c, 1), ("ada", 4 + n, 1)]
    loads += [("bf", 0, 0)] + _halves("C", 6) + _halves("gate", 6)
    loads += _halves("pa", 2, 1) + _halves("pb", 2, 1) + _halves("pc", 2) + _halves("out", 2)
    loads += _halves("up", FF1 // P, 1)
    for c in range(FF1 // 256):
        loads += [("down", c, 0)]
        if c < 2:
            loads += [("ada", 10 + c, i) for i in range(2)]
    return loads


W_LOADS = {
    "start": [],
    "layer": _layer_loads(),
    "middle": _halves("qkv", 8, 1) + _halves("z", 2) + [("ba", 0, 0)] + _halves("gout", 2)
    + _halves("up", FF2 // P, 1) + _halves("down", FF2 // 256, 1)
    + _halves("wq", 2) + [("wkv", 0, 0)] + _halves("wout", 2) + [("router", 0, 0)],
    "expert": _halves("up", FFE // 256) + _halves("down", FFE // 256, 1),
    "end": [],
}
W_LOADS["over"] = W_LOADS["expert"]
ADA_LOADS = {part: [w for w in loads if w[0] == "ada" and w[1] > 3] for part, loads in W_LOADS.items()}
EXPERT_LOADS = {part: loads if part in ("expert", "over") else [] for part, loads in W_LOADS.items()}
RING_LOADS = {part: [w for w in loads if not EXPERT_LOADS[part] and (w[0] != "ada" or w[1] < 4)]
              for part, loads in W_LOADS.items()}
SPLIT = {part: [w for w in loads if w[0] != "ada"] for part, loads in W_LOADS.items()}
for _part in ("expert", "over"):
    SPLIT[_part] = [w for w in W_LOADS[_part]
                    if (w[0] == "up" and w[1] % 2 + w[2] > 0) or (w[0] == "down" and w[1] % 4)]

LN_ROWS = ["g0", "b0", "g1", "b1"]
R_LOADS = {
    "start": [],
    "layer": [("adac", 0), ("lam", 0)] + [("A", 0), ("ada", 4), ("A", 1), ("ada", 5), ("A", 2)]
    + [("B", c) for c in range(3)] + [("bf", 0)] + [("C", c) for c in range(6)] + [("gdiff", 0)]
    + [("gate", c) for c in range(6)] + [("gret", 0), ("gret", 1)]
    + [("ln1", r) for r in LN_ROWS] + [("conv", 0)]
    + [("ada", 10), ("ada", 11)] + [("ln2", r) for r in LN_ROWS],
    "middle": [("gconv", 0), ("gpar", 0)] + [("ln1", r) for r in LN_ROWS]
    + [("relb", 0), ("hot", 0), ("tmask", 0)] + [("ln2", r) for r in LN_ROWS]
    + [("wq", c) for c in range(2)] + [("wkv", 0), ("sink", 0)] + [("ln3", r) for r in LN_ROWS],
    "expert": [], "over": [],
    "end": [("ln4", r) for r in LN_ROWS],
}
PER_PARTITION = {"adac", "conv", "gconv", "relb", "hot"}
HALF = 2048
W_WIDTH = {"bf": 32, "ba": 128, "router": 64}
W_SLOTS, E_SLOTS, R_SLOTS, BANKS = 4, 7, 4, 8
ARENA = 22544
JOBS = {'start': 0, 'layer': 196, 'middle': 290, 'expert': 37, 'over': 37, 'end': 0}
GIVEN = {
    'low_ready': {'layer': 164, 'middle': 120, 'expert': 62, 'over': 62},
    'group_high': {'layer': 20, 'middle': 26, 'expert': 12, 'over': 12},
    'group_split': {'layer': 20, 'middle': 24},
    'ada_ready': {'layer': 12},
    'mod_ready': {'layer': 2},
    'c_silu': {'start': 1},
    'h_ready': {'layer': 6, 'middle': 7, 'end': 2},
    'zA_ready': {'layer': 6},
    'zB_ready': {'layer': 6, 'middle': 1},
    'zC_ready': {'layer': 2},
    'qkT_ready': {'layer': 12, 'middle': 6},
    'lam_dots': {'layer': 1},
    'lam_exps': {'layer': 1},
    'forget_pre': {'layer': 2},
    'forget_exp': {'layer': 1},
    'forget_ln': {'layer': 1},
    'forget_ready': {'layer': 1},
    'masked': {'layer': 16, 'middle': 16},
    'exped': {'layer': 16, 'middle': 16},
    'probs': {'layer': 16, 'middle': 16},
    'probsT_ready': {'layer': 16, 'middle': 16},
    'retained': {'layer': 8},
    'gate_pre': {'layer': 4, 'middle': 1},
    'gate_done': {'layer': 4, 'middle': 1},
    'var_ready': {'layer': 4, 'middle': 4, 'end': 1},
    'std_ready': {'layer': 4, 'middle': 4, 'end': 1},
    'y_ready': {'layer': 6, 'middle': 4},
    'hid_pre': {'layer': 22},
    'hid_act': {'layer': 22, 'middle': 22, 'expert': 14, 'over': 14},
    'hid_ready': {'layer': 22, 'middle': 22, 'expert': 14, 'over': 14},
    'g_pre': {'middle': 15},
    'g_act': {'middle': 23},
    'g_in': {'middle': 25},
    'g_out': {'middle': 36},
    'bias_made': {'middle': 1},
    'route_in': {'middle': 1},
    'plan_ready': {'middle': 1},
    'chosen_split': {'middle': 2, 'expert': 2, 'over': 2},
    'down_split': {'expert': 10, 'over': 10},
    'weigh_ready': {'expert': 1, 'over': 1},
    'weighT_ready': {'expert': 1, 'over': 1},
    'out_ready': {'expert': 2, 'over': 2},
    'select_ready': {'middle': 1, 'expert': 1, 'over': 1},
    'chosen_ready': {'middle': 1, 'expert': 1, 'over': 1},
    'down_ready': {'expert': 4, 'over': 4},
}

CONST = {}
for _name, _width in (("ident", P), ("ones", P), ("steps", 3 * P), ("causal", 2 * P),
                      ("blocks", 2 * P), ("strict", P), ("levels", LEVELS * P),
                      ("decay", C_HEADS * S), ("cos", NT * 64), ("sin", NT * 64), ("below", NE * NE),
                      ("slots", 2 * P)):
    CONST[_name] = (sum(w for _, w in CONST.values()), _width)
N_CONST = sum(w for _, w in CONST.values())


def constants():
    j = np.arange(P)[:, None]
    i = np.arange(P)[None, :]
    t = {}
    t["ident"] = np.eye(P)
    t["ones"] = np.ones((P, P))
    upto = (j <= i).astype(np.float64)
    t["steps"] = np.concatenate([np.zeros((P, P)), upto, np.ones((P, P))], 1)
    t["causal"] = np.concatenate([np.zeros((P, P)), np.where(i <= j, 0.0, NEG)], 1)
    t["blocks"] = np.concatenate([np.zeros((P, P)), np.where(i // CHUNK <= j // CHUNK, 0.0, NEG)], 1)
    t["strict"] = (i < j).astype(np.float64)
    t["levels"] = np.concatenate(
        [((i >> n) % 2 == 1) & ((i >> n) - 1 == (j >> n)) for n in range(LEVELS)], 1)
    gamma = 1.0 - 2.0 ** (-5.0 - np.arange(C_HEADS))
    far = np.arange(S)[None, :] - j
    t["decay"] = np.concatenate(
        [np.where(far >= 0, g ** np.maximum(far, 0), 0.0) * C_DK ** -0.5 for g in gamma], 1)
    half = C_DK // 2
    inv = (1.0 / (10000.0 ** np.linspace(0.0, 1.0, half, dtype=np.float32))).astype(np.float32)
    ang = (np.arange(S, dtype=np.float32)[:, None] * inv[None, :]).astype(np.float32).astype(np.float64)
    for name, f in (("cos", np.cos), ("sin", np.sin)):
        t[name] = f(ang).reshape(NT, P, half).transpose(1, 0, 2).reshape(P, NT * half)
    e = np.arange(NE)
    t["below"] = np.broadcast_to((e[None, :] < e[:, None]).reshape(1, NE * NE), (P, NE * NE))
    t["slots"] = np.broadcast_to(np.arange(2 * P)[None, :], (P, 2 * P))
    return np.ascontiguousarray(np.concatenate([t[n] for n in CONST], 1).astype(np.float32))


def bias_tables():
    dist = 255 - np.arange(384)
    d = np.clip(dist, 0, None)
    exact = BUCKETS // 2
    df = np.maximum(d, 1).astype(np.float32)
    large = exact + (np.log(df / np.float32(exact)) / np.float32(math.log(MAX_DIST / exact))
                     * np.float32(BUCKETS - exact)).astype(np.int32)
    bucket = np.where(d < exact, d, np.minimum(large, BUCKETS - 1))
    ok = (dist >= 0) & (dist < WINDOW)
    hot = np.zeros((P, 512), np.float32)
    hot[:BUCKETS, :384] = (np.arange(BUCKETS)[:, None] == bucket[None, :]) & ok[None, :]
    mask = np.zeros(512, np.float32)
    mask[:384] = np.where(ok, 0.0, NEG)
    return hot, mask


class Pass:

    def __init__(self, part, turn=None):
        self.part, self.turn = part, turn

    def value(self, per, k):
        for part, times in PASSES:
            if part == self.part:
                break
            assert times is not None or not per.get(part, 0)
            k += (times or 0) * per.get(part, 0)
        step = per.get(self.part, 0)
        return k if self.turn is None or step == 0 else self.turn * step + k


class Signal:

    def __init__(self, sem, name):
        self.sem, self.name, self.per, self.seen = sem, name, GIVEN.get(name, {}), {}

    def event(self, at):
        self.seen[at.part] = self.seen.get(at.part, 0) + 1
        return self.sem, 1

    def nth(self, at, k):
        return self.sem, at.value(self.per, k)

    def last(self, at):
        return self.nth(at, self.seen[at.part])


class Ring:

    def __init__(self, n, filled, freed, unit, order, count):
        self.n, self.filled, self.freed, self.unit = n, filled, freed, unit
        self.order, self.count = order, count

    def place(self, at, name):
        i = self.order[at.part].index(name)
        slot = i % self.n
        per = {p: (c + self.n - 1 - slot) // self.n for p, c in self.count.items()}
        return slot, i // self.n, per

    def slot(self, at, name):
        return self.place(at, name)[0]

    def vacant(self, at, name):
        slot, before, per = self.place(at, name)
        return self.freed[slot], at.value(per, before + 1)

    def fills(self, at, name):
        return self.filled[self.slot(at, name)], self.unit

    def full(self, at, name):
        slot, before, per = self.place(at, name)
        v = at.value(per, before + 1)
        return self.filled[slot], v * self.unit

    def part(self, at, name, k):
        sem, v = self.full(at, name)
        return sem, v - (self.unit - k) if k < self.unit else v

    def frees(self, at, name):
        return self.freed[self.slot(at, name)], 1

    def vacated(self, at, name):
        slot, before, per = self.place(at, name)
        return self.freed[slot], at.value(per, before + 2)


class Banks(Ring):

    def vacant(self, at, name):
        self.order[at.part].append(name)
        return super().vacant(at, name)


class Steps:

    def __init__(self):
        self.n, self.at = 0, None

    def count(self):
        self.n += 1
        return self.n

    def enter(self, part, turn=None):
        self.at, self.n = Pass(part, turn), 0


def program(nc, ins, out):
    ctx = ExitStack()
    with ctx:
        def sb(name, shape):
            return ctx.enter_context(nc.sbuf_tensor(name, shape, F32))

        def sem(name):
            return ctx.enter_context(nc.semaphore(name))

        def sig(name):
            s = Signal(sem(name), name)
            signals.append(s)
            return s

        signals = []
        def base():
            return (nc.sbuf_base + 31) // 32 * 32

        def parts(name, shape, offset):
            return nc.alloc_sbuf_tensor_at(name, shape, F32R, offset=offset)

        at_W = base()
        W = sb("W", [P, W_SLOTS, HALF])
        W_low = parts("W_low", [P, W_SLOTS, HALF], at_W)
        W_high = ctx.enter_context(nc.sbuf_tensor("W_high", [P, 2, HALF], F32R))
        R = sb("R", [P, R_SLOTS, 512])
        x = sb("x", [P, NT, D])
        h = sb("h", [P, NT, D])
        hT_high = ctx.enter_context(nc.sbuf_tensor("hT_high", [P, KD, S], F32R))
        at_hT = base()
        hT = sb("hT", [P, KD, S])
        hT_low = parts("hT_low", [P, KD, S], at_hT)
        consts = sb("consts", [P, N_CONST])
        at_arena = base()
        arena = sb("arena", [P, ARENA])
        arena_parts = parts("arena_parts", [P, ARENA], at_arena)
        scores = sb("scores", [P, 2, 2, S])
        probsT = sb("probsT", [P, 2, 4, P])
        work = sb("work", [P, 1024])
        acted = sb("acted", [P, 2, S])
        small = sb("small", [P, 256])
        modc = sb("modc", [P, 32])
        banks = [ctx.enter_context(nc.psum_tensor(f"bank{i}", [P, 512], F32)) for i in range(BANKS)]
        spread = nc.dram_tensor("spread", (WQ_HEADS, P, 384), F32, kind="Internal").ap()

        def const(name):
            a, w = CONST[name]
            return consts[:, a:a + w]

        def view(at, *dims, of=None):
            n = int(np.prod(dims))
            v = (arena if of is None else of)[:, at:at + n]
            if len(dims) == 1:
                return v
            names = "abc"[:len(dims)]
            return v.rearrange("p (" + " ".join(names) + ") -> p " + " ".join(names),
                               **dict(zip(names, dims)))

        def both(high, low, *dims):
            return view(high, *dims, of=arena_parts), view(low, *dims, of=arena_parts)

        ident, ones = const("ident"), const("ones")
        steps, causal, blocks = const("steps"), const("causal"), const("blocks")
        upto = steps[:, P:2 * P]
        levels = const("levels").rearrange("p (n i) -> p n i", n=LEVELS)
        decay = const("decay").rearrange("p (h i) -> p h i", h=C_HEADS)
        cos = const("cos").rearrange("p (t f) -> p t f", t=NT)
        sin = const("sin").rearrange("p (t f) -> p t f", t=NT)
        below = const("below").rearrange("p (a b) -> p a b", a=NE)

        mod = view(0, 4, 512)
        forget = view(2048, NT, B_HEADS, S)
        zA = view(4096, NT, 1536)
        zB = view(7168, NT, 1544)
        zCqk = view(10256, NT, 1024)
        zCv = view(12304, NT, 1024)
        zCg = view(14352, NT, 1024)
        aT = view(16400, 8, S)
        bT = view(18448, 8, S)
        cT = view(20496, 8, S)
        forget_neg = view(20496, NT, B_HEADS, P)
        gA, gB, gC = h, view(16400, NT, 1024), zA[:, :, 512:1536]
        yA, yB, yC = zA[:, :, 0:512], zB[:, :, 0:512], zCqk
        ada_slots = view(18448, 2, HALF)
        hTs = hT_high, hT_low
        yATs = hT_high[:, 0:4, :], hT_low[:, 0:4, :]
        yBTs = hT_high[:, 4:8, :], hT_low[:, 4:8, :]
        yCTs = both(18448, 20496, KD, S)
        mix, mixTs = zCv, both(14352, 2048, KD, S)
        hid1 = both(4096, 9728, FF1 // P, S)
        gT = view(0, 16, S)
        gq, gk = gT[:, 0:4, :], gT[:, 4:8, :]
        gz = view(4096, NT, 1024)
        gvb = view(6144, NT, GV, P)
        gkn = view(8192, NT, GK, P)
        go = view(9216, NT, 1024)
        gsq = view(11264, 8, S)
        g9 = [view(11264 + 1024 * n, GV, P) for n in range(9)]
        gdec, gaT, gbT, gt, gtT, gu, gaq, gvn, gst = g9
        gplus, gminus, gpair = gbT, gu, gt
        goTs = both(0, 2048, KD, S)
        hid2 = both(0, 15872, FF2 // P, S)
        relw = view(5632, WQ_HEADS, 384)
        wbias = view(11776, WQ_HEADS, S)
        relspread = h[:, :, :].rearrange("p t (a i) -> p (t a) i", i=P)
        wq = view(0, NT, 1024)
        wkv = view(2048, NT, 256)
        wkd = view(2560, NT, 256)
        wqT = view(3072, 8, S)
        wkT = view(5120, 2, S)
        wo = view(15872, NT, 1024)
        woTs = both(0, 3072, KD, S)
        hidT = view(0, 8, P)
        chosenT = view(3584, KD, P)
        chosen_out = view(4608, NT, 512)
        select = view(5632, NT, P, of=arena_parts)
        weigh = view(5888, NT, P)
        weighT = view(6144, NT, P)
        hid_tok = view(6400, 2, S)
        hidTs = both(7168, 10752, FFE // P, P)
        chosenTs = both(14336, 15360, KD, P)
        xins = [m[:, :, :].rearrange("p (t a) s -> p t (a s)", t=NT) for m in (hT_high, hT_low)]

        nmax = small[:, 0:4].rearrange("p (b m) -> p b m", b=2)
        rsum = small[:, 4:8].rearrange("p (b m) -> p b m", b=2)
        lam = small[:, 8:12]
        stats = small[:, 12:36].rearrange("p (a s) -> p a s", a=4)
        meanvar = small[:, 36:52].rearrange("p (a s) -> p a s", a=8)
        inv = small[:, 52:60]
        logf = small[:, 60:76]
        beta = small[:, 76:92]
        decays = small[:, 92:108]
        cums = small[:, 108:140]
        egc = small[:, 140:156]
        egl = small[:, 156:172]
        tmp = small[:, 172:204]
        esink = small[:, 204:208].rearrange("p (b m) -> p b m", b=2)
        route = sb("route", [P, 2, NT, NE + 1])
        gates, places = route[:, 0, :, 0:NE], route[:, 1, :, 0:NE]
        now = small[:, 208:212].rearrange("p (a t) -> p a t", a=2)
        coming = small[:, 212:214]
        plan = ctx.enter_context(nc.sbuf_tensor("plan", [P, 1 + OVER], mybir.dt.int32))
        csil = small[:, 226:234]
        rinv = small[:, 234:240].rearrange("p (b m) -> p b m", b=3)
        invs = tmp[:, 0:8]
        nw = acted[:, 0, 0:P]

        weights = Ring(W_SLOTS, [sem(f"weights_in{i}") for i in range(W_SLOTS)],
                       [sem(f"weights_freed{i}") for i in range(W_SLOTS)], 16, RING_LOADS,
                       {p: len(n) for p, n in RING_LOADS.items()})
        expert_weights = Ring(E_SLOTS, [sem(f"expert_in{i}") for i in range(E_SLOTS)],
                              [sem(f"expert_freed{i}") for i in range(E_SLOTS)], 16, EXPERT_LOADS,
                              {p: len(n) for p, n in EXPERT_LOADS.items()})

        def ring(at):
            return expert_weights if at.part in ("expert", "over") else weights

        expert_split = {p: n if EXPERT_LOADS[p] else [] for p, n in SPLIT.items()}
        expert_highs = Ring(3, [sem(f"expert_high_ready{i}") for i in range(3)],
                            [sem(f"expert_high_used{i}") for i in range(3)], 2, expert_split,
                            {p: len(n) for p, n in expert_split.items()})

        def highs(at):
            return expert_highs if at.part in ("expert", "over") else main_highs

        def high_slot(at, w):
            slot = highs(at).slot(at, w)
            return W_high[:, slot, :] if slot < 2 else view(1024, HALF, of=arena_parts)

        def raw(at, w):
            slot = ring(at).slot(at, w)
            return W[:, slot, :] if slot < W_SLOTS else view(16384 + (slot - W_SLOTS) * HALF, HALF)

        def lows(at, w):
            slot = ring(at).slot(at, w)
            if slot < W_SLOTS:
                return W_low[:, slot, :]
            return view(16384 + (slot - W_SLOTS) * HALF, HALF, of=arena_parts)

        adas = Ring(2, [sem(f"ada_in{i}") for i in range(2)], [sem(f"ada_used{i}") for i in range(2)], 16,
                    ADA_LOADS, {p: len(n) for p, n in ADA_LOADS.items()})
        main_split = {p: [] if EXPERT_LOADS[p] else n for p, n in SPLIT.items()}
        main_highs = Ring(2, [sem(f"high_ready{i}") for i in range(2)],
                          [sem(f"high_used{i}") for i in range(2)], 2, main_split,
                          {p: len(n) for p, n in main_split.items()})
        rows = Ring(R_SLOTS, [sem(f"rows_in{i}") for i in range(R_SLOTS)],
                    [sem(f"rows_freed{i}") for i in range(R_SLOTS)], 16, R_LOADS,
                    {p: len(n) for p, n in R_LOADS.items()})
        psum = Banks(BANKS, [sem(f"product_done{i}") for i in range(BANKS)],
                    [sem(f"bank_freed{i}") for i in range(BANKS)], 1, {p: [] for p, _ in PASSES}, JOBS)
        consts_in, x_in, c_in = sem("consts_in"), sem("x_in"), sem("c_in")
        out_written, bias_out, bias_in = sem("out_written"), sem("bias_out"), sem("bias_in")
        pe_step, act_done, dve_done = sem("pe_step"), sem("act_done"), sem("dve_done")

        low_ready = sig("low_ready")
        group_high = sig("group_high")
        group_split = sig("group_split")
        ada_ready = sig("ada_ready")
        mod_ready = sig("mod_ready")
        c_silu = sig("c_silu")
        h_ready = sig("h_ready")
        hT_ready = sig("hT_ready")
        zA_ready, zB_ready, zC_ready = sig("zA_ready"), sig("zB_ready"), sig("zC_ready")
        qkT_ready = sig("qkT_ready")
        lam_dots, lam_exps = sig("lam_dots"), sig("lam_exps")
        forget_pre, forget_exp, forget_ln = sig("forget_pre"), sig("forget_exp"), sig("forget_ln")
        forget_ready = sig("forget_ready")
        masked = sig("masked")
        exped = sig("exped")
        probs = sig("probs")
        probsT_ready = sig("probsT_ready")
        retained = sig("retained")
        y_done = sig("y_done")
        gate_pre, gate_done = sig("gate_pre"), sig("gate_done")
        var_ready, std_ready = sig("var_ready"), sig("std_ready")
        y_ready = sig("y_ready")
        yT_ready = sig("yT_ready")
        hid_pre, hid_act, hid_ready = sig("hid_pre"), sig("hid_act"), sig("hid_ready")
        g_pre, g_act = sig("g_pre"), sig("g_act")
        g_in = sig("g_in")
        g_out = sig("g_out")
        bias_made = sig("bias_made")
        route_in, plan_ready = sig("route_in"), sig("plan_ready")
        chosen_split, down_split = sig("chosen_split"), sig("down_split")
        weigh_ready = sig("weigh_ready")
        weighT_ready = sig("weighT_ready")
        out_ready = sig("out_ready")
        select_ready, chosen_ready, down_ready = sig("select_ready"), sig("chosen_ready"), sig("down_ready")

        block = ctx.enter_context(nc.Block())

        @block.sync
        def _(sp):
            def load_weight(at, name, src):
                sp.wait_ge(*ring(at).vacant(at, name))
                n = W_WIDTH.get(name[0], HALF)
                sp.dma_start(raw(at, name)[:, 0:n], src[:, 0:n]).then_inc(*ring(at).fills(at, name))

            def load_row(at, name, src):
                sp.wait_ge(*rows.vacant(at, name))
                slot = rows.slot(at, name)
                sp.dma_start(R[:, slot, :], src).then_inc(*rows.fills(at, name))

            def row_source(at, name, turn):
                n = R_LOADS[at.part].index(name)
                if name[0] in PER_PARTITION:
                    src = ins["cols_" + at.part]
                    n = [r for r in R_LOADS[at.part] if r[0] in PER_PARTITION].index(name)
                    return src[turn, n] if turn is not None else src[n]
                src = ins["rows_" + at.part]
                src = src[turn, n:n + 1, :] if turn is not None else src[n:n + 1, :]
                return src.to_broadcast([P, 512])

            def stream(at, turn, after):
                src = ins["w_" + at.part]
                done = []

                def row(name):
                    load_row(at, name, row_source(at, name, turn))
                    done.append(name)

                for n, name in enumerate(W_LOADS[at.part]):
                    if name not in ADA_LOADS[at.part]:
                        load_weight(at, name, src[turn, n] if turn is not None else src[n])
                    if name[:2] in R_LOADS[at.part] and name[:2] + (1 - name[2],) not in W_LOADS[at.part][n:]:
                        row(name[:2])
                    for r in after.get(name, []):
                        row(r)
                assert done == R_LOADS[at.part], (done, R_LOADS[at.part])

            sp.dma_start(consts[:, :], ins["constants"]).then_inc(consts_in, 16)
            sp.dma_start(csil, ins["c_columns"]).then_inc(c_in, 16)
            sp.dma_start(x[:, :, :], ins["x"].rearrange("(t p) d -> p t d", p=P)).then_inc(x_in, 16)
            with sp.Fori(0, DEPTH) as l:
                at = Pass("layer", l)
                stream(at, l, {("ada", 0, 1): [("adac", 0), ("lam", 0)],
                               ("C", 5, 1): [("gdiff", 0)],
                               ("gate", 5, 1): [("gret", 0), ("gret", 1)],
                               ("out", 1, 1): [("ln1", r) for r in LN_ROWS],
                               ("up", 1, 0): [("conv", 0)],
                               ("down", 10, 0): [("ln2", r) for r in LN_ROWS]})
            at = Pass("middle")
            src = W_LOADS["middle"]
            after = {("qkv", 0, 0): [("gconv", 0), ("gpar", 0)],
                     ("gout", 1, 1): [("ln1", r) for r in LN_ROWS],
                     ("up", 1, 0): [("relb", 0), ("hot", 0), ("tmask", 0)],
                     ("down", 10, 0): [("ln2", r) for r in LN_ROWS],
                     ("wkv", 0, 0): [("sink", 0)],
                     ("wout", 1, 1): [("ln3", r) for r in LN_ROWS]}
            stream(at, None, after)
            sp.wait_ge(*route_in.nth(at, 1))
            with sp.Fori(0, NE) as e:
                stream(Pass("expert", e), e, {})
            sp.wait_ge(*plan_ready.nth(Pass("middle"), 1))
            n_over = sp.value_load(plan[0:1, 0:1], min_val=0, max_val=OVER)
            with sp.If(n_over):
                with sp.Fori(0, n_over) as i:
                    e = sp.value_load(plan[0:1, bass.ds(1 + i, 1)], min_val=0, max_val=NE - 1)
                    at = Pass("over", i)
                    for n, name in enumerate(W_LOADS["over"]):
                        load_weight(at, name, ins["w_expert"][e, n])
            at = Pass("end")
            for name in R_LOADS["end"]:
                load_row(at, name, row_source(at, name, None))
            sp.wait_ge(*h_ready.nth(at, 2))
            sp.dma_start(out.rearrange("(t p) d -> p t d", p=P), x[:, :, :]).then_inc(out_written, 16)
            sp.wait_ge(out_written, 16)

        @block.gpsimd
        def _(pool):
            for s in weights.freed + expert_weights.freed + main_highs.freed + expert_highs.freed + adas.freed + rows.freed + psum.freed:
                pool.sem_inc(s, 1)
            with pool.Fori(0, DEPTH) as l:
                at = Pass("layer", l)
                for name in ADA_LOADS["layer"]:
                    if name == ("ada", 4, 0):
                        pool.wait_ge(*ada_ready.nth(at, 3))
                    if name == ("ada", 10, 0):
                        pool.wait_ge(*group_split.nth(at, 20))
                    pool.wait_ge(*adas.vacant(at, name))
                    n = W_LOADS["layer"].index(name)
                    pool.dma_start(ada_slots[:, adas.slot(at, name), :],
                                   ins["w_layer"][l, n]).then_inc(*adas.fills(at, name))
            at = Pass("middle")
            pool.wait_ge(*bias_made.nth(at, 1))
            pool.dma_start(spread.rearrange("h p m -> p h m"), relw).then_inc(bias_out, 16)
            pool.wait_ge(bias_out, 16)
            shifted = bass.AP(spread.tensor, P - 1, [[383, P], [P * 384, WQ_HEADS], [1, S]])
            pool.dma_start(wbias, shifted).then_inc(bias_in, 16)

        @block.tensor
        def _(pe):
            mm, turn_over = nc.tensor.matmul, nc.tensor.transpose
            at = None

            used = []

            def hand_back():
                while used:
                    w, job = used.pop()
                    pe.wait_ge(*psum.full(at, job))
                    pe.nop().then_inc(*ring(at).frees(at, w))
                    if w in SPLIT[at.part]:
                        pe.nop().then_inc(*highs(at).frees(at, w))

            def split_weights(w):
                return high_slot(at, w), lows(at, w)

            def product(bank, lhs, rhs, start, stop):
                mm(bank, lhs[0], rhs[0], start=start, stop=False)
                mm(bank, lhs[0], rhs[1], start=False, stop=False)
                return mm(bank, lhs[1], rhs[0], start=False, stop=stop)

            def chunk(name, w, src, kt, width, after=None):
                halves = (kt * width + HALF - 1) // HALF
                each = kt // halves
                for half in range(halves):
                    quarter = 2 * SPLIT[at.part].index(w + (half,)) + 1
                    pe.wait_ge(*low_ready.nth(at, quarter))
                    parts_ = [v[:, 0:each * width].rearrange("p (k n) -> p k n", k=each)
                              for v in split_weights(w + (half,))]
                    if half == 0:
                        acc = []
                        for t in range(NT):
                            pe.wait_ge(*psum.vacant(at, name + (t,)))
                            acc.append(banks[psum.slot(at, name + (t,))])
                    for t in range(NT):
                        if after is not None:
                            for g in range(each // 4):
                                pe.wait_ge(*group_split.nth(at, after + (half * each // 4 + g) * NT + t + 1))
                        for k in range(each):
                            kk = half * each + k
                            if t == 0 and k == each // 2:
                                pe.wait_ge(*low_ready.nth(at, quarter + 1))
                            last = product(acc[t][:, 0:width], [v[:, kk, t * P:(t + 1) * P] for v in src],
                                           [v[:, k, :] for v in parts_], kk == 0, kk == kt - 1)
                            if k == 0:
                                hand_back()
                        if half == halves - 1:
                            last.then_inc(*psum.fills(at, name + (t,)))
                    if half == halves - 1:
                        used.append((w + (half,), name + (NT - 1,)))
                    else:
                        last.then_inc(*weights.frees(at, w + (half,)))
                        pe.wait_ge(*weights.vacated(at, w + (half,)))
                        pe.nop().then_inc(*highs(at).frees(at, w + (half,)))
                    yield

            def run(*gens):
                for g in gens:
                    for _ in g:
                        pass

            def transposes(name, src, tiles, signal, first, waits_each=1, halves_each=0):
                hand_back()
                for q in range((tiles + 3) // 4):
                    for t in range(NT):
                        if signal is not None:
                            pe.wait_ge(*signal.nth(at, first + t * waits_each + q * halves_each))
                        pe.wait_ge(*psum.vacant(at, (name, t, q)))
                        bank = banks[psum.slot(at, (name, t, q))]
                        for i in range(min(4, tiles - 4 * q)):
                            f = (4 * q + i) * P
                            last = turn_over(bank[:, i * P:(i + 1) * P], src[:, t, f:f + P], ident)
                        last.then_inc(*psum.fills(at, (name, t, q)))

            def up(tiles):
                for j in range(tiles):
                    quarter = 2 * SPLIT[at.part].index(("up", j, 0)) + 1
                    pe.wait_ge(*low_ready.nth(at, quarter))
                    parts_ = [v.rearrange("p (k g n) -> p k g n", k=KD, g=2) for v in split_weights(("up", j, 0))]
                    pe.wait_ge(*psum.vacant(at, ("up", j)))
                    bank = banks[psum.slot(at, ("up", j))]
                    for g in range(2):
                        for k in range(KD):
                            if g == 0 and k == KD // 2:
                                pe.wait_ge(*low_ready.nth(at, quarter + 1))
                            last = product(bank[:, g * S:(g + 1) * S], [v[:, k, g, :] for v in parts_],
                                           [v[:, k, :] for v in hTs], k == 0, k == KD - 1)
                            if k == 0:
                                hand_back()
                    last.then_inc(*psum.fills(at, ("up", j)))
                    used.append((("up", j, 0), ("up", j)))


            def down(hid, tiles):
                jobs = [("down", t, n) for t in range(NT) for n in range(2)]
                acc = []
                for j in jobs:
                    pe.wait_ge(*psum.vacant(at, j))
                    acc.append(banks[psum.slot(at, j)])
                for c in range(tiles // 2):
                    w = ("down", c, 0)
                    parts_ = [v.rearrange("p (k n) -> p k n", k=2) for v in split_weights(w)]
                    for i in range(2):
                        pe.wait_ge(*low_ready.nth(at, 2 * SPLIT[at.part].index(w) + 1 + i))
                        k = 2 * c + i
                        pe.wait_ge(*hid_ready.nth(at, k + 1))
                        for j, (_, t, n) in enumerate(jobs):
                            last = product(acc[j][:, :], [v[:, k, t * P:(t + 1) * P] for v in hid],
                                           [v[:, i, n * 512:(n + 1) * 512] for v in parts_],
                                           k == 0, k == tiles - 1)
                            hand_back()
                            if k == tiles - 1:
                                last.then_inc(*psum.fills(at, jobs[j]))
                    if 2 * c + 2 < tiles:
                        last.then_inc(*weights.frees(at, w))
                        pe.wait_ge(*weights.vacated(at, w))
                        pe.nop().then_inc(*highs(at).frees(at, w))
                        if at.part == "layer" and c in (4, 8):
                            ada_row(9 + c // 4)
                    else:
                        used.append((w, jobs[-1]))
                        hand_back()

            def ada_column(c):
                pe.wait_ge(*ada_ready.nth(at, c + 1))
                pe.wait_ge(*psum.vacant(at, ("ada", c)))
                bank = banks[psum.slot(at, ("ada", c))]
                for i in range(4):
                    a_ = c % 2 * 512 + i * P
                    last = mm(bank[:, i:i + 1], work[:, a_:a_ + P], ones[:, 0:1], start=True, stop=True)
                last.then_inc(*psum.fills(at, ("ada", c)))

            def ada_row(c):
                pe.wait_ge(*ada_ready.nth(at, c + 1))
                pe.wait_ge(*psum.vacant(at, ("ada", c)))
                bank = banks[psum.slot(at, ("ada", c))]
                a_ = 512 if c > 9 else c % 2 * 512
                mm(bank[:, :], ones, work[:, a_:a_ + 512], start=True, stop=True).then_inc(*psum.fills(at, ("ada", c)))

            def attend(kind, h_, t, qT, kT, maps):
                K = (t + 1) * P
                for m in range(maps):
                    pe.wait_ge(*psum.vacant(at, (kind + "s", h_, t, m)))
                    bank = banks[psum.slot(at, (kind + "s", h_, t, m))]
                    a, b = (m * 64, m * 64 + 64) if maps == 2 else (0, P)
                    last = mm(bank[:, 0:K], qT[a:b, t * P:(t + 1) * P], kT[a:b, 0:K],
                              start=True, stop=kind != "B")
                    if kind == "B":
                        for j in range(t + 1):
                            lhs = upto if j == t else ones
                            mm(bank[:, 0:K], lhs, forget[:, j, h_, 0:K], start=False, stop=False)
                            last = mm(bank[:, 0:K], forget_neg[:, j, h_, :],
                                      steps[:, P - j * P:P - j * P + K], start=False, stop=j == t)
                    last.then_inc(*psum.fills(at, (kind + "s", h_, t, m)))

            def attend_T(kind, h_, t, u, maps):
                hand_back()
                pe.wait_ge(*probs.nth(at, u + 1))
                pe.wait_ge(*psum.vacant(at, (kind + "t", h_, t)))
                bank = banks[psum.slot(at, (kind + "t", h_, t))]
                for m in range(maps):
                    for kt in range(t + 1):
                        i = m * (t + 1) + kt
                        last = turn_over(bank[:, i * P:(i + 1) * P],
                                         scores[:, u % 2, m, kt * P:(kt + 1) * P], ident)
                last.then_inc(*psum.fills(at, (kind + "t", h_, t)))

            def attend_out(kind, h_, t, u, v, maps):
                pe.wait_ge(*probsT_ready.nth(at, u + 1))
                pe.wait_ge(*psum.vacant(at, (kind + "o", h_, t)))
                bank = banks[psum.slot(at, (kind + "o", h_, t))]
                for m in range(maps):
                    for kt in range(t + 1):
                        vv = v(m, kt)
                        n = vv.shape[-1]
                        last = mm(bank[:, m * n:(m + 1) * n], probsT[:, u % 2, m * (t + 1) + kt, :], vv,
                                  start=kt == 0, stop=kt == t)
                last.then_inc(*psum.fills(at, (kind + "o", h_, t)))

            pe.wait_ge(consts_in, 16)
            with pe.Fori(0, DEPTH) as l:
                at = Pass("layer", l)
                transposes("hT", x, KD, h_ready, 1, 0)
                for c in range(4):
                    ada_column(c)
                for n in range(6):
                    kind, c = ("A", n) if n < 3 else ("B", n - 3)
                    run(chunk((kind, c), (kind, c), hTs, KD, 512, 0 if n == 0 else None))
                    if n:
                        hand_back()
                        (ada_row if n < 3 else ada_column)(3 + n)
                    if n == 3:
                        pe.wait_ge(*zA_ready.nth(at, 6))
                        transposes("aT", zA, 8, None, 0)
                run(chunk(("bf", 0), ("bf", 0), hTs, KD, 4))

                def background():
                    for c in range(6):
                        yield from chunk(("C", c), ("C", c), hTs, KD, 512)
                    for c in range(6):
                        yield from chunk(("gate", c), ("gate", c), hTs, KD, 512)

                bg = background()
                next(bg)
                hand_back()
                ada_column(9)
                pe.wait_ge(*qkT_ready.nth(at, 4))
                u = 0
                for h_ in range(A_HEADS):
                    for t in range(NT):
                        attend("A", h_, t, aT[:, h_, :], aT[:, 4 + h_, :], 2)
                        next(bg)
                        attend_T("A", h_, t, u, 1)
                        if u:
                            ph, pt = divmod(u - 1, NT)
                            attend_out("A", ph, pt, u - 1, lambda m, kt: zA[:, kt, 1024 + ph * P:1024 + (ph + 1) * P], 1)
                        u += 1
                next(bg)
                hand_back()
                pe.wait_ge(*zB_ready.nth(at, 6))
                transposes("bT", zB, 8, None, 0)
                attend_out("A", 3, 1, u - 1, lambda m, kt: zA[:, kt, 1024 + 3 * P:1024 + 4 * P], 1)
                pe.wait_ge(*qkT_ready.nth(at, 8))
                pe.wait_ge(*forget_ready.nth(at, 1))
                for h_ in range(B_HEADS):
                    for t in range(NT):
                        attend("B", h_, t, bT[:, h_, :], bT[:, 4 + h_, :], 1)
                        next(bg)
                        attend_T("B", h_, t, u, 1)
                        if u > 8:
                            ph, pt = divmod(u - 9, NT)
                            attend_out("B", ph, pt, u - 1, lambda m, kt: zB[:, kt, 1024 + ph * P:1024 + (ph + 1) * P], 1)
                        u += 1
                pe.wait_ge(*zC_ready.nth(at, 2))
                attend_out("B", 3, 1, u - 1, lambda m, kt: zB[:, kt, 1024 + 3 * P:1024 + 4 * P], 1)
                transposes("cT", zCqk, 8, None, 0)
                next(bg)
                pe.wait_ge(*qkT_ready.nth(at, 12))
                for h_ in range(C_HEADS):
                    for j in range(NT):
                        pe.wait_ge(*psum.vacant(at, ("Cs", h_, j)))
                        bank = banks[psum.slot(at, ("Cs", h_, j))]
                        n = S - j * P
                        mm(bank[:, 0:n], cT[:, 4 + h_, j * P:(j + 1) * P], cT[:, h_, j * P:S],
                           start=True, stop=True).then_inc(*psum.fills(at, ("Cs", h_, j)))
                    next(bg)
                    hand_back()
                    pe.wait_ge(*retained.nth(at, 2 * h_ + 2))
                    flat = scores[:, h_ % 2, :, :].rearrange("p m k -> p (m k)")
                    for t in range(NT):
                        pe.wait_ge(*psum.vacant(at, ("Co", h_, t)))
                        bank = banks[psum.slot(at, ("Co", h_, t))]
                        for j in range(t + 1):
                            at_ = 256 if j else t * P
                            last = mm(bank[:, 0:C_DV], flat[:, at_:at_ + P],
                                      zCv[:, j, h_ * C_DV:(h_ + 1) * C_DV], start=j == 0, stop=j == t)
                        last.then_inc(*psum.fills(at, ("Co", h_, t)))
                for _ in bg:
                    pass
                transposes("yA", yA, 4, y_ready, 1)
                transposes("yB", yB, 4, y_ready, 3)
                for b, (yT, kt) in enumerate(((yATs, 4), (yBTs, 4), (yCTs, 8))):
                    if b == 2:
                        transposes("yC", yC, 8, y_ready, 5)
                    for n in range(2):
                        run(chunk(("p", b, n), ("p" + "abc"[b], n), yT, kt, 512,
                                  None if n else (4, 6, 8)[b]))
                transposes("mT", mix, KD, h_ready, 2, 0)
                for n in range(2):
                    run(chunk(("out", n), ("out", n), mixTs, KD, 512, None if n else 12))
                transposes("h2T", x, KD, h_ready, 3, 0, 1)
                pe.wait_ge(*group_split.nth(at, 20))
                up(FF1 // P)
                down(hid1, FF1 // P)

            at = Pass("middle")
            transposes("gxT", x, KD, h_ready, 1, 0)
            pe.wait_ge(*group_split.nth(at, 4))
            for i in range(8):
                pe.wait_ge(*low_ready.nth(at, 2 * i + 1))
                parts_ = [v.rearrange("p (k n) -> p k n", k=KD) for v in split_weights(("qkv", i, 0))]
                pe.wait_ge(*psum.vacant(at, ("qkv", i)))
                bank = banks[psum.slot(at, ("qkv", i))]
                for g in range(2):
                    for k in range(KD):
                        if g == 0 and k == KD // 2:
                            pe.wait_ge(*low_ready.nth(at, 2 * i + 2))
                        last = product(bank[:, g * S:(g + 1) * S], [v[:, k, g * P:(g + 1) * P] for v in parts_],
                                       [v[:, k, :] for v in hTs], k == 0, k == KD - 1)
                        if k == 0:
                            hand_back()
                last.then_inc(*psum.fills(at, ("qkv", i)))
                used.append((("qkv", i, 0), ("qkv", i)))
            for c in range(2):
                run(chunk(("z", c), ("z", c), hTs, KD, 512))
            run(chunk(("ba", 0), ("ba", 0), hTs, KD, 16))
            hand_back()
            pe.wait_ge(*g_act.nth(at, 8))
            for t in range(NT):
                for q in range(2):
                    pe.wait_ge(*psum.vacant(at, ("vn", t, q)))
                    bank = banks[psum.slot(at, ("vn", t, q))]
                    for i in range(4):
                        last = turn_over(bank[:, i * P:(i + 1) * P], gT[:, 8 + 4 * q + i, t * P:(t + 1) * P], ident)
                    last.then_inc(*psum.fills(at, ("vn", t, q)))
            for p in range(4):
                pe.wait_ge(*g_out.nth(at, p + 1))
                pe.wait_ge(*psum.vacant(at, ("ss", p)))
                bank = banks[psum.slot(at, ("ss", p))]
                mm(bank[:, :], ones, gsq[:, 2 * p:2 * p + 2, :].rearrange("p a n -> p (a n)"),
                   start=True, stop=True).then_inc(*psum.fills(at, ("ss", p)))
            pe.wait_ge(*g_in.nth(at, 1))
            pe.wait_ge(*psum.vacant(at, ("cum", 0)))
            bank = banks[psum.slot(at, ("cum", 0))]
            mm(bank[:, 0:16], upto, decays, start=True, stop=True)
            mm(bank[:, 16:32], ones, decays, start=True, stop=True).then_inc(*psum.fills(at, ("cum", 0)))
            pe.wait_ge(*g_in.nth(at, 2))
            for t in range(NT):
                pe.wait_ge(*psum.vacant(at, ("kn", t)))
                bank = banks[psum.slot(at, ("kn", t))]
                for i in range(GK):
                    last = turn_over(bank[:, i * P:(i + 1) * P], gk[:, i, t * P:(t + 1) * P], ident)
                last.then_inc(*psum.fills(at, ("kn", t)))
            n_in, n_out = 2, 6
            for t in range(NT):
                tok = slice(t * P, (t + 1) * P)
                n_in += 1
                pe.wait_ge(*g_in.nth(at, n_in))
                for q in range(2):
                    pe.wait_ge(*psum.vacant(at, ("G", t, q)))
                    bank = banks[psum.slot(at, ("G", t, q))]
                    for i in range(4):
                        hh = 4 * q + i
                        mm(bank[:, i * P:(i + 1) * P], upto, gplus[:, hh, :], start=True, stop=False)
                        last = mm(bank[:, i * P:(i + 1) * P], gminus[:, hh, :], upto, start=False, stop=True)
                    last.then_inc(*psum.fills(at, ("G", t, q)))
                for name, rhs in (("kk", gk), ("qk", gq)):
                    pe.wait_ge(*psum.vacant(at, (name, t)))
                    bank = banks[psum.slot(at, (name, t))]
                    for i in range(GK):
                        last = mm(bank[:, i * P:(i + 1) * P], gk[:, i, tok], rhs[:, i, tok], start=True, stop=True)
                    last.then_inc(*psum.fills(at, (name, t)))
                n_in += 1
                pe.wait_ge(*g_in.nth(at, n_in))
                for name, src in (("DT", gdec), ("AT", gpair)):
                    for q in range(2):
                        pe.wait_ge(*psum.vacant(at, (name, t, q)))
                        bank = banks[psum.slot(at, (name, t, q))]
                        for i in range(4):
                            last = turn_over(bank[:, i * P:(i + 1) * P], src[:, 4 * q + i, :], ident)
                        last.then_inc(*psum.fills(at, (name, t, q)))
                for lv in range(LEVELS):
                    n_in += 1
                    pe.wait_ge(*g_in.nth(at, n_in))
                    for q in range(2):
                        pe.wait_ge(*psum.vacant(at, ("U", t, lv, q)))
                        bank = banks[psum.slot(at, ("U", t, lv, q))]
                        for i in range(4):
                            last = mm(bank[:, i * P:(i + 1) * P], gbT[:, 4 * q + i, :], gt[:, 4 * q + i, :],
                                      start=True, stop=True)
                        last.then_inc(*psum.fills(at, ("U", t, lv, q)))
                    for q in range(2):
                        n_out += 1
                        pe.wait_ge(*g_out.nth(at, n_out))
                        for name, lhs, rhs in (("V", gtT, gu), ("VT", gu, gtT)):
                            if name == "V" and lv == LEVELS - 1:
                                continue
                            pe.wait_ge(*psum.vacant(at, (name, t, lv, q)))
                            bank = banks[psum.slot(at, (name, t, lv, q))]
                            for i in range(4):
                                last = mm(bank[:, i * P:(i + 1) * P], lhs[:, 4 * q + i, :], rhs[:, 4 * q + i, :],
                                          start=True, stop=True)
                            last.then_inc(*psum.fills(at, (name, t, lv, q)))
                n_in += 1
                pe.wait_ge(*g_in.nth(at, n_in))
                if t:
                    for q in range(2):
                        pe.wait_ge(*psum.vacant(at, ("wT", t, q)))
                        bank = banks[psum.slot(at, ("wT", t, q))]
                        for i in range(4):
                            last = mm(bank[:, i * P:(i + 1) * P], gdec[:, 4 * q + i, :], gtT[:, 4 * q + i, :],
                                      start=True, stop=True)
                        last.then_inc(*psum.fills(at, ("wT", t, q)))
                    n_out += 2
                    pe.wait_ge(*g_out.nth(at, n_out))
                for q in range(2):
                    pe.wait_ge(*psum.vacant(at, ("vnew", t, q)))
                    bank = banks[psum.slot(at, ("vnew", t, q))]
                    for i in range(4):
                        hh = 4 * q + i
                        last = mm(bank[:, i * P:(i + 1) * P], gtT[:, hh, :], gvb[:, t, hh, :],
                                  start=True, stop=t == 0)
                        if t:
                            last = mm(bank[:, i * P:(i + 1) * P], gaT[:, hh, :], gst[:, hh, :],
                                      start=False, stop=True)
                    last.then_inc(*psum.fills(at, ("vnew", t, q)))
                n_in += 1
                pe.wait_ge(*g_in.nth(at, n_in))
                for q in range(2):
                    if t:
                        pe.wait_ge(*psum.vacant(at, ("oa", q)))
                        bank = banks[psum.slot(at, ("oa", q))]
                        for i in range(4):
                            hh = 4 * q + i
                            last = mm(bank[:, i * P:(i + 1) * P], gq[:, hh // 2, tok], gst[:, hh, :],
                                      start=True, stop=True)
                        last.then_inc(*psum.fills(at, ("oa", q)))
                    pe.wait_ge(*psum.vacant(at, ("ob", t, q)))
                    bank = banks[psum.slot(at, ("ob", t, q))]
                    for i in range(4):
                        hh = 4 * q + i
                        last = mm(bank[:, i * P:(i + 1) * P], gaq[:, hh, :], gvn[:, hh, :], start=True, stop=True)
                    last.then_inc(*psum.fills(at, ("ob", t, q)))
                    if not t:
                        pe.wait_ge(*psum.vacant(at, ("st", q)))
                        bank = banks[psum.slot(at, ("st", q))]
                        for i in range(4):
                            hh = 4 * q + i
                            last = mm(bank[:, i * P:(i + 1) * P], gdec[:, hh, :], gvn[:, hh, :],
                                      start=True, stop=True)
                        last.then_inc(*psum.fills(at, ("st", q)))
            transposes("goT", go, KD, y_ready, 1)
            for n in range(2):
                run(chunk(("gout", n), ("gout", n), goTs, KD, 512, None if n else 4))
            transposes("fxT", x, KD, h_ready, 2, 0, 1)
            pe.wait_ge(*group_split.nth(at, 12))
            up(FF2 // P)
            hand_back()
            pe.wait_ge(*g_in.nth(at, n_in + 1))
            pe.wait_ge(*rows.full(at, ("hot", 0)))
            hot = rows.slot(at, ("hot", 0))
            for h_ in range(WQ_HEADS):
                pe.wait_ge(*psum.vacant(at, ("rel", h_)))
                bank = banks[psum.slot(at, ("rel", h_))]
                mm(bank[:, 0:384], relspread[0:BUCKETS, h_, :], R[0:BUCKETS, hot, 0:384],
                   start=True, stop=True).then_inc(*psum.fills(at, ("rel", h_)))
            down(hid2, FF2 // P)
            transposes("wxT", x, KD, h_ready, 4, 0, 1)
            for c in range(2):
                run(chunk(("wq", c), ("wq", c), hTs, KD, 512, None if c else 12))
            run(chunk(("wkv", 0), ("wkv", 0), hTs, KD, 256))
            hand_back()
            pe.wait_ge(*zB_ready.nth(at, 1))
            transposes("wqT", wq, 8, None, 0)
            transposes("wkT", wkd, 2, None, 0)
            pe.wait_ge(*qkT_ready.nth(at, 6))
            u = 0

            def window_out(u):
                ph, pt = divmod(u, NT)
                g = ph // 4
                attend_out("W", ph, pt, u, lambda m, kt: wkv[:, kt, 128 + g * 64:192 + g * 64], 2)

            for hp in range(WQ_HEADS // 2):
                for t in range(NT):
                    attend("W", hp, t, wqT[:, hp, :], wkT[:, hp // 4, :], 2)
                    if u:
                        attend_T("W", (u - 1) // NT, (u - 1) % NT, u - 1, 2)
                    if u > 1:
                        window_out(u - 2)
                    u += 1
            attend_T("W", (u - 1) // NT, (u - 1) % NT, u - 1, 2)
            window_out(u - 2)
            window_out(u - 1)
            transposes("woT", wo, KD, y_ready, 3)
            for n in range(2):
                run(chunk(("wout", n), ("wout", n), woTs, KD, 512, None if n else 16))
            transposes("mxT", x, KD, h_ready, 6, 0, 1)
            run(chunk(("router", 0), ("router", 0), hTs, KD, NE, 20))
            hand_back()
            pe.wait_ge(*route_in.nth(at, 1))
            pe.wait_ge(*psum.vacant(at, ("count", 0)))
            bank = banks[psum.slot(at, ("count", 0))]
            mm(bank[:, 0:NE], upto, places[:, 0, :], start=True, stop=True)
            mm(bank[:, NE:2 * NE], ones, places[:, 0, :], start=True, stop=False)
            mm(bank[:, NE:2 * NE], upto, places[:, 1, :], start=False, stop=True)
            mm(bank[:, 2 * NE:3 * NE], ones, places[:, 0, :], start=True, stop=False)
            mm(bank[:, 2 * NE:3 * NE], ones, places[:, 1, :], start=False,
               stop=True).then_inc(*psum.fills(at, ("count", 0)))

            def gather():
                pe.wait_ge(*select_ready.nth(at, 1))
                for q in range(2):
                    pe.wait_ge(*psum.vacant(at, ("chosen", q)))
                    bank = banks[psum.slot(at, ("chosen", q))]
                    for i in range(4):
                        f = (4 * q + i) * P
                        for t in range(NT):
                            mm(bank[:, i * P:(i + 1) * P], xins[0][:, t, f:f + P], select[:, t, :],
                               start=t == 0, stop=False)
                            last = mm(bank[:, i * P:(i + 1) * P], xins[1][:, t, f:f + P], select[:, t, :],
                                      start=False, stop=t == NT - 1)
                    last.then_inc(*psum.fills(at, ("chosen", q)))

            def expert(gather_next):
                pe.wait_ge(*weigh_ready.nth(at, 1))
                pe.wait_ge(*psum.vacant(at, ("weigh", 0)))
                bank = banks[psum.slot(at, ("weigh", 0))]
                for t in range(NT):
                    last = turn_over(bank[:, t * P:(t + 1) * P], weigh[:, t, :], ident)
                last.then_inc(*psum.fills(at, ("weigh", 0)))

                def hid_turn(c):
                    pe.wait_ge(*hid_ready.nth(at, c + 1))
                    pe.wait_ge(*psum.vacant(at, ("turn", c)))
                    bank = banks[psum.slot(at, ("turn", c))]
                    for i in range(2):
                        last = turn_over(bank[:, i * P:(i + 1) * P], hid_tok[:, c % 2, i * P:(i + 1) * P], ident)
                    last.then_inc(*psum.fills(at, ("turn", c)))

                n = FFE // 256
                for c in range(n):
                    pe.wait_ge(*psum.vacant(at, ("up", c)))
                    bank = banks[psum.slot(at, ("up", c))]
                    for half in range(2):
                        w = ("up", c, half)
                        split = w in SPLIT[at.part]
                        if not split:
                            pe.wait_ge(*ring(at).full(at, w))
                        else:
                            quarter = 2 * SPLIT[at.part].index(w) + 1
                            pe.wait_ge(*low_ready.nth(at, quarter))
                            parts_ = split_weights(w)
                        for k in range(4):
                            if split and k == 2:
                                pe.wait_ge(*low_ready.nth(at, quarter + 1))
                            cols = slice(k * 512, (k + 1) * 512)
                            kk = 4 * half + k
                            if not split:
                                last = mm(bank[:, :], chosenT[:, k, :], raw(at, w)[:, cols], start=k == 0, stop=False)
                            else:
                                last = product(bank[:, :], [v[:, kk, :] for v in chosenTs],
                                               [v[:, cols] for v in parts_], kk == 0, kk == KD - 1)
                            if k == 0:
                                hand_back()
                        if half == 0:
                            last.then_inc(*ring(at).frees(at, w))
                            if split:
                                pe.wait_ge(*ring(at).vacated(at, w))
                                pe.nop().then_inc(*highs(at).frees(at, w))
                    last.then_inc(*psum.fills(at, ("up", c)))
                    used.append((w, ("up", c)))
                    if c:
                        hid_turn(c - 1)
                acc = []
                for half in range(2):
                    pe.wait_ge(*psum.vacant(at, ("down", half)))
                    acc.append(banks[psum.slot(at, ("down", half))])
                for k in range(FFE // P):
                    c, i = divmod(k, 2)
                    w = ("down", c, 0)
                    if c % 4 == 0 and i == 0:
                        pe.wait_ge(*ring(at).full(at, w))
                        pe.wait_ge(*down_ready.nth(at, c // 4 + 1))
                    elif i == 1 and c % 4:
                        pe.wait_ge(*low_ready.nth(at, 2 * SPLIT[at.part].index(w) + 2))
                    elif c % 4 and i == 0:
                        pe.wait_ge(*low_ready.nth(at, 2 * SPLIT[at.part].index(w) + 1))
                        parts_ = split_weights(w)
                        pe.wait_ge(*down_split.nth(at, c - c // 4))
                    for half in range(2):
                        at_ = i * D + half * 512
                        cols = slice(at_, at_ + 512)
                        if c % 4 == 0:
                            last = mm(acc[half][:, :], hidT[:, c // 2 + i, :], raw(at, w)[:, cols], start=k == 0, stop=False)
                        else:
                            last = product(acc[half][:, :], [v[:, k, :] for v in hidTs],
                                           [v[:, cols] for v in parts_], False, k == FFE // P - 1)
                        hand_back()
                        if k == FFE // P - 1:
                            last.then_inc(*psum.fills(at, ("down", half)))
                    if k == 0:
                        hid_turn(n - 1)
                    if i == 1 and k < FFE // P - 1:
                        if c % 4 == 0:
                            last.then_inc(*ring(at).frees(at, w))
                        else:
                            last.then_inc(*ring(at).frees(at, w))
                            pe.wait_ge(*ring(at).vacated(at, w))
                            pe.nop().then_inc(*highs(at).frees(at, w))
                used.append((w, ("down", 1)))
                hand_back()
                if gather_next:
                    gather()
                pe.wait_ge(*weighT_ready.nth(at, 1))
                for half in range(2):
                    pe.wait_ge(*out_ready.nth(at, 1 + half))
                    for t in range(NT):
                        pe.wait_ge(*psum.vacant(at, ("back", t, half)))
                        bank = banks[psum.slot(at, ("back", t, half))]
                        last = mm(bank[:, :], weighT[:, t, :], chosen_out[:, half, :], start=True, stop=True)
                        last.then_inc(*psum.fills(at, ("back", t, half)))

            gather()
            pe.wait_ge(*chosen_ready.nth(at, 1))
            pe.wait_ge(*chosen_split.nth(at, 2))
            with pe.Fori(0, NE) as e:
                at = Pass("expert", e)
                expert(True)
                pe.wait_ge(*chosen_ready.nth(at, 1))
                pe.wait_ge(*chosen_split.nth(at, 2))
            pe.wait_ge(*plan_ready.nth(Pass("middle"), 1))
            n_over = pe.value_load(plan[0:1, 0:1], min_val=0, max_val=OVER)
            with pe.If(n_over):
                with pe.Fori(0, n_over) as i:
                    at = Pass("over", i)
                    gather()
                    pe.wait_ge(*chosen_ready.nth(at, 1))
                    pe.wait_ge(*chosen_split.nth(at, 2))
                    expert(False)

        @block.scalar
        def _(act):
            a = Steps()
            do = nc.scalar.activation

            def evacuate(jobs, dst, signal, scale=None):
                for job in jobs:
                    act.wait_ge(*psum.full(a.at, job))
                    bank = banks[psum.slot(a.at, job)]
                    d = dst(job)
                    n = d.shape[1]
                    src = bank[:, 0:n * P].rearrange("p (a i) -> p a i", a=n)
                    do(d, src, ACT.Copy, scale=1.0 if scale is None else scale(job)
                       ).then_inc(*psum.frees(a.at, job))
                    act.wait_ge(*psum.vacated(a.at, job))
                    act.nop().then_inc(*signal.event(a.at))

            def tiles(name, n, dst, signal, scale=None, width=4):
                evacuate([(name, t, q) for q in range(n) for t in range(NT)],
                         lambda j: dst[:, 4 * j[2]:4 * j[2] + width, j[1] * P:(j[1] + 1) * P], signal, scale)

            def high(n):
                for _ in range(n):
                    w = next(state["split"])
                    act.wait_ge(*highs(a.at).vacant(a.at, w))
                    act.wait_ge(*ring(a.at).full(a.at, w))
                    width = W_WIDTH.get(w[0], HALF)
                    for cols in (slice(0, width // 2), slice(width // 2, width)):
                        do(high_slot(a.at, w)[:, cols], raw(a.at, w)[:, cols],
                           ACT.Copy).then_inc(highs(a.at).filled[highs(a.at).slot(a.at, w)], 1)

            def high_tiles(name, n, dst, shift=None):
                if shift is not None:
                    act.wait_ge(*mod_ready.nth(a.at, 1 + shift // 16))
                for q in range(n):
                    for t in range(NT):
                        job = (name, t, q)
                        act.wait_ge(*psum.full(a.at, job))
                        bank = banks[psum.slot(a.at, job)]
                        cols = slice(t * P, (t + 1) * P)
                        d = dst[0][:, 4 * q:4 * q + 4, cols]
                        if shift is None:
                            do(d, bank[:, :].rearrange("p (a i) -> p a i", a=4), ACT.Copy
                               ).then_inc(*group_high.event(a.at))
                            act.wait_ge(*group_high.last(a.at))
                            continue
                        for i in range(4):
                            f = 4 * q + i
                            o = do(hT[:, f, cols], bank[:, i * P:(i + 1) * P], ACT.Identity,
                                   scale=modc[:, shift + 8 + f:shift + 9 + f], bias=modc[:, shift + f:shift + 1 + f])
                        o.then_inc(*psum.frees(a.at, job))
                        act.wait_ge(*psum.vacated(a.at, job))
                        do(d, hT[:, 4 * q:4 * q + 4, cols], ACT.Copy).then_inc(*group_high.event(a.at))
                        act.wait_ge(*group_high.last(a.at))

            def evict_probsT(kind, h_, t, u, maps):
                n = maps * (t + 1)
                evacuate([(kind + "t", h_, t)], lambda j: probsT[:, u % 2, 0:n, :], probsT_ready)

            def exps(u, t, maps, sink=False):
                act.wait_ge(*masked.nth(a.at, u + 1))
                K = (t + 1) * P
                b = u % 2
                if sink:
                    do(esink[:, b, :], esink[:, b, :], ACT.Exp).then_inc(act_done, 1)
                    act.wait_ge(act_done, a.count())
                for m in range(maps):
                    i = do(scores[:, b, m, 0:K], scores[:, b, m, 0:K], ACT.Exp,
                           bias=nmax[:, b, m:m + 1], accum_out=rsum[:, b, m:m + 1])
                    if m < maps - 1:
                        i.then_inc(act_done, 1)
                        act.wait_ge(act_done, a.count())
                    else:
                        i.then_inc(*exped.event(a.at))
                        act.wait_ge(*exped.last(a.at))

            def root(n):
                state["var"] += 1
                act.wait_ge(*var_ready.nth(a.at, state["var"]))
                r = inv[:, 0:n] if n < 8 else invs
                do(r, r, ACT.Sqrt).then_inc(*std_ready.event(a.at))
                act.wait_ge(*std_ready.last(a.at))

            def hidden(n, func, conv):
                for j in range(n):
                    act.wait_ge(*psum.full(a.at, ("up", j)))
                    bank = banks[psum.slot(a.at, ("up", j))]
                    high(1)
                    if conv:
                        act.wait_ge(*hid_pre.nth(a.at, j + 1))
                    if j >= 2:
                        act.wait_ge(*hid_ready.nth(a.at, j - 1))
                    src = work[:, (j % 2) * S:(j % 2 + 1) * S] if conv else bank[:, 0:S]
                    do(acted[:, j % 2, :], src, func).then_inc(*hid_act.event(a.at))
                    act.wait_ge(*hid_act.last(a.at))

            state = {"var": 0, "split": iter(())}
            a.enter("start")
            act.wait_ge(c_in, 16)
            do(csil, csil, ACT.Silu).then_inc(*c_silu.event(a.at))
            act.wait_ge(*c_silu.last(a.at))
            with act.Fori(0, DEPTH) as l:
                a.enter("layer", l)
                state["var"], state["split"] = 0, iter(SPLIT["layer"])
                high(2)
                high_tiles("hT", 2, hTs, shift=0)
                act.wait_ge(*lam_dots.nth(a.at, 1))
                do(lam[:, 0:2], lam[:, 0:2], ACT.Exp).then_inc(*lam_exps.event(a.at))
                act.wait_ge(*lam_exps.last(a.at))
                high(8)
                tiles("aT", 2, aT, qkT_ready)
                high(4)
                high(2)
                for u in range(8):
                    exps(u, u % NT, 2)
                    evict_probsT("A", u // NT, u % NT, u, 1)
                    high(1)
                    if u == 2:
                        act.wait_ge(*forget_pre.nth(a.at, 1))
                        do(tmp[:, 0:8], tmp[:, 0:8], ACT.Exp).then_inc(*forget_exp.event(a.at))
                        act.wait_ge(*forget_exp.last(a.at))
                        act.wait_ge(*forget_pre.nth(a.at, 2))
                        do(tmp[:, 0:8], tmp[:, 0:8], ACT.Ln).then_inc(*forget_ln.event(a.at))
                        act.wait_ge(*forget_ln.last(a.at))
                tiles("bT", 2, bT, qkT_ready, scale=lambda j: B_DH ** -0.5 if j[2] == 0 else 1.0)
                high(1)
                for u in range(8, 16):
                    exps(u, u % NT, 1)
                    evict_probsT("B", (u - 8) // NT, u % NT, u, 1)
                    high(1)
                    if u == 12:
                        root(8)
                tiles("cT", 2, cT, qkT_ready)
                high(1)
                act.wait_ge(*gate_pre.nth(a.at, 1))
                do(zCg, zCg, ACT.Silu).then_inc(*gate_done.event(a.at))
                act.wait_ge(*gate_done.last(a.at))
                for n, g in enumerate((gA, gB, gC)):
                    act.wait_ge(*gate_pre.nth(a.at, 2 + n))
                    do(g[:, :, :], g[:, :, :], ACT.Sigmoid).then_inc(*gate_done.event(a.at))
                    act.wait_ge(*gate_done.last(a.at))
                    high(2 if n < 2 else 1)
                root(8)
                high_tiles("yA", 1, yATs)
                high_tiles("yB", 1, yBTs)
                high(2)
                high_tiles("yC", 2, yCTs)
                high(6)
                high_tiles("mT", 2, mixTs)
                high(4)
                root(2)
                high_tiles("h2T", 2, hTs, shift=16)
                hidden(FF1 // P, ACT.Gelu, True)
                high(9)
                root(2)
                assert next(state["split"], None) is None
                act.nop().then_inc(act_done, 1)
                act.wait_ge(act_done, a.count())
                act.sem_clear(act_done)
            a.enter("middle")
            state["var"], state["split"] = 0, iter(SPLIT["middle"])
            high(2)
            high_tiles("gxT", 2, hTs)
            for p in range(8):
                high(1)
                act.wait_ge(*g_pre.nth(a.at, p + 1))
                do(gT[:, 2 * p:2 * p + 2, :], gT[:, 2 * p:2 * p + 2, :], ACT.Silu).then_inc(*g_act.event(a.at))
                act.wait_ge(*g_act.last(a.at))
            for p in range(4):
                do(gsq[:, 2 * p:2 * p + 2, :], gT[:, 2 * p:2 * p + 2, :], ACT.Square).then_inc(*g_out.event(a.at))
                act.wait_ge(*g_out.last(a.at))
                if p % 2:
                    high(1)
            high(3)
            act.wait_ge(*g_pre.nth(a.at, 9))
            do(beta, beta, ACT.Sigmoid).then_inc(act_done, 1)
            act.wait_ge(act_done, a.count())
            do(tmp[:, 0:16], tmp[:, 0:16], ACT.Exp).then_inc(act_done, 1)
            act.wait_ge(act_done, a.count())
            do(cums[:, 0:8], cums[:, 0:8], ACT.Exp).then_inc(*g_act.event(a.at))
            act.wait_ge(*g_act.last(a.at))
            act.wait_ge(*g_pre.nth(a.at, 10))
            do(tmp[:, 0:16], tmp[:, 0:16], ACT.Ln).then_inc(*g_act.event(a.at))
            act.wait_ge(*g_act.last(a.at))
            act.wait_ge(*g_pre.nth(a.at, 11))
            do(gsq[:, :, :], gsq[:, :, :], ACT.Sqrt).then_inc(*g_act.event(a.at))
            act.wait_ge(*g_act.last(a.at))
            evacuate([("kn", t) for t in range(NT)], lambda j: gkn[:, j[1], :, :], g_out)
            act.wait_ge(*g_pre.nth(a.at, 12))
            do(egc, cums[:, 0:16], ACT.Exp).then_inc(act_done, 1)
            act.wait_ge(act_done, a.count())
            do(egl, egl, ACT.Exp).then_inc(*g_act.event(a.at))
            act.wait_ge(*g_act.last(a.at))
            n_pre = 12
            for t in range(NT):
                n_pre += 1
                act.wait_ge(*g_pre.nth(a.at, n_pre))
                do(gdec[:, :, :], gdec[:, :, :], ACT.Exp).then_inc(*g_act.event(a.at))
                act.wait_ge(*g_act.last(a.at))
                evacuate([("DT", t, q) for q in range(2)], lambda j: gaq[:, 4 * j[2]:4 * j[2] + 4, :], g_act)
                evacuate([("AT", t, q) for q in range(2)], lambda j: gaT[:, 4 * j[2]:4 * j[2] + 4, :], g_act)
                for lv in range(LEVELS):
                    evacuate([("U", t, lv, q) for q in range(2)], lambda j: gu[:, 4 * j[3]:4 * j[3] + 4, :], g_out)
                if t:
                    evacuate([("wT", t, q) for q in range(2)], lambda j: gaT[:, 4 * j[2]:4 * j[2] + 4, :], g_out,
                             scale=lambda j: -1.0)
            act.wait_ge(*gate_pre.nth(a.at, 1))
            do(gz[:, :, :], gz[:, :, :], ACT.Silu).then_inc(*gate_done.event(a.at))
            act.wait_ge(*gate_done.last(a.at))
            state["var"] += 1
            act.wait_ge(*var_ready.nth(a.at, state["var"]))
            do(tmp[:, 0:16], tmp[:, 0:16], ACT.Sqrt).then_inc(*std_ready.event(a.at))
            act.wait_ge(*std_ready.last(a.at))
            high_tiles("goT", 2, goTs)
            high(4)
            root(2)
            high_tiles("fxT", 2, hTs)
            hidden(FF2 // P, ACT.Silu, False)
            high(11)
            root(2)
            high_tiles("wxT", 2, hTs)
            high(5)
            tiles("wqT", 2, wqT, qkT_ready)
            tiles("wkT", 1, wkT, qkT_ready, width=2)
            for u in range(16):
                exps(u, u % NT, 2, sink=True)
                if u:
                    evict_probsT("W", (u - 1) // NT, (u - 1) % NT, u - 1, 2)
            evict_probsT("W", 7, 1, 15, 2)
            high_tiles("woT", 2, woTs)
            high(3)
            root(2)
            high_tiles("mxT", 2, hTs)
            assert next(state["split"], None) is None
            act.wait_ge(*g_pre.nth(a.at, n_pre + 1))
            do(tmp[:, 0:16], tmp[:, 0:16], ACT.Exp).then_inc(*g_act.event(a.at))
            act.wait_ge(*g_act.last(a.at))
            def high_part(job, d):
                act.wait_ge(*psum.full(a.at, job))
                bank = banks[psum.slot(a.at, job)]
                n = d.shape[1]
                do(d, bank[:, 0:n * P].rearrange("p (a i) -> p a i", a=n), ACT.Copy
                   ).then_inc(*group_high.event(a.at))
                act.wait_ge(*group_high.last(a.at))

            def gathered():
                act.wait_ge(*psum.full(a.at, ("chosen", 0)))
                bank = banks[psum.slot(a.at, ("chosen", 0))]
                do(chosenT[:, 0:4, :], bank[:, :].rearrange("p (a i) -> p a i", a=4), ACT.Copy
                   ).then_inc(*chosen_ready.event(a.at))
                act.wait_ge(*chosen_ready.last(a.at))
                high_part(("chosen", 0), chosenTs[0][:, 0:4, :])
                high_part(("chosen", 1), chosenTs[0][:, 4:8, :])

            gathered()
            act.nop().then_inc(act_done, 1)
            act.wait_ge(act_done, a.count())
            act.sem_clear(act_done)

            def expert():
                state["split"] = iter(SPLIT["expert"])

                def turned(c):
                    if c % 4 == 0:
                        evacuate([("turn", c)], lambda j: hidT[:, c // 2:c // 2 + 2, :], down_ready)
                    else:
                        high_part(("turn", c), hidTs[0][:, 2 * c:2 * c + 2, :])

                high(2)
                evacuate([("weigh", 0)], lambda j: weighT, weighT_ready)
                high(1)
                n = FFE // 256
                for c in range(n):
                    act.wait_ge(*psum.full(a.at, ("up", c)))
                    bank = banks[psum.slot(a.at, ("up", c))]
                    if c >= 2:
                        act.wait_ge(*hid_ready.nth(a.at, c - 1))
                    do(acted[:, c % 2, :], bank[:, 0:S], ACT.Silu).then_inc(*hid_act.event(a.at))
                    act.wait_ge(*hid_act.last(a.at))
                    high(1 + c % 2)
                    if c:
                        turned(c - 1)
                turned(n - 1)
                high(7)
                assert next(state["split"], None) is None
                evacuate([("down", half) for half in range(2)],
                         lambda j: chosen_out[:, j[1], :].rearrange("p (a i) -> p a i", a=4), out_ready)

            with act.Fori(0, NE) as e:
                a.enter("expert", e)
                expert()
                gathered()
            act.wait_ge(*plan_ready.nth(Pass("middle"), 1))
            n_over = act.value_load(plan[0:1, 0:1], min_val=0, max_val=OVER)
            with act.If(n_over):
                with act.Fori(0, n_over) as i:
                    a.enter("over", i)
                    gathered()
                    expert()
            a.enter("end")
            state["var"] = 0
            root(2)

        @block.vector
        def _(dve):
            v = Steps()
            V = nc.vector
            tt, ts, stt = V.tensor_tensor, V.tensor_scalar, V.scalar_tensor_tensor

            def add_row(job, r, dst, width=512, plus=None):
                dve.wait_ge(*psum.full(v.at, job))
                bank = banks[psum.slot(v.at, job)]
                if plus is None:
                    tt(dst, bank[:, 0:width], r[:, 0:width], ALU.add).then_inc(*psum.frees(v.at, job))
                    dve.wait_ge(*psum.vacated(v.at, job))
                else:
                    stt(dst, bank[:, 0:width], plus, r[:, 0:width], ALU.add, ALU.add).then_inc(*psum.frees(v.at, job))
                    dve.wait_ge(*psum.vacated(v.at, job))

            def low(n):
                for _ in range(n):
                    w = next(state["split"])
                    width = W_WIDTH.get(w[0], HALF)
                    for n, cols in enumerate((slice(0, width // 2), slice(width // 2, width))):
                        dve.wait_ge(*highs(v.at).part(v.at, w, n + 1))
                        tt(lows(v.at, w)[:, cols], raw(v.at, w)[:, cols],
                           high_slot(v.at, w)[:, cols].bitcast(F32), ALU.subtract
                           ).then_inc(*low_ready.event(v.at))

            def low_tiles(name, n, dst, shifted=False):
                for q in range(n):
                    for t in range(NT):
                        job = (name, t, q)
                        state["group"] += 1
                        dve.wait_ge(*group_high.nth(v.at, state["group"]))
                        f, cols = slice(4 * q, 4 * q + 4), slice(t * P, (t + 1) * P)
                        hi = dst[0][:, f, cols].bitcast(F32)
                        if shifted:
                            tt(dst[1][:, f, cols], hT[:, f, cols], hi, ALU.subtract
                               ).then_inc(*group_split.event(v.at))
                            continue
                        dve.wait_ge(*psum.full(v.at, job))
                        bank = banks[psum.slot(v.at, job)]
                        tt(dst[1][:, f, cols], bank[:, :].rearrange("p (a i) -> p a i", a=4), hi,
                           ALU.subtract).then_inc(*psum.frees(v.at, job))
                        dve.wait_ge(*psum.vacated(v.at, job))
                        dve.nop().then_inc(*group_split.event(v.at))

            def ada(c, half):
                at_ = 512 if c > 9 else c % 2 * 512
                acc = work[:, at_:at_ + 512]
                w = ("ada", c, half)
                if c < 4:
                    dve.wait_ge(*weights.full(v.at, w))
                    src = W[:, weights.slot(v.at, w), :]
                else:
                    dve.wait_ge(*adas.full(v.at, w))
                    src = ada_slots[:, adas.slot(v.at, w), :]
                for k in range(4):
                    f = 4 * half + k
                    part = src[:, k * 512:(k + 1) * 512]
                    if f == 0:
                        i = ts(acc, part, csil[:, 0:1], None, ALU.mult)
                    else:
                        i = stt(acc, part, csil[:, f:f + 1], acc, ALU.mult, ALU.add)
                    i.then_inc(dve_done, 1)
                    dve.wait_ge(dve_done, v.count())
                if c < 4:
                    dve.nop().then_inc(*weights.frees(v.at, w))
                else:
                    dve.nop().then_inc(*adas.frees(v.at, w))
                if half:
                    dve.nop().then_inc(*ada_ready.event(v.at))

            def ada_in(c):
                if c in (4, 5, 10, 11):
                    dve.wait_ge(*rows.full(v.at, ("ada", c)))
                    r = R[:, rows.slot(v.at, ("ada", c)), :]
                    add_row(("ada", c), r, mod[:, (4, 5, 10, 11).index(c), :])
                    dve.nop().then_inc(*rows.frees(v.at, ("ada", c)))
                    return
                dve.wait_ge(*psum.full(v.at, ("ada", c)))
                bank = banks[psum.slot(v.at, ("ada", c))]
                n = (c if c < 4 else c - 2) * 4
                m = modc[:, n:n + 4]
                stt(m, bank[:, 0:4], 1.0 if c in (2, 3, 8, 9) else 0.0, m, ALU.add, ALU.add
                    ).then_inc(*psum.frees(v.at, ("ada", c)))
                dve.wait_ge(*psum.vacated(v.at, ("ada", c)))
                if c in (3, 9):
                    dve.nop().then_inc(*mod_ready.event(v.at))

            def chunk_in(kind, c, dst):
                dve.wait_ge(*rows.full(v.at, (kind, c)))
                r = R[:, rows.slot(v.at, (kind, c)), :]
                for t in range(NT):
                    add_row((kind, c, t), r, dst(t))
                dve.nop().then_inc(*rows.frees(v.at, (kind, c)))

            def std(n):
                state["std"] += 1
                dve.wait_ge(*std_ready.nth(v.at, state["std"]))
                r = inv[:, 0:n] if n < 8 else invs
                V.reciprocal(r, r).then_inc(dve_done, 1)
                dve.wait_ge(dve_done, v.count())

            def half_stats(t, n):
                V.bn_stats(stats[:, 2 * t + n, :], x[:, t, n * 512:(n + 1) * 512]).then_inc(dve_done, 1)
                dve.wait_ge(dve_done, v.count())

            def layernorm(name):
                for t in range(NT):
                    if name == "ln4":
                        for n in range(2):
                            half_stats(t, n)
                    V.bn_aggr(meanvar[:, t, :], stats[:, 2 * t:2 * t + 2, :]).then_inc(dve_done, 1)
                    dve.wait_ge(dve_done, v.count())
                ts(inv[:, 0:2], meanvar[:, 0:2, 1], EPS, None, ALU.add).then_inc(*var_ready.event(v.at))
                dve.wait_ge(*var_ready.last(v.at))
                std(2)
                for t in range(NT):
                    ts(x[:, t, :], x[:, t, :], meanvar[:, t, 0:1], inv[:, t:t + 1], ALU.subtract, ALU.mult).then_inc(dve_done, 1)
                    dve.wait_ge(dve_done, v.count())
                for n in range(2):
                    dve.wait_ge(*rows.full(v.at, (name, f"g{n}")))
                    g = R[:, rows.slot(v.at, (name, f"g{n}")), :]
                    dve.wait_ge(*rows.full(v.at, (name, f"b{n}")))
                    b = R[:, rows.slot(v.at, (name, f"b{n}")), :]
                    half = x[:, :, n * 512:(n + 1) * 512]
                    tt(half, half, g.unsqueeze(1).to_broadcast([P, NT, 512]), ALU.mult).then_inc(dve_done, 1)
                    dve.wait_ge(dve_done, v.count())
                    tt(half, half, b.unsqueeze(1).to_broadcast([P, NT, 512]), ALU.add).then_inc(dve_done, 1)
                    dve.wait_ge(dve_done, v.count())
                    dve.nop().then_inc(*h_ready.event(v.at))
                    dve.nop().then_inc(*rows.frees(v.at, (name, f"g{n}")))
                    dve.nop().then_inc(*rows.frees(v.at, (name, f"b{n}")))

            def residual(jobs, gate, alpha):
                for job in jobs:
                    t, n = (job[2], job[1]) if job[0] != "down" else (job[1], job[2])
                    dve.wait_ge(*psum.full(v.at, job))
                    bank = banks[psum.slot(v.at, job)]
                    dst = x[:, t, n * 512:(n + 1) * 512]
                    if gate is None:
                        stt(dst, dst, alpha, bank[:, :], ALU.mult, ALU.add).then_inc(*psum.frees(v.at, job))
                        dve.wait_ge(*psum.vacated(v.at, job))
                    else:
                        tt(work[:, 0:512], bank[:, :], mod[:, gate + n, :], ALU.mult).then_inc(*psum.frees(v.at, job))
                        dve.wait_ge(*psum.vacated(v.at, job))
                        stt(dst, dst, alpha, work[:, 0:512], ALU.mult, ALU.add).then_inc(dve_done, 1)
                        dve.wait_ge(dve_done, v.count())
                    half_stats(t, n)

            def outs(name):
                return [(name, n, t) for n in range(2) for t in range(NT)]

            DOWN = [("down", t, n) for t in range(NT) for n in range(2)]

            def finish_hidden(j, hid, conv):
                dve.wait_ge(*hid_act.nth(v.at, j + 1))
                dve.wait_ge(*psum.full(v.at, ("up", j)))
                bank = banks[psum.slot(v.at, ("up", j))]
                whole = acted[:, j % 2, :]
                tt(whole, whole, bank[:, S:2 * S], ALU.mult).then_inc(*psum.frees(v.at, ("up", j)))
                dve.wait_ge(*psum.vacated(v.at, ("up", j)))
                V.tensor_copy(hid[0][:, j, :], whole).then_inc(dve_done, 1)
                dve.wait_ge(dve_done, v.count())
                tt(hid[1][:, j, :], whole, hid[0][:, j, :].bitcast(F32), ALU.subtract
                   ).then_inc(*hid_ready.event(v.at))
                dve.wait_ge(*hid_ready.last(v.at))

            def hidden(n, hid):
                for j in range(n):
                    low(1)
                    finish_hidden(j, hid, False)

            def hidden_conv(n, hid, taps):
                for j in range(n):
                    dve.wait_ge(*psum.full(v.at, ("up", j)))
                    u = banks[psum.slot(v.at, ("up", j))]
                    c = work[:, (j % 2) * S:(j % 2 + 1) * S]
                    low(1)
                    ts(c, u[:, 0:S], taps[:, 2 * n + j:2 * n + j + 1], taps[:, 3 * n + j:3 * n + j + 1], ALU.mult, ALU.add).then_inc(dve_done, 1)
                    dve.wait_ge(dve_done, v.count())
                    stt(c[:, 1:S], u[:, 0:S - 1], taps[:, n + j:n + j + 1], c[:, 1:S], ALU.mult, ALU.add).then_inc(dve_done, 1)
                    dve.wait_ge(dve_done, v.count())
                    stt(c[:, 2:S], u[:, 0:S - 2], taps[:, j:j + 1], c[:, 2:S], ALU.mult, ALU.add).then_inc(*hid_pre.event(v.at))
                    dve.wait_ge(*hid_pre.last(v.at))
                    if j:
                        finish_hidden(j - 1, hid, True)

                finish_hidden(n - 1, hid, True)

            def mask(kind, h_, t, u, maps, scale, bias):
                K = (t + 1) * P
                b = u % 2
                for m in range(maps):
                    job = (kind + "s", h_, t, m)
                    dve.wait_ge(*psum.full(v.at, job))
                    bank = banks[psum.slot(v.at, job)]
                    stt(scores[:, b, m, 0:K], bank[:, 0:K], scale, bias(m, K), ALU.mult, ALU.add).then_inc(*psum.frees(v.at, job))
                    dve.wait_ge(*psum.vacated(v.at, job))
                if kind != "W":
                    V.reduce_max(nmax[:, b, 0:maps], scores[:, b, 0:maps, 0:K], axis=AX, negate=True).then_inc(*masked.event(v.at))
                    dve.wait_ge(*masked.last(v.at))
                else:
                    V.reduce_max(nmax[:, b, :], scores[:, b, :, 0:K], axis=AX).then_inc(dve_done, 1)
                    dve.wait_ge(dve_done, v.count())
                    sink = sinks[:, 2 * h_:2 * h_ + 2]
                    tt(nmax[:, b, :], nmax[:, b, :], sink, ALU.max).then_inc(dve_done, 1)
                    dve.wait_ge(dve_done, v.count())
                    ts(nmax[:, b, :], nmax[:, b, :], -1.0, None, ALU.mult).then_inc(dve_done, 1)
                    dve.wait_ge(dve_done, v.count())
                    tt(esink[:, b, :], sink, nmax[:, b, :], ALU.add).then_inc(*masked.event(v.at))
                    dve.wait_ge(*masked.last(v.at))

            state = {"std": 0, "group": 0, "split": iter(())}
            v.enter("start")
            dve.wait_ge(*c_silu.nth(v.at, 1))
            dve.wait_ge(consts_in, 16)
            dve.wait_ge(x_in, 16)
            dve.nop().then_inc(dve_done, 1)
            dve.wait_ge(dve_done, v.count())
            dve.sem_clear(dve_done)
            with dve.Fori(0, DEPTH) as l:
                v.enter("layer", l)
                state["std"] = 0
                state["group"], state["split"] = 0, iter(SPLIT["layer"])
                dve.nop().then_inc(*h_ready.event(v.at))
                ada(0, 0)
                ada(0, 1)
                dve.wait_ge(*rows.full(v.at, ("adac", 0)))
                V.tensor_copy(modc[:, :], R[:, rows.slot(v.at, ("adac", 0)), 0:32]
                              ).then_inc(*rows.frees(v.at, ("adac", 0)))
                dve.wait_ge(*rows.vacated(v.at, ("adac", 0)))
                for c in range(1, 4):
                    ada(c, 0)
                    ada(c, 1)
                    ada_in(c - 1)
                ada_in(3)
                low(2)
                low_tiles("hT", 2, hTs, shifted=True)
                dve.wait_ge(*rows.full(v.at, ("lam", 0)))
                r = R[:, rows.slot(v.at, ("lam", 0)), :]
                pairs = r[:, 0:256].rearrange("p (a b n) -> p a b n", a=2, b=2)
                dots = scores[:, 0, 0, 0:128].rearrange("p (a n) -> p a n", a=2)
                tt(dots, pairs[:, :, 0, :], pairs[:, :, 1, :], ALU.mult).then_inc(dve_done, 1)
                dve.wait_ge(dve_done, v.count())
                V.reduce_sum(lam[:, 0:2], dots, axis=AX).then_inc(*lam_dots.event(v.at))
                dve.wait_ge(*lam_dots.last(v.at))
                dve.wait_ge(*lam_exps.nth(v.at, 1))
                tt(lam[:, 2:3], lam[:, 1:2], lam[:, 0:1], ALU.subtract).then_inc(dve_done, 1)
                dve.wait_ge(dve_done, v.count())
                tt(lam[:, 2:3], lam[:, 2:3], r[:, 256:257], ALU.subtract).then_inc(dve_done, 1)
                dve.wait_ge(dve_done, v.count())
                V.tensor_copy(lam[:, 3:4], r[:, 257:258]).then_inc(dve_done, 1)
                dve.wait_ge(dve_done, v.count())
                dve.nop().then_inc(*rows.frees(v.at, ("lam", 0)))

                def take_chunk(kind, c, dst, signal):
                    dve.wait_ge(*rows.full(v.at, (kind, c)))
                    r = R[:, rows.slot(v.at, (kind, c)), :]
                    for t in range(NT):
                        add_row((kind, c, t), r, dst(t))
                        if signal is not None:
                            dve.nop().then_inc(*signal.event(v.at))
                    dve.nop().then_inc(*rows.frees(v.at, (kind, c)))

                for n in range(6):
                    kind, c = ("A", n) if n < 3 else ("B", n - 3)
                    z, ready = (zA, zA_ready) if n < 3 else (zB, zB_ready)
                    low(1)
                    ada(4 + n, 0)
                    low(1)
                    ada(4 + n, 1)
                    take_chunk(kind, c, lambda t: z[:, t, c * 512:(c + 1) * 512], ready)
                    if n:
                        ada_in(3 + n)
                dve.wait_ge(*rows.full(v.at, ("bf", 0)))
                r = R[:, rows.slot(v.at, ("bf", 0)), :]
                for t in range(NT):
                    add_row(("bf", 0, t), r, logf[:, 4 * t:4 * t + 4], width=4)
                dve.nop().then_inc(*rows.frees(v.at, ("bf", 0)))
                low(2)
                ada_in(9)

                def background():
                    def one(kind, c, dst):
                        dve.wait_ge(*rows.full(v.at, (kind, c)))
                        r = R[:, rows.slot(v.at, (kind, c)), :]
                        for t in range(NT):
                            add_row((kind, c, t), r, dst(t))
                        dve.nop().then_inc(*rows.frees(v.at, (kind, c)))
                        if kind == "C" and c == 5:
                            dve.nop().then_inc(*gate_pre.event(v.at))
                        if kind == "gate" and c % 2:
                            dve.nop().then_inc(*gate_pre.event(v.at))
                    for c in range(6):
                        part = (zCqk, zCv, zCg)[c // 2]
                        one("C", c, lambda t: part[:, t, (c % 2) * 512:(c % 2 + 1) * 512])
                        yield
                    for c in range(6):
                        g = (gA, gB, gC)[c // 2]
                        one("gate", c, lambda t: g[:, t, (c % 2) * 512:(c % 2 + 1) * 512])
                        yield

                bg = background()

                def a_out(u):
                    job = ("Ao", u // NT, u % NT)
                    dve.wait_ge(*psum.full(v.at, job))
                    bank = banks[psum.slot(v.at, job)]
                    V.tensor_copy(yA[:, u % NT, (u // NT) * P:(u // NT + 1) * P], bank[:, 0:P]).then_inc(*psum.frees(v.at, job))
                    dve.wait_ge(*psum.vacated(v.at, job))

                def b_out(u):
                    job = ("Bo", (u - 8) // NT, u % NT)
                    dve.wait_ge(*psum.full(v.at, job))
                    bank = banks[psum.slot(v.at, job)]
                    hh = (u - 8) // NT
                    ts(yB[:, u % NT, hh * P:(hh + 1) * P], bank[:, 0:P],
                                         rinv[:, u % 3, 0:1], None, ALU.mult).then_inc(*psum.frees(v.at, job))
                    dve.wait_ge(*psum.vacated(v.at, job))

                f8, t8 = logf[:, 0:8], tmp[:, 0:8]
                f3 = f8.rearrange("p (t h) -> p t h", t=NT)

                def log_forget():
                    stt(t8, f8, -1.0, f8, ALU.mult, ALU.min).then_inc(dve_done, 1)
                    dve.wait_ge(dve_done, v.count())
                    dve.nop().then_inc(*forget_pre.event(v.at))
                    dve.wait_ge(*forget_exp.nth(v.at, 1))
                    ts(t8, t8, 1.0, None, ALU.add).then_inc(dve_done, 1)
                    dve.wait_ge(dve_done, v.count())
                    dve.nop().then_inc(*forget_pre.event(v.at))
                    dve.wait_ge(*forget_ln.nth(v.at, 1))
                    stt(f8, f8, 0.0, t8, ALU.min, ALU.subtract).then_inc(dve_done, 1)
                    dve.wait_ge(dve_done, v.count())

                def spread_forget():
                    for t in range(NT):
                        V.tensor_copy(forget[:, t, :, :], f3[:, t, :].unsqueeze(2).to_broadcast([P, B_HEADS, S])).then_inc(dve_done, 1)
                        dve.wait_ge(dve_done, v.count())
                    for t in range(NT):
                        i = ts(forget_neg[:, t, :, :], f3[:, t, :].unsqueeze(2).to_broadcast([P, B_HEADS, P]),
                               -1.0, None, ALU.mult)
                        if t == 0:
                            i.then_inc(dve_done, 1)
                            dve.wait_ge(dve_done, v.count())
                        else:
                            i.then_inc(*forget_ready.event(v.at))
                            dve.wait_ge(*forget_ready.last(v.at))

                for u in range(8):
                    h_, t = divmod(u, NT)
                    K, b = (t + 1) * P, u % 2
                    mask("A", h_, t, u, 2, A_DQK ** -0.5, lambda m, K: blocks[:, 2 * P - K:2 * P])
                    dve.wait_ge(*exped.nth(v.at, u + 1))
                    V.reciprocal(rsum[:, b, :], rsum[:, b, :]).then_inc(dve_done, 1)
                    dve.wait_ge(dve_done, v.count())
                    tt(rsum[:, b, 1:2], rsum[:, b, 1:2], lam[:, 2:3], ALU.mult).then_inc(dve_done, 1)
                    dve.wait_ge(dve_done, v.count())
                    ts(scores[:, b, 1, 0:K], scores[:, b, 1, 0:K], rsum[:, b, 1:2], None, ALU.mult).then_inc(dve_done, 1)
                    dve.wait_ge(dve_done, v.count())
                    stt(scores[:, b, 0, 0:K], scores[:, b, 0, 0:K], rsum[:, b, 0:1],
                                      scores[:, b, 1, 0:K], ALU.mult, ALU.add).then_inc(*probs.event(v.at))
                    dve.wait_ge(*probs.last(v.at))
                    if u % 2 == 0:
                        next(bg)
                    if u:
                        a_out(u - 1)
                    low(1)
                    if u == 2:
                        log_forget()
                    if u == 5:
                        spread_forget()
                next(bg)
                a_out(7)
                low(1)

                def sums_a():
                    for t in range(NT):
                        sq = work[:, 0:512]
                        tt(sq, yA[:, t, :], yA[:, t, :], ALU.mult).then_inc(dve_done, 1)
                        dve.wait_ge(dve_done, v.count())
                        V.reduce_sum(invs[:, 4 * t:4 * t + 4], sq.rearrange("p (h f) -> p h f", h=A_HEADS), axis=AX).then_inc(dve_done, 1)
                        dve.wait_ge(dve_done, v.count())
                        if t == NT - 1:
                            ts(invs, invs, 1.0 / P, EPS, ALU.mult, ALU.add).then_inc(*var_ready.event(v.at))
                            dve.wait_ge(*var_ready.last(v.at))

                def scale_a():
                    std(8)
                    dve.wait_ge(*rows.full(v.at, ("gdiff", 0)))
                    g = R[:, rows.slot(v.at, ("gdiff", 0)), :]
                    for t in range(NT):
                        ya = yA[:, t, :].rearrange("p (h f) -> p h f", h=A_HEADS)
                        tt(ya, ya, invs[:, 4 * t:4 * t + 4].unsqueeze(2).to_broadcast([P, A_HEADS, P]), ALU.mult).then_inc(dve_done, 1)
                        dve.wait_ge(dve_done, v.count())
                        stt(yA[:, t, :], yA[:, t, :], lam[:, 3:4], g, ALU.mult, ALU.mult).then_inc(*y_ready.event(v.at))
                        dve.wait_ge(*y_ready.last(v.at))
                    dve.nop().then_inc(*rows.frees(v.at, ("gdiff", 0)))


                def rotate(t):
                    for s in range(2):
                        z = zCqk[:, t, s * 512:(s + 1) * 512].rearrange("p (h f) -> p h f", h=C_HEADS)
                        t1, t2 = z[:, :, 0:64], z[:, :, 64:128]
                        w = [work[:, i * 256:(i + 1) * 256].rearrange("p (h f) -> p h f", h=C_HEADS) for i in range(3)]
                        cs = cos[:, t, :].unsqueeze(1).to_broadcast([P, C_HEADS, 64])
                        sn = sin[:, t, :].unsqueeze(1).to_broadcast([P, C_HEADS, 64])
                        tt(w[0], t1, cs, ALU.mult).then_inc(dve_done, 1)
                        dve.wait_ge(dve_done, v.count())
                        tt(w[1], t2, sn, ALU.mult).then_inc(dve_done, 1)
                        dve.wait_ge(dve_done, v.count())
                        tt(w[2], t1, sn, ALU.mult).then_inc(dve_done, 1)
                        dve.wait_ge(dve_done, v.count())
                        tt(t1, w[0], w[1], ALU.subtract).then_inc(dve_done, 1)
                        dve.wait_ge(dve_done, v.count())
                        tt(w[0], t2, cs, ALU.mult).then_inc(dve_done, 1)
                        dve.wait_ge(dve_done, v.count())
                        tt(t2, w[0], w[2], ALU.add).then_inc(dve_done, 1)
                        dve.wait_ge(dve_done, v.count())

                for u in range(8, 16):
                    h_, t = divmod(u - 8, NT)
                    b = u % 2
                    mask("B", h_, t, u, 1, 1.0, lambda m, K: causal[:, 2 * P - K:2 * P])
                    dve.wait_ge(*exped.nth(v.at, u + 1))
                    V.reciprocal(rinv[:, u % 3, 0:1], rsum[:, b, 0:1]).then_inc(*probs.event(v.at))
                    dve.wait_ge(*probs.last(v.at))
                    if u % 2:
                        next(bg)
                    if u > 8:
                        b_out(u - 1)
                    low(1)
                    if u == 12:
                        sums_a()
                    if u == 13:
                        scale_a()
                    if u in (9, 10):
                        rotate(u - 9)
                        dve.nop().then_inc(*zC_ready.event(v.at))
                b_out(15)
                low(1)
                for h_ in range(C_HEADS):
                    flat = scores[:, h_ % 2, :, :].rearrange("p m k -> p (m k)")
                    for j in range(NT):
                        job = ("Cs", h_, j)
                        dve.wait_ge(*psum.full(v.at, job))
                        bank = banks[psum.slot(v.at, job)]
                        n, o = S - j * P, j * S
                        tt(flat[:, o:o + n], bank[:, 0:n], decay[:, h_, 0:n], ALU.mult).then_inc(*psum.frees(v.at, job))
                        dve.wait_ge(*psum.vacated(v.at, job))
                        dve.nop().then_inc(*retained.event(v.at))
                    if h_ % 2 == 0:
                        next(bg)
                    low(1)
                    for t in range(NT):
                        job = ("Co", h_, t)
                        dve.wait_ge(*psum.full(v.at, job))
                        bank = banks[psum.slot(v.at, job)]
                        V.bn_stats(stats[:, 0, :], bank[:, 0:C_DV]).then_inc(dve_done, 1)
                        dve.wait_ge(dve_done, v.count())
                        V.bn_aggr(meanvar[:, 4 * t + h_, :], stats[:, 0, :]).then_inc(dve_done, 1)
                        dve.wait_ge(dve_done, v.count())
                        V.tensor_copy(yC[:, t, h_ * C_DV:(h_ + 1) * C_DV], bank[:, 0:C_DV]).then_inc(*psum.frees(v.at, job))
                        dve.wait_ge(*psum.vacated(v.at, job))
                next(bg)
                low(1)
                dve.nop().then_inc(*y_ready.event(v.at))
                dve.nop().then_inc(*y_ready.event(v.at))
                ts(invs, meanvar[:, 0:8, 1], EPS, None, ALU.add).then_inc(*var_ready.event(v.at))
                dve.wait_ge(*var_ready.last(v.at))
                std(8)
                low_tiles("yA", 1, yATs)
                low_tiles("yB", 1, yBTs)
                dve.wait_ge(*gate_done.nth(v.at, 1))
                dve.wait_ge(*rows.full(v.at, ("gret", 0)))
                g0 = R[:, rows.slot(v.at, ("gret", 0)), :]
                dve.wait_ge(*rows.full(v.at, ("gret", 1)))
                g1 = R[:, rows.slot(v.at, ("gret", 1)), :]
                for t in range(NT):
                    for h_ in range(C_HEADS):
                        yc = yC[:, t, h_ * C_DV:(h_ + 1) * C_DV]
                        ts(yc, yc, meanvar[:, 4 * t + h_, 0:1], invs[:, 4 * t + h_:4 * t + h_ + 1],
                             ALU.subtract, ALU.mult).then_inc(dve_done, 1)
                        dve.wait_ge(dve_done, v.count())
                    for n, g in enumerate((g0, g1)):
                        yc = yC[:, t, n * 512:(n + 1) * 512]
                        tt(yc, yc, g, ALU.mult).then_inc(dve_done, 1)
                        dve.wait_ge(dve_done, v.count())
                    tt(yC[:, t, :], yC[:, t, :], zCg[:, t, :], ALU.mult).then_inc(*y_ready.event(v.at))
                    dve.wait_ge(*y_ready.last(v.at))
                    low(1)
                dve.nop().then_inc(*rows.frees(v.at, ("gret", 0)))
                dve.nop().then_inc(*rows.frees(v.at, ("gret", 1)))
                for b_, g in enumerate((gA, gB, gC)):
                    dve.wait_ge(*gate_done.nth(v.at, 2 + b_))
                    for n in range(2):
                        for t in range(NT):
                            job = ("p", b_, n, t)
                            dve.wait_ge(*psum.full(v.at, job))
                            bank = banks[psum.slot(v.at, job)]
                            cols = slice(n * 512, (n + 1) * 512)
                            if b_ == 0:
                                tt(mix[:, t, cols], bank[:, :], g[:, t, cols], ALU.mult).then_inc(*psum.frees(v.at, job))
                                dve.wait_ge(*psum.vacated(v.at, job))
                            else:
                                tt(work[:, 0:512], bank[:, :], g[:, t, cols], ALU.mult).then_inc(*psum.frees(v.at, job))
                                dve.wait_ge(*psum.vacated(v.at, job))
                                tt(mix[:, t, cols], mix[:, t, cols], work[:, 0:512], ALU.add).then_inc(dve_done, 1)
                                dve.wait_ge(dve_done, v.count())
                    if b_ == 0:
                        low_tiles("yC", 2, yCTs)
                    low(2 if b_ < 2 else 0)
                dve.nop().then_inc(*h_ready.event(v.at))
                low(2)
                low_tiles("mT", 2, mixTs)
                low(2)
                residual(outs("out")[0:2], 0, ALPHA)
                low(2)
                residual(outs("out")[2:4], 0, ALPHA)
                layernorm("ln1")
                low_tiles("h2T", 2, hTs, shifted=True)
                dve.wait_ge(*rows.full(v.at, ("conv", 0)))
                taps = R[:, rows.slot(v.at, ("conv", 0)), :]
                hidden_conv(FF1 // P, hid1, taps)
                dve.nop().then_inc(*rows.frees(v.at, ("conv", 0)))
                low(2)
                ada(10, 0)
                low(1)
                ada(10, 1)
                low(2)
                ada_in(10)
                ada(11, 0)
                low(1)
                ada(11, 1)
                low(3)
                ada_in(11)
                residual(DOWN, 2, ALPHA)
                layernorm("ln2")
                assert next(state["split"], None) is None
                dve.nop().then_inc(dve_done, 1)
                dve.wait_ge(dve_done, v.count())
                dve.sem_clear(dve_done)

            v.enter("middle")
            state["std"], state["group"], state["split"] = 0, 0, iter(SPLIT["middle"])
            dve.nop().then_inc(*h_ready.event(v.at))
            low(2)
            low_tiles("gxT", 2, hTs)
            dve.wait_ge(*rows.full(v.at, ("gconv", 0)))
            taps = R[:, rows.slot(v.at, ("gconv", 0)), :]
            for p in range(8):
                dve.wait_ge(*psum.full(v.at, ("qkv", p)))
                u = banks[psum.slot(v.at, ("qkv", p))]
                for g in range(2):
                    f = 2 * p + g
                    c, s = gT[:, f, :], u[:, g * S:(g + 1) * S]
                    ts(c, s, taps[:, 48 + f:49 + f], None, ALU.mult).then_inc(dve_done, 1)
                    dve.wait_ge(dve_done, v.count())
                    for back in range(1, GDN_TAPS):
                        tap = 16 * (GDN_TAPS - 1 - back) + f
                        i = stt(c[:, back:S], s[:, 0:S - back], taps[:, tap:tap + 1], c[:, back:S], ALU.mult, ALU.add)
                        if g == 1 and back == GDN_TAPS - 1:
                            i.then_inc(*psum.frees(v.at, ("qkv", p)))
                            dve.wait_ge(*psum.vacated(v.at, ("qkv", p)))
                            dve.nop().then_inc(*g_pre.event(v.at))
                        else:
                            i.then_inc(dve_done, 1)
                            dve.wait_ge(dve_done, v.count())
                low(1)
            dve.nop().then_inc(*rows.frees(v.at, ("gconv", 0)))
            for c in range(2):
                low(2 - c)
                for t in range(NT):
                    dve.wait_ge(*psum.full(v.at, ("z", c, t)))
                    bank = banks[psum.slot(v.at, ("z", c, t))]
                    V.tensor_copy(gz[:, t, c * 512:(c + 1) * 512], bank[:, :]).then_inc(*psum.frees(v.at, ("z", c, t)))
                    dve.wait_ge(*psum.vacated(v.at, ("z", c, t)))
            dve.nop().then_inc(*gate_pre.event(v.at))
            dve.wait_ge(*rows.full(v.at, ("gpar", 0)))
            par = R[:, rows.slot(v.at, ("gpar", 0)), :]
            low(2)
            d16 = decays.rearrange("p (t h) -> p t h", t=NT)
            b16 = beta.rearrange("p (t h) -> p t h", t=NT)
            for t in range(NT):
                dve.wait_ge(*psum.full(v.at, ("ba", 0, t)))
                bank = banks[psum.slot(v.at, ("ba", 0, t))]
                V.tensor_copy(b16[:, t, :], bank[:, 0:8]).then_inc(dve_done, 1)
                dve.wait_ge(dve_done, v.count())
                tt(d16[:, t, :], bank[:, 8:16], par[:, 8:16], ALU.add).then_inc(*psum.frees(v.at, ("ba", 0, t)))
                dve.wait_ge(*psum.vacated(v.at, ("ba", 0, t)))
            V.tensor_copy(cums[:, 0:8], par[:, 0:8]).then_inc(dve_done, 1)
            dve.wait_ge(dve_done, v.count())
            V.tensor_copy(nw, par[:, 16:144]).then_inc(dve_done, 1)
            dve.wait_ge(dve_done, v.count())
            dve.nop().then_inc(*rows.frees(v.at, ("gpar", 0)))
            t16 = tmp[:, 0:16]
            stt(t16, decays, -1.0, decays, ALU.mult, ALU.min).then_inc(dve_done, 1)
            dve.wait_ge(dve_done, v.count())
            dve.nop().then_inc(*g_pre.event(v.at))
            dve.wait_ge(*g_act.nth(v.at, 9))
            ts(t16, t16, 1.0, None, ALU.add).then_inc(dve_done, 1)
            dve.wait_ge(dve_done, v.count())
            dve.nop().then_inc(*g_pre.event(v.at))
            dve.wait_ge(*g_act.nth(v.at, 10))
            stt(decays, decays, 0.0, t16, ALU.max, ALU.add).then_inc(dve_done, 1)
            dve.wait_ge(dve_done, v.count())
            tt(d16, d16, cums[:, 0:8].unsqueeze(1).to_broadcast([P, NT, GV]), ALU.mult).then_inc(dve_done, 1)
            dve.wait_ge(dve_done, v.count())
            ts(decays, decays, -1.0, None, ALU.mult).then_inc(*g_in.event(v.at))
            dve.wait_ge(*g_in.last(v.at))
            for t in range(NT):
                for q in range(2):
                    dve.wait_ge(*psum.full(v.at, ("vn", t, q)))
                    bank = banks[psum.slot(v.at, ("vn", t, q))]
                    tt(gvb[:, t, 4 * q:4 * q + 4, :], bank[:, :].rearrange("p (a i) -> p a i", a=4),
                              b16[:, t, 4 * q:4 * q + 4].unsqueeze(2).to_broadcast([P, 4, P]), ALU.mult).then_inc(*psum.frees(v.at, ("vn", t, q)))
                    dve.wait_ge(*psum.vacated(v.at, ("vn", t, q)))
            for p in range(4):
                dve.wait_ge(*psum.full(v.at, ("ss", p)))
                bank = banks[psum.slot(v.at, ("ss", p))]
                ts(gsq[:, 2 * p:2 * p + 2, :].rearrange("p a n -> p (a n)"), bank[:, :],
                                           GDN_EPS, None, ALU.add).then_inc(*psum.frees(v.at, ("ss", p)))
                dve.wait_ge(*psum.vacated(v.at, ("ss", p)))
            dve.nop().then_inc(*g_pre.event(v.at))
            dve.wait_ge(*g_act.nth(v.at, 11))
            V.reciprocal(gsq[:, :, :], gsq[:, :, :]).then_inc(dve_done, 1)
            dve.wait_ge(dve_done, v.count())
            stt(gq, gq, GD ** -0.5, gsq[:, 0:4, :], ALU.mult, ALU.mult).then_inc(dve_done, 1)
            dve.wait_ge(dve_done, v.count())
            tt(gk, gk, gsq[:, 4:8, :], ALU.mult).then_inc(*g_in.event(v.at))
            dve.wait_ge(*g_in.last(v.at))
            dve.wait_ge(*psum.full(v.at, ("cum", 0)))
            bank = banks[psum.slot(v.at, ("cum", 0))]
            V.tensor_copy(cums, bank[:, 0:32]).then_inc(dve_done, 1)
            dve.wait_ge(dve_done, v.count())
            tt(egl, cums[:, 16:32], cums[:, 0:16], ALU.subtract).then_inc(*psum.frees(v.at, ("cum", 0)))
            dve.wait_ge(*psum.vacated(v.at, ("cum", 0)))
            dve.nop().then_inc(*g_pre.event(v.at))
            dve.wait_ge(*g_act.nth(v.at, 12))
            n_act = 12
            e16 = egc.rearrange("p (t h) -> p t h", t=NT)
            l16 = egl.rearrange("p (t h) -> p t h", t=NT)

            def spread8(col):
                return col.unsqueeze(2).to_broadcast([P, GV, P])

            def pairs8(t):
                return gkn[:, t, :, :].unsqueeze(2).to_broadcast([P, GK, 2, P])

            def split8(m):
                return m.rearrange("p (a b) i -> p a b i", b=2)

            for t in range(NT):
                V.tensor_copy(gplus, spread8(d16[:, t, :])).then_inc(dve_done, 1)
                dve.wait_ge(dve_done, v.count())
                ts(gminus, spread8(d16[:, t, :]), -1.0, None, ALU.mult).then_inc(*g_in.event(v.at))
                dve.wait_ge(*g_in.last(v.at))
                for q in range(2):
                    dve.wait_ge(*psum.full(v.at, ("G", t, q)))
                    bank = banks[psum.slot(v.at, ("G", t, q))]
                    tt(gdec[:, 4 * q:4 * q + 4, :], bank[:, :].rearrange("p (a i) -> p a i", a=4),
                              causal[:, P:2 * P].unsqueeze(1).to_broadcast([P, 4, P]), ALU.add).then_inc(*psum.frees(v.at, ("G", t, q)))
                    dve.wait_ge(*psum.vacated(v.at, ("G", t, q)))
                dve.nop().then_inc(*g_pre.event(v.at))
                n_act += 1
                dve.wait_ge(*g_act.nth(v.at, n_act))
                dve.wait_ge(*psum.full(v.at, ("kk", t)))
                bank = banks[psum.slot(v.at, ("kk", t))]
                kk = bank[:, :].rearrange("p (a i) -> p a i", a=4)
                for half in range(2):
                    i = tt(split8(gpair)[:, :, half, :], kk, split8(gdec)[:, :, half, :], ALU.mult)
                    if half == 0:
                        i.then_inc(dve_done, 1)
                        dve.wait_ge(dve_done, v.count())
                    else:
                        i.then_inc(*psum.frees(v.at, ("kk", t)))
                        dve.wait_ge(*psum.vacated(v.at, ("kk", t)))
                tt(gpair, gpair, const("strict").unsqueeze(1).to_broadcast([P, GV, P]), ALU.mult).then_inc(dve_done, 1)
                dve.wait_ge(dve_done, v.count())
                tt(gpair, gpair, spread8(b16[:, t, :]), ALU.mult).then_inc(*g_in.event(v.at))
                dve.wait_ge(*g_in.last(v.at))
                n_act += 2
                dve.wait_ge(*g_act.nth(v.at, n_act))
                dve.wait_ge(*psum.full(v.at, ("qk", t)))
                bank = banks[psum.slot(v.at, ("qk", t))]
                qk = bank[:, :].rearrange("p (a i) -> p a i", a=4)
                for half in range(2):
                    g = split8(gaq)[:, :, half, :]
                    i = tt(g, qk, g, ALU.mult)
                    if half == 0:
                        i.then_inc(dve_done, 1)
                        dve.wait_ge(dve_done, v.count())
                    else:
                        i.then_inc(*psum.frees(v.at, ("qk", t)))
                        dve.wait_ge(*psum.vacated(v.at, ("qk", t)))
                n_act += 2
                dve.wait_ge(*g_act.nth(v.at, n_act))
                eye = ident.unsqueeze(1).to_broadcast([P, GV, P])
                V.tensor_copy(gt, eye).then_inc(dve_done, 1)
                dve.wait_ge(dve_done, v.count())
                V.tensor_copy(gtT, eye).then_inc(dve_done, 1)
                dve.wait_ge(dve_done, v.count())
                for lv in range(LEVELS):
                    tt(gbT, gaT, levels[:, lv, :].unsqueeze(1).to_broadcast([P, GV, P]), ALU.mult).then_inc(*g_in.event(v.at))
                    dve.wait_ge(*g_in.last(v.at))
                    for q in range(2):
                        for name, m in (("V", gt), ("VT", gtT)):
                            if name == "V" and lv == LEVELS - 1:
                                continue
                            job = (name, t, lv, q)
                            dve.wait_ge(*psum.full(v.at, job))
                            bank = banks[psum.slot(v.at, job)]
                            if name == "V":
                                dve.wait_ge(*psum.full(v.at, ("VT", t, lv, q)))
                            mq = m[:, 4 * q:4 * q + 4, :]
                            tt(mq, mq, bank[:, :].rearrange("p (a i) -> p a i", a=4), ALU.subtract).then_inc(*psum.frees(v.at, job))
                            dve.wait_ge(*psum.vacated(v.at, job))
                if t:
                    tt(split8(gdec), pairs8(t), split8(spread8(e16[:, t, :])), ALU.mult).then_inc(dve_done, 1)
                    dve.wait_ge(dve_done, v.count())
                    tt(gdec, gdec, spread8(b16[:, t, :]), ALU.mult).then_inc(*g_in.event(v.at))
                    dve.wait_ge(*g_in.last(v.at))
                else:
                    g_out_wait = 6
                    dve.wait_ge(*g_out.nth(v.at, g_out_wait))
                    tt(split8(gdec), pairs8(t), split8(spread8(l16[:, t, :])), ALU.mult).then_inc(*g_in.event(v.at))
                    dve.wait_ge(*g_in.last(v.at))
                for q in range(2):
                    dve.wait_ge(*psum.full(v.at, ("vnew", t, q)))
                    bank = banks[psum.slot(v.at, ("vnew", t, q))]
                    V.tensor_copy(gvn[:, 4 * q:4 * q + 4, :],
                                                              bank[:, :].rearrange("p (a i) -> p a i", a=4)).then_inc(*psum.frees(v.at, ("vnew", t, q)))
                    dve.wait_ge(*psum.vacated(v.at, ("vnew", t, q)))
                dve.nop().then_inc(*g_in.event(v.at))
                for q in range(2):
                    cols = go[:, t, q * 512:(q + 1) * 512]
                    c4 = cols.rearrange("p (a i) -> p a i", a=4)
                    if t:
                        dve.wait_ge(*psum.full(v.at, ("oa", q)))
                        bank = banks[psum.slot(v.at, ("oa", q))]
                        tt(c4, bank[:, :].rearrange("p (a i) -> p a i", a=4),
                                                   e16[:, t, 4 * q:4 * q + 4].unsqueeze(2).to_broadcast([P, 4, P]), ALU.mult).then_inc(*psum.frees(v.at, ("oa", q)))
                        dve.wait_ge(*psum.vacated(v.at, ("oa", q)))
                        dve.wait_ge(*psum.full(v.at, ("ob", t, q)))
                        bank = banks[psum.slot(v.at, ("ob", t, q))]
                        tt(cols, cols, bank[:, :], ALU.add).then_inc(*psum.frees(v.at, ("ob", t, q)))
                        dve.wait_ge(*psum.vacated(v.at, ("ob", t, q)))
                    else:
                        dve.wait_ge(*psum.full(v.at, ("ob", t, q)))
                        bank = banks[psum.slot(v.at, ("ob", t, q))]
                        V.tensor_copy(cols, bank[:, :]).then_inc(*psum.frees(v.at, ("ob", t, q)))
                        dve.wait_ge(*psum.vacated(v.at, ("ob", t, q)))
                        dve.wait_ge(*psum.full(v.at, ("st", q)))
                        bank = banks[psum.slot(v.at, ("st", q))]
                        V.tensor_copy(gst[:, 4 * q:4 * q + 4, :],
                                                             bank[:, :].rearrange("p (a i) -> p a i", a=4)).then_inc(*psum.frees(v.at, ("st", q)))
                        dve.wait_ge(*psum.vacated(v.at, ("st", q)))
            for t in range(NT):
                tt(work[:, :], go[:, t, :], go[:, t, :], ALU.mult).then_inc(dve_done, 1)
                dve.wait_ge(dve_done, v.count())
                V.reduce_sum(tmp[:, 8 * t:8 * t + 8], work[:, :].rearrange("p (h f) -> p h f", h=GV), axis=AX).then_inc(dve_done, 1)
                dve.wait_ge(dve_done, v.count())
            ts(t16, t16, 1.0 / P, GDN_EPS, ALU.mult, ALU.add).then_inc(*var_ready.event(v.at))
            dve.wait_ge(*var_ready.last(v.at))
            state["std"] += 1
            dve.wait_ge(*std_ready.nth(v.at, state["std"]))
            V.reciprocal(t16, t16).then_inc(dve_done, 1)
            dve.wait_ge(dve_done, v.count())
            dve.wait_ge(*gate_done.nth(v.at, 1))
            for t in range(NT):
                o3 = go[:, t, :].rearrange("p (h f) -> p h f", h=GV)
                tt(o3, o3, t16[:, 8 * t:8 * t + 8].unsqueeze(2).to_broadcast([P, GV, P]), ALU.mult).then_inc(dve_done, 1)
                dve.wait_ge(dve_done, v.count())
                tt(o3, o3, nw.unsqueeze(1).to_broadcast([P, GV, P]), ALU.mult).then_inc(dve_done, 1)
                dve.wait_ge(dve_done, v.count())
                tt(go[:, t, :], go[:, t, :], gz[:, t, :], ALU.mult).then_inc(*y_ready.event(v.at))
                dve.wait_ge(*y_ready.last(v.at))
            low_tiles("goT", 2, goTs)
            low(2)
            residual(outs("gout")[0:2], None, ALPHA)
            low(2)
            residual(outs("gout")[2:4], None, ALPHA)
            layernorm("ln1")
            low_tiles("fxT", 2, hTs)
            dve.wait_ge(*rows.full(v.at, ("relb", 0)))
            r = R[:, rows.slot(v.at, ("relb", 0)), :]
            V.tensor_copy(relspread[0:BUCKETS, :, :], r[0:BUCKETS, 0:WQ_HEADS].unsqueeze(2)
                                       .to_broadcast([BUCKETS, WQ_HEADS, P])).then_inc(*g_in.event(v.at))
            dve.wait_ge(*g_in.last(v.at))
            dve.nop().then_inc(*rows.frees(v.at, ("relb", 0)))
            hidden(FF2 // P, hid2)
            dve.wait_ge(*rows.full(v.at, ("tmask", 0)))
            r = R[:, rows.slot(v.at, ("tmask", 0)), :]
            for h_ in range(WQ_HEADS):
                add_row(("rel", h_), r, relw[:, h_, :], width=384)
            dve.nop().then_inc(*bias_made.event(v.at))
            dve.nop().then_inc(*rows.frees(v.at, ("tmask", 0)))
            dve.nop().then_inc(*rows.frees(v.at, ("hot", 0)))
            low(11)
            residual(DOWN, None, ALPHA)
            layernorm("ln2")
            low_tiles("wxT", 2, hTs)
            for c in range(2):
                low(2 - c)
                chunk_in("wq", c, lambda t: wq[:, t, c * 512:(c + 1) * 512])
            low(2)
            dve.wait_ge(*rows.full(v.at, ("wkv", 0)))
            r = R[:, rows.slot(v.at, ("wkv", 0)), :]
            for t in range(NT):
                add_row(("wkv", 0, t), r, wkv[:, t, :], width=256)
            dve.nop().then_inc(*rows.frees(v.at, ("wkv", 0)))
            for t in range(NT):
                i = V.tensor_copy(wkd[:, t, :].rearrange("p (g d f) -> p g d f", g=2, d=2),
                                  wkv[:, t, 0:128].rearrange("p (g f) -> p g f", g=2).unsqueeze(2)
                                  .to_broadcast([P, 2, 2, WD]))
                if t == 0:
                    i.then_inc(dve_done, 1)
                    dve.wait_ge(dve_done, v.count())
                else:
                    i.then_inc(*zB_ready.event(v.at))
                    dve.wait_ge(*zB_ready.last(v.at))
            dve.wait_ge(*rows.full(v.at, ("sink", 0)))
            sinks = R[:, rows.slot(v.at, ("sink", 0)), :]
            dve.wait_ge(bias_in, 16)

            def w_out(u):
                hp, t = divmod(u, NT)
                dve.wait_ge(*psum.full(v.at, ("Wo", hp, t)))
                bank = banks[psum.slot(v.at, ("Wo", hp, t))]
                tt(wo[:, t, hp * P:(hp + 1) * P].rearrange("p (m f) -> p m f", m=2),
                          bank[:, 0:P].rearrange("p (m f) -> p m f", m=2),
                          rinv[:, u % 3, :].unsqueeze(2).to_broadcast([P, 2, WD]), ALU.mult).then_inc(*psum.frees(v.at, ("Wo", hp, t)))
                dve.wait_ge(*psum.vacated(v.at, ("Wo", hp, t)))

            for u in range(16):
                hp, t = divmod(u, NT)
                b = u % 2
                mask("W", hp, t, u, 2, WD ** -0.5, lambda m, K: wbias[:, 2 * hp + m, 2 * P - K:2 * P])
                dve.wait_ge(*exped.nth(v.at, u + 1))
                tt(rsum[:, b, :], rsum[:, b, :], esink[:, b, :], ALU.add).then_inc(dve_done, 1)
                dve.wait_ge(dve_done, v.count())
                V.reciprocal(rinv[:, u % 3, :], rsum[:, b, :]).then_inc(*probs.event(v.at))
                dve.wait_ge(*probs.last(v.at))
                if u > 1:
                    w_out(u - 2)
            w_out(14)
            w_out(15)
            dve.nop().then_inc(*rows.frees(v.at, ("sink", 0)))
            dve.nop().then_inc(*y_ready.event(v.at))
            dve.nop().then_inc(*y_ready.event(v.at))
            low_tiles("woT", 2, woTs)
            low(2)
            residual(outs("wout")[0:2], None, ALPHA)
            low(1)
            residual(outs("wout")[2:4], None, ALPHA)
            layernorm("ln3")
            low_tiles("mxT", 2, hTs)
            assert next(state["split"], None) is None
            lg = small[:, 60:76].rearrange("p (t e) -> p t e", t=NT)
            tm = tmp[:, 0:16].rearrange("p (t e) -> p t e", t=NT)
            for t in range(NT):
                dve.wait_ge(*psum.full(v.at, ("router", 0, t)))
                bank = banks[psum.slot(v.at, ("router", 0, t))]
                V.tensor_copy(lg[:, t, :], bank[:, 0:NE]).then_inc(*psum.frees(v.at, ("router", 0, t)))
                dve.wait_ge(*psum.vacated(v.at, ("router", 0, t)))
            V.reduce_max(nmax[:, 0, :], lg, axis=AX).then_inc(dve_done, 1)
            dve.wait_ge(dve_done, v.count())
            tt(tm, lg, nmax[:, 0, :].unsqueeze(2).to_broadcast([P, NT, NE]), ALU.subtract).then_inc(dve_done, 1)
            dve.wait_ge(dve_done, v.count())
            dve.nop().then_inc(*g_pre.event(v.at))
            dve.wait_ge(*g_act.nth(v.at, n_act + 1))
            for t in range(NT):
                other = lg[:, t, :].unsqueeze(1).to_broadcast([P, NE, NE])
                own = lg[:, t, :].unsqueeze(2).to_broadcast([P, NE, NE])
                gt_, eq = [work[:, i * 64:(i + 1) * 64].rearrange("p (a b) -> p a b", a=NE) for i in range(2)]
                tt(gt_, other, own, ALU.is_gt).then_inc(dve_done, 1)
                dve.wait_ge(dve_done, v.count())
                tt(eq, other, own, ALU.is_equal).then_inc(dve_done, 1)
                dve.wait_ge(dve_done, v.count())
                tt(eq, eq, below, ALU.mult).then_inc(dve_done, 1)
                dve.wait_ge(dve_done, v.count())
                tt(gt_, gt_, eq, ALU.add).then_inc(dve_done, 1)
                dve.wait_ge(dve_done, v.count())
                V.reduce_sum(gates[:, t, :], gt_, axis=AX).then_inc(dve_done, 1)
                dve.wait_ge(dve_done, v.count())
            ts(places, gates, 2.0, None, ALU.is_lt).then_inc(*route_in.event(v.at))
            dve.wait_ge(*route_in.last(v.at))
            tt(gates, places, tm, ALU.mult).then_inc(dve_done, 1)
            dve.wait_ge(dve_done, v.count())
            V.reduce_sum(nmax[:, 0, :], gates, axis=AX).then_inc(dve_done, 1)
            dve.wait_ge(dve_done, v.count())
            V.reciprocal(nmax[:, 0, :], nmax[:, 0, :]).then_inc(dve_done, 1)
            dve.wait_ge(dve_done, v.count())
            tt(gates, gates, nmax[:, 0, :].unsqueeze(2).to_broadcast([P, NT, NE]), ALU.mult).then_inc(dve_done, 1)
            dve.wait_ge(dve_done, v.count())
            counts = work[:, 0:3 * NE].rearrange("p (a e) -> p a e", a=3)
            dve.wait_ge(*psum.full(v.at, ("count", 0)))
            bank = banks[psum.slot(v.at, ("count", 0))]
            V.tensor_copy(work[:, 0:3 * NE], bank[:, 0:3 * NE]).then_inc(*psum.frees(v.at, ("count", 0)))
            dve.wait_ge(*psum.vacated(v.at, ("count", 0)))
            tt(places, places, counts[:, 0:NT, :], ALU.mult).then_inc(dve_done, 1)
            dve.wait_ge(dve_done, v.count())
            ts(places, places, -1.0, None, ALU.add).then_inc(dve_done, 1)
            dve.wait_ge(dve_done, v.count())
            more, number = work[:, 64:64 + NE], work[:, 72:72 + NE]
            hits = work[:, 128:128 + OVER * NE].rearrange("p (i e) -> p i e", i=OVER)
            listed = work[:, 200:201 + OVER]
            ts(more, counts[:, 2, :], P + 0.5, None, ALU.is_gt).then_inc(dve_done, 1)
            dve.wait_ge(dve_done, v.count())
            V.reduce_sum(listed[:, 0:1], more, axis=AX).then_inc(dve_done, 1)
            dve.wait_ge(dve_done, v.count())
            more_all = more.unsqueeze(1).to_broadcast([P, NE, NE])
            before = work[:, 256:256 + NE * NE].rearrange("p (a b) -> p a b", a=NE)
            tt(before, more_all, below, ALU.mult).then_inc(dve_done, 1)
            dve.wait_ge(dve_done, v.count())
            V.reduce_sum(number, before, axis=AX).then_inc(dve_done, 1)
            dve.wait_ge(dve_done, v.count())
            index = const("slots")
            tt(hits, number.unsqueeze(1).to_broadcast([P, OVER, NE]),
               index[:, 0:OVER].unsqueeze(2).to_broadcast([P, OVER, NE]), ALU.is_equal).then_inc(dve_done, 1)
            dve.wait_ge(dve_done, v.count())
            tt(hits, hits, more.unsqueeze(1).to_broadcast([P, OVER, NE]), ALU.mult).then_inc(dve_done, 1)
            dve.wait_ge(dve_done, v.count())
            tt(hits, hits, index[:, 0:NE].unsqueeze(1).to_broadcast([P, OVER, NE]), ALU.mult).then_inc(dve_done, 1)
            dve.wait_ge(dve_done, v.count())
            V.reduce_sum(listed[:, 1:1 + OVER], hits, axis=AX).then_inc(dve_done, 1)
            dve.wait_ge(dve_done, v.count())
            V.tensor_copy(plan[:, :], listed).then_inc(*plan_ready.event(v.at))
            dve.wait_ge(*plan_ready.last(v.at))
            V.memset(route[:, :, :, NE:NE + 1], -1.0).then_inc(dve_done, 1)
            dve.wait_ge(dve_done, v.count())
            V.tensor_copy(xins[0], x[:, :, :]).then_inc(dve_done, 1)
            dve.wait_ge(dve_done, v.count())
            tt(xins[1], x[:, :, :], xins[0].bitcast(F32), ALU.subtract).then_inc(dve_done, 1)
            dve.wait_ge(dve_done, v.count())
            ts(x[:, :, :], x[:, :, :], ALPHA, None, ALU.mult).then_inc(dve_done, 1)
            dve.wait_ge(dve_done, v.count())
            def low_part(job, d, signal):
                state["group"] += 1
                dve.wait_ge(*group_high.nth(v.at, state["group"]))
                dve.wait_ge(*psum.full(v.at, job))
                bank = banks[psum.slot(v.at, job)]
                n = d[0].shape[1]
                tt(d[1], bank[:, 0:n * P].rearrange("p (a i) -> p a i", a=n), d[0].bitcast(F32),
                   ALU.subtract).then_inc(*psum.frees(v.at, job))
                dve.wait_ge(*psum.vacated(v.at, job))
                dve.nop().then_inc(*signal.event(v.at))

            def pick(e, block):
                slots = index[:, block * P:(block + 1) * P]
                V.tensor_copy(coming, route[:, 1, :, e].rearrange("p t e -> p (t e)")).then_inc(dve_done, 1)
                dve.wait_ge(dve_done, v.count())
                for t in range(NT):
                    i = ts(select[:, t, :], slots, coming[:, t:t + 1], None, ALU.is_equal)
                    if t < NT - 1:
                        i.then_inc(dve_done, 1)
                        dve.wait_ge(dve_done, v.count())
                    else:
                        i.then_inc(*select_ready.event(v.at))
                        dve.wait_ge(*select_ready.last(v.at))

            def gathered():
                for q in range(2):
                    low_part(("chosen", q), [m[:, 4 * q:4 * q + 4, :] for m in chosenTs], chosen_split)

            pick(slice(0, 1), 0)
            gathered()
            dve.nop().then_inc(dve_done, 1)
            dve.wait_ge(dve_done, v.count())
            dve.sem_clear(dve_done)

            def expert(e, block):
                slots = index[:, block * P:(block + 1) * P]
                state["split"] = iter(SPLIT["expert"])

                def turned(c):
                    if c % 4:
                        low_part(("turn", c), [m[:, 2 * c:2 * c + 2, :] for m in hidTs], down_split)

                V.tensor_copy(now, route[:, :, :, bass.ds(e, 1)].rearrange("p a t e -> p a (t e)")
                              ).then_inc(dve_done, 1)
                dve.wait_ge(dve_done, v.count())
                for t in range(NT):
                    i = ts(weigh[:, t, :], slots, now[:, 1, t:t + 1], now[:, 0, t:t + 1], ALU.is_equal, ALU.mult)
                    if t < NT - 1:
                        i.then_inc(dve_done, 1)
                        dve.wait_ge(dve_done, v.count())
                    else:
                        i.then_inc(*weigh_ready.event(v.at))
                        dve.wait_ge(*weigh_ready.last(v.at))
                low(3)
                for c in range(FFE // 256):
                    dve.wait_ge(*hid_act.nth(v.at, c + 1))
                    dve.wait_ge(*psum.full(v.at, ("up", c)))
                    bank = banks[psum.slot(v.at, ("up", c))]
                    tt(hid_tok[:, c % 2, :], acted[:, c % 2, :], bank[:, S:2 * S], ALU.mult
                       ).then_inc(*psum.frees(v.at, ("up", c)))
                    dve.wait_ge(*psum.vacated(v.at, ("up", c)))
                    dve.nop().then_inc(*hid_ready.event(v.at))
                    low(1 + c % 2)
                    if c:
                        turned(c - 1)
                turned(FFE // 256 - 1)
                if block == 0:
                    pick(bass.ds(e + 1, 1), 0)
                low(7)
                assert next(state["split"], None) is None
                if block == 0:
                    gathered()
                for half in range(2):
                    for t in range(NT):
                        dve.wait_ge(*psum.full(v.at, ("back", t, half)))
                        bank = banks[psum.slot(v.at, ("back", t, half))]
                        dst = x[:, t, half * 512:(half + 1) * 512]
                        tt(dst, dst, bank[:, :], ALU.add).then_inc(*psum.frees(v.at, ("back", t, half)))
                        dve.wait_ge(*psum.vacated(v.at, ("back", t, half)))
                dve.nop().then_inc(dve_done, 1)
                dve.wait_ge(dve_done, v.count())
                dve.sem_clear(dve_done)

            with dve.Fori(0, NE) as e:
                v.enter("expert", e)
                state["group"] = 0
                expert(e, 0)
            n_over = dve.value_load(plan[0:1, 0:1], min_val=0, max_val=OVER)
            with dve.If(n_over):
                with dve.Fori(0, n_over) as i:
                    e = dve.value_load(plan[0:1, bass.ds(1 + i, 1)], min_val=0, max_val=NE - 1)
                    v.enter("over", i)
                    state["group"] = 0
                    pick(bass.ds(e, 1), 1)
                    gathered()
                    expert(e, 1)
            v.enter("end")
            state["std"] = 0
            layernorm("ln4")

        jobs = {p: len(n) for p, n in psum.order.items()}
        given = {s.name: s.seen for s in signals}
        return jobs, given


def _columns(w, width=512):
    K, N = w.shape
    out = []
    for c in range(0, N, width):
        v = w[:, c:c + width].reshape(K // P, P, -1).transpose(1, 0, 2).reshape(P, -1)
        out += [v[:, a:a + HALF] for a in range(0, v.shape[1], HALF)]
    return out


def _tiles(a, b):
    F = a.shape[1]
    both = np.stack([a.reshape(KD, P, F // P, P), b.reshape(KD, P, F // P, P)], 3)
    return list(both.transpose(2, 1, 0, 3, 4).reshape(F // P, P, HALF))


def _pairs(a, b):
    F = a.shape[1]
    both = np.stack([a.reshape(2, 4, P, F // 256, 256), b.reshape(2, 4, P, F // 256, 256)], 4)
    return list(both.transpose(3, 0, 2, 1, 4, 5).reshape(F // P, P, HALF))


def _down(w):
    t = w.reshape(-1, 2, P, D)
    return list(t.transpose(0, 2, 1, 3).reshape(-1, P, HALF))


def _pack(slots, width=HALF):
    out = np.zeros((len(slots), P, width), np.float32)
    for i, s in enumerate(slots):
        out[i, :, :s.shape[1]] = s
    return out


def _row(*parts):
    r = np.zeros(512, np.float32)
    at = 0
    for p in parts:
        p = np.asarray(p).reshape(-1)
        r[at:at + len(p)] = p
        at += len(p)
    return r


def pack(i):
    arrays = {"constants": constants(), "x": i["x"].reshape(S, D),
              "c_columns": np.ascontiguousarray(i["c"].reshape(KD, P).T)}
    w, r, c = [], [], []
    for l in range(DEPTH):
        w_in, b_in = i["w_in"][l], i["b_in"][l]
        bf = 3072
        cuts = [(0, 1536), (1536, 3072), (bf, bf + 4), (bf + 4, bf + 3076), (bf + 3076, bf + 6148)]
        ada = _columns(i["w_ada"][l])
        slots, bias = [], []
        b_ada = i["b_ada"][l].reshape(12, 512)
        init = 0.8 - 0.6 * math.exp(-0.3 * l)
        bias.append(_row())
        bias.append(_row(i["lam_q1"][l], i["lam_k1"][l], i["lam_q2"][l], i["lam_k2"][l],
                         np.array([init, 1.0 - init], np.float32)))
        for a, b in cuts:
            slots += _columns(w_in[:, a:b])
            for n in range(a, b, 512):
                bias.append(_row(b_in[n:min(n + 512, b)]))
                if n in (0, 512):
                    bias.append(_row(b_ada[4 + n // 512]))
        for name in ("w_pa", "w_pb", "w_pc", "w_out"):
            slots += _columns(i[name][l])
        slots += _tiles(i["w_up"][l][:, :FF1], i["w_up"][l][:, FF1:]) + _down(i["w_down"][l])
        slots = iter(slots)
        slots = [ada[2 * name[1] + name[2]] if name[0] == "ada" else next(slots) for name in W_LOADS["layer"]]
        bias.insert(R_LOADS["layer"].index(("gdiff", 0)), _row(i["g_diff"][l]))
        bias += [_row(g) for g in i["g_ret"][l].reshape(2, 512)]

        def ln(g, b):
            return [_row(g[:512]), _row(b[:512]), _row(g[512:]), _row(b[512:])]

        bias += ln(i["ln_g"][l, 0], i["ln_b"][l, 0]) + [_row(), _row(b_ada[10]), _row(b_ada[11])] + ln(i["ln_g"][l, 1], i["ln_b"][l, 1])
        taps = np.zeros((P, 512), np.float32)
        nf = FF1 // P
        for n, a in enumerate([*i["w_conv"][l], i["b_conv"][l]]):
            taps[:, n * nf:(n + 1) * nf] = a.reshape(nf, P).T
        modulation = np.zeros((P, 512), np.float32)
        for n, a in enumerate((0, 2, 6, 8)):
            modulation[:, 8 * n:8 * n + 8] = b_ada[a:a + 2].reshape(KD, P).T
        w.append(_pack(slots))
        r.append(np.stack(bias))
        c.append(np.stack([modulation, taps]))
    arrays["w_layer"], arrays["rows_layer"], arrays["cols_layer"] = np.stack(w), np.stack(r), np.stack(c)

    g = i["a_w_in_2"][0]
    slots = _columns(g[:, :2048], 256) + _columns(g[:, 2048:3072]) + _columns(g[:, 3072:])
    slots += _columns(i["a_w_out_2"][0])
    slots += _tiles(i["ffn_w_gate_2"][0], i["ffn_w_up_2"][0]) + _down(i["ffn_w_down_2"][0])
    slots += _columns(i["b_w_in_2"][0][:, :1024]) + _columns(i["b_w_in_2"][0][:, 1024:], 256)
    slots += _columns(i["b_w_out_2"][0]) + _columns(i["moe_router_2"][0])
    arrays["w_middle"] = _pack(slots)
    hot, mask = bias_tables()
    lng, lnb = i["ln_g_2"], i["ln_b_2"]
    bias = [_row(), _row(i["a_a_log_2"][0], i["a_dt_bias_2"][0], i["a_norm_w_2"][0])]
    bias += ln(lng[0, 0], lnb[0, 0]) + [_row(), _row(), mask] + ln(lng[0, 1], lnb[0, 1])
    b = i["b_b_in_2"][0]
    bias += [_row(b[:512]), _row(b[512:1024]), _row(b[1024:]), _row(i["b_sinks_2"][0])]
    bias += ln(lng[1, 0], lnb[1, 0])
    arrays["rows_middle"] = np.stack(bias)
    gconv = np.zeros((P, 512), np.float32)
    for n in range(GDN_TAPS):
        gconv[:, 16 * n:16 * n + 16] = i["a_conv_w_2"][0][n].reshape(16, P).T
    relb = np.zeros((P, 512), np.float32)
    relb[:BUCKETS, :WQ_HEADS] = i["rel_bias_2"]
    arrays["cols_middle"] = np.stack([gconv, relb, hot])
    arrays["rows_end"] = np.stack(ln(lng[1, 1], lnb[1, 1]))
    e = np.empty((NE, len(W_LOADS["expert"]), P, HALF), np.float32)
    for n in range(NE):
        for k, s in enumerate(_pairs(i["moe_w_gate_2"][0, n], i["moe_w_up_2"][0, n])
                              + _down(i["moe_w_down_2"][0, n])):
            e[n, k] = s
    arrays["w_expert"] = e
    return arrays


def kernel(**inputs):
    import concourse.bacc as bacc
    from concourse.bass_utils import run_bass_kernel_spmd

    arrays = pack({k: np.asarray(a) for k, a in inputs.items()})
    nc = bacc.Bacc("TRN2", target_bir_lowering=False, num_devices=1)
    ins = {n: nc.dram_tensor("in_" + n, a.shape, F32, kind="ExternalInput").ap() for n, a in arrays.items()}
    out = nc.dram_tensor("out_x", (S, D), F32, kind="ExternalOutput").ap()
    program(nc, ins, out)
    r = run_bass_kernel_spmd(nc, [{"in_" + n: a for n, a in arrays.items()}], core_ids=[0])
    return r.results[0]["out_x"].reshape(1, S, D)
```
